# Optimizing a Trainium2 kernel written in Bass

```python
import math
import jax, jax.numpy as jnp
from jax import lax
import numpy as np

D_MODEL = 1024
BATCH = 1
SEQ = 256
DEPTH = 2

N_HEADS = 8
QK_NOPE_DIM = 64
QK_ROPE_DIM = 32
QK_HEAD_DIM = QK_NOPE_DIM + QK_ROPE_DIM
V_HEAD_DIM = 64
Q_LORA_RANK = 256
KV_LORA_RANK = 128
ROPE_THETA = 10000.0
Q_BLOCK = 128
ATTN_WIDTH = N_HEADS * V_HEAD_DIM

S5_WIDTH = 512
S5_GROUP = 16
S5_GROUPS = S5_WIDTH // S5_GROUP
S5_STATE = 64
DT_MIN = 1e-3
DT_MAX = 1e-1

D_FF_DENSE = 2816
N_EXPERTS = 8
TOP_K = 2
D_FF_EXPERT = 3584
N_DENSE = (DEPTH + 1) // 2
N_MOE = DEPTH // 2

EPS = 1e-6

IN_PARTS = [Q_LORA_RANK, KV_LORA_RANK, QK_ROPE_DIM, S5_WIDTH, D_MODEL, D_MODEL]
IN_COLS = sum(IN_PARTS)
IN_SPLITS = [int(v) for v in np.cumsum(IN_PARTS)[:-1]]

kernel_name = "hybrid_mla_s5_gated_moe_block"

def rmsnorm(x, g):
    xf = x.astype(jnp.float32)
    y = xf * lax.rsqrt(jnp.mean(xf * xf, axis=-1, keepdims=True) + EPS) * g.astype(jnp.float32)
    return y.astype(x.dtype)

def rope_tables(s, dtype):
    pos = jnp.arange(s, dtype=jnp.float32)
    inv = jnp.power(ROPE_THETA, -jnp.arange(0, QK_ROPE_DIM, 2, dtype=jnp.float32) / QK_ROPE_DIM)
    ang = pos[:, None] * inv[None, :]
    return jnp.cos(ang)[:, None, :].astype(dtype), jnp.sin(ang)[:, None, :].astype(dtype)

def rope(x, cos, sin):
    half = QK_ROPE_DIM // 2
    x1, x2 = x[..., :half], x[..., half:]
    return jnp.concatenate([x1 * cos - x2 * sin, x2 * cos + x1 * sin], axis=-1)

def causal_block_attention(q, k, v):
    b, s, h, dq = q.shape
    nb = s // Q_BLOCK
    qb = q.reshape(b, nb, Q_BLOCK, h, dq).transpose(1, 0, 2, 3, 4)
    kpos = jnp.arange(s)
    scale = QK_HEAD_DIM ** -0.5

    def one_block(args):
        qi, i = args
        qpos = i * Q_BLOCK + jnp.arange(Q_BLOCK)
        sc = jnp.einsum('bqhd,bkhd->bhqk', qi, k, preferred_element_type=jnp.float32) * scale
        sc = jnp.where(kpos[None, :] <= qpos[:, None], sc, -jnp.inf)
        p = jax.nn.softmax(sc, axis=-1).astype(v.dtype)
        return jnp.einsum('bhqk,bkhd->bqhd', p, v)

    out = lax.map(one_block, (qb, jnp.arange(nb)))
    return out.transpose(1, 0, 2, 3, 4).reshape(b, s, h, v.shape[-1])

def mla_branch(q_lat, kv_lat, k_rope, q_norm_g, w_uq, kv_norm_g, w_ukv, q_head_g, k_head_g):
    b, s, _ = q_lat.shape
    q = (rmsnorm(q_lat, q_norm_g) @ w_uq).reshape(b, s, N_HEADS, QK_HEAD_DIM)
    kv = (rmsnorm(kv_lat, kv_norm_g) @ w_ukv).reshape(b, s, N_HEADS, QK_NOPE_DIM + V_HEAD_DIM)
    k_nope, v = kv[..., :QK_NOPE_DIM], kv[..., QK_NOPE_DIM:]
    k_rope_h = jnp.broadcast_to(k_rope[:, :, None, :], (b, s, N_HEADS, QK_ROPE_DIM))
    k = jnp.concatenate([k_nope, k_rope_h], axis=-1)
    q = rmsnorm(q, q_head_g)
    k = rmsnorm(k, k_head_g)
    cos, sin = rope_tables(s, q.dtype)
    q = jnp.concatenate([q[..., :QK_NOPE_DIM], rope(q[..., QK_NOPE_DIM:], cos, sin)], axis=-1)
    k = jnp.concatenate([k[..., :QK_NOPE_DIM], rope(k[..., QK_NOPE_DIM:], cos, sin)], axis=-1)
    out = causal_block_attention(q, k, v)
    return out.reshape(b, s, ATTN_WIDTH)

def s5_branch(u, lam_re, lam_im, log_step, b_re, b_im, c_re, c_im, d_skip, w_glu, b_glu):
    bsz, s, _ = u.shape
    uf = u.astype(jnp.float32)
    ug = uf.reshape(bsz, s, S5_GROUPS, S5_GROUP).astype(jnp.complex64)
    lam = lax.complex(lam_re.astype(jnp.float32), lam_im.astype(jnp.float32))
    step = jnp.exp(log_step.astype(jnp.float32))[:, None]
    lam_bar = jnp.exp(lam * step)
    b_mat = lax.complex(b_re.astype(jnp.float32), b_im.astype(jnp.float32))
    b_bar = ((lam_bar - 1.0) / lam)[..., None] * b_mat
    bu = jnp.einsum('gpc,bsgc->bsgp', b_bar, ug)
    a = jnp.broadcast_to(lam_bar, bu.shape)

    def combine(left, right):
        a1, b1 = left
        a2, b2 = right
        return a2 * a1, a2 * b1 + b2

    _, states = lax.associative_scan(combine, (a, bu), axis=1)
    c_mat = lax.complex(c_re.astype(jnp.float32), c_im.astype(jnp.float32))
    y = jnp.real(jnp.einsum('gcp,bsgp->bsgc', c_mat, states)).reshape(bsz, s, S5_WIDTH)
    y = (y + d_skip.astype(jnp.float32) * uf).astype(u.dtype)
    y = jax.nn.gelu(y)
    return y * jax.nn.sigmoid(y @ w_glu + b_glu)

def swiglu(h, w_gate, w_up, w_down):
    return (jax.nn.silu(h @ w_gate) * (h @ w_up)) @ w_down

def moe_swiglu(h, router_w, router_b, w_gate, w_up, w_down):
    b, s, d = h.shape
    t = h.reshape(b * s, d)
    logits = (t @ router_w).astype(jnp.float32) + router_b.astype(jnp.float32)
    top_val, top_idx = lax.top_k(logits, TOP_K)
    top_w = jax.nn.softmax(top_val, axis=-1)
    comb = jnp.sum(jax.nn.one_hot(top_idx, N_EXPERTS, dtype=jnp.float32) * top_w[..., None], axis=1)
    comb = comb.astype(t.dtype)
    out = jnp.zeros_like(t)
    for e in range(N_EXPERTS):
        out = out + comb[:, e:e + 1] * swiglu(t, w_gate[e], w_up[e], w_down[e])
    return out.reshape(b, s, d)

def setup_inputs(seed: int = 0) -> dict:
    key = jax.random.key(seed)
    ks = iter(jax.random.split(key, 48))
    f32 = jnp.float32

    def nrm(shape, fan_in):
        return jax.random.normal(next(ks), shape, f32) * (fan_in ** -0.5)

    def gain(shape):
        return 1.0 + 0.02 * jax.random.normal(next(ks), shape, f32)

    def small(shape, scale=0.01):
        return scale * jax.random.normal(next(ks), shape, f32)

    L, G, P, C = DEPTH, S5_GROUPS, S5_STATE, S5_GROUP
    lam_re = -0.5 + small((L, G, P))
    lam_im = math.pi * jnp.broadcast_to(jnp.arange(P, dtype=f32), (L, G, P)) + small((L, G, P))
    log_step = jax.random.uniform(next(ks), (L, G), f32, math.log(DT_MIN), math.log(DT_MAX))
    return {
        "x": jax.random.normal(next(ks), (BATCH, SEQ, D_MODEL), f32),
        "ln_mix_g": gain((L, D_MODEL)),
        "w_in": nrm((L, D_MODEL, IN_COLS), D_MODEL),
        "b_in": small((L, IN_COLS)),
        "q_norm_g": gain((L, Q_LORA_RANK)),
        "w_uq": nrm((L, Q_LORA_RANK, N_HEADS * QK_HEAD_DIM), Q_LORA_RANK),
        "kv_norm_g": gain((L, KV_LORA_RANK)),
        "w_ukv": nrm((L, KV_LORA_RANK, N_HEADS * (QK_NOPE_DIM + V_HEAD_DIM)), KV_LORA_RANK),
        "q_head_g": gain((L, QK_HEAD_DIM)),
        "k_head_g": gain((L, QK_HEAD_DIM)),
        "s5_lam_re": lam_re,
        "s5_lam_im": lam_im,
        "s5_log_step": log_step,
        "s5_b_re": nrm((L, G, P, C), 2 * C),
        "s5_b_im": nrm((L, G, P, C), 2 * C),
        "s5_c_re": nrm((L, G, C, P), P),
        "s5_c_im": nrm((L, G, C, P), P),
        "s5_d": jax.random.normal(next(ks), (L, S5_WIDTH), f32),
        "w_glu": nrm((L, S5_WIDTH, S5_WIDTH), S5_WIDTH),
        "b_glu": small((L, S5_WIDTH)),
        "w_proj_attn": nrm((L, ATTN_WIDTH, D_MODEL), ATTN_WIDTH),
        "w_proj_ssm": nrm((L, S5_WIDTH, D_MODEL), S5_WIDTH),
        "w_out": nrm((L, D_MODEL, D_MODEL), D_MODEL),
        "ln_ffn_g": gain((L, D_MODEL)),
        "ffn_w_gate": nrm((N_DENSE, D_MODEL, D_FF_DENSE), D_MODEL),
        "ffn_w_up": nrm((N_DENSE, D_MODEL, D_FF_DENSE), D_MODEL),
        "ffn_w_down": nrm((N_DENSE, D_FF_DENSE, D_MODEL), D_FF_DENSE),
        "router_w": nrm((N_MOE, D_MODEL, N_EXPERTS), D_MODEL),
        "router_b": small((N_MOE, N_EXPERTS)),
        "moe_w_gate": nrm((N_MOE, N_EXPERTS, D_MODEL, D_FF_EXPERT), D_MODEL),
        "moe_w_up": nrm((N_MOE, N_EXPERTS, D_MODEL, D_FF_EXPERT), D_MODEL),
        "moe_w_down": nrm((N_MOE, N_EXPERTS, D_FF_EXPERT, D_MODEL), D_FF_EXPERT),
    }

def reference(x, ln_mix_g, w_in, b_in, q_norm_g, w_uq, kv_norm_g, w_ukv, q_head_g, k_head_g,
              s5_lam_re, s5_lam_im, s5_log_step, s5_b_re, s5_b_im, s5_c_re, s5_c_im, s5_d,
              w_glu, b_glu, w_proj_attn, w_proj_ssm, w_out, ln_ffn_g,
              ffn_w_gate, ffn_w_up, ffn_w_down, router_w, router_b,
              moe_w_gate, moe_w_up, moe_w_down):
    for l in range(DEPTH):
        h = rmsnorm(x, ln_mix_g[l])
        proj = h @ w_in[l] + b_in[l]
        q_lat, kv_lat, k_rope, u, gate_a, gate_b = jnp.split(proj, IN_SPLITS, axis=-1)
        attn = mla_branch(q_lat, kv_lat, k_rope, q_norm_g[l], w_uq[l], kv_norm_g[l], w_ukv[l],
                          q_head_g[l], k_head_g[l])
        ssm = s5_branch(u, s5_lam_re[l], s5_lam_im[l], s5_log_step[l], s5_b_re[l], s5_b_im[l],
                        s5_c_re[l], s5_c_im[l], s5_d[l], w_glu[l], b_glu[l])
        mix = (jax.nn.sigmoid(gate_a) * (attn @ w_proj_attn[l])
               + jax.nn.sigmoid(gate_b) * (ssm @ w_proj_ssm[l]))
        x = x + mix @ w_out[l]
        h = rmsnorm(x, ln_ffn_g[l])
        if l % 2 == 0:
            j = l // 2
            x = x + swiglu(h, ffn_w_gate[j], ffn_w_up[j], ffn_w_down[j])
        else:
            j = l // 2
            x = x + moe_swiglu(h, router_w[j], router_b[j], moe_w_gate[j], moe_w_up[j], moe_w_down[j])
    return x


_drawn_inputs = setup_inputs


def setup_inputs(seed=0):
    import zlib

    import numpy as np

    out = dict(_drawn_inputs(seed))
    spreads = {}
    factors = {'ln_mix_g': 2.964,
     'q_norm_g': 3.0,
     'kv_norm_g': 3.113,
     'q_head_g': 3.366,
     'k_head_g': 5.72,
     's5_lam_re': 8.0,
     's5_c_im': 2.822,
     'b_glu': 8.0,
     'router_b': 2.706}
    for name, (base, spread) in spreads.items():
        noise = np.random.default_rng([zlib.crc32(name.encode()), seed]).standard_normal(out[name].shape)
        drawn = base * np.exp(spread * noise) if base else spread * noise
        out[name] = __import__('jax').numpy.asarray(drawn.astype(out[name].dtype))
    for name, factor in factors.items():
        out[name] = (out[name] * factor).astype(out[name].dtype)
    return out
```

```python
from contextlib import ExitStack

import numpy as np

import concourse.bass as bass
from concourse import mybir

F32 = mybir.dt.float32
I32 = mybir.dt.int32
U32 = mybir.dt.uint32
ALU = mybir.AluOpType
ACT = mybir.ActivationFunctionType
AX_X = mybir.AxisListType.X

P = 128
D = 1024
KD = D // P
SEQ = 256
TB = SEQ // P
DEPTH = 2
H = 8
NOPE = 64
ROPE = 32
HALF = ROPE // 2
QK = NOPE + ROPE
VD = 64
QR = 256
KR = 128
LAT = QR + KR + ROPE
S5W = 512
S5M = S5W // P
GROUPS = 32
STATES = 64
CH = 16
PAIRS = GROUPS // 2
PQ = PAIRS // S5M
FF = 2816
FFC = 6
E = 8
FE = 3584
FEC = FE // 512
EPS = 1e-6
NEG = -1e30
SCALE = QK ** -0.5
PI2_A = 6.28125
PI2_B = float(np.float32(2 * np.pi - 6.28125).astype(np.float16))
PI2_C = float(2 * np.pi - PI2_A - PI2_B)
MAGIC = 1.5 * 2 ** 23

FIELDS = [("g_mix", KD), ("g_ffn", KD), ("b_u", S5M), ("b_gate", 2 * KD), ("s5_d", S5M), ("b_glu", S5M),
          ("g_q", QR // P), ("g_kv", KR // P), ("lam_re", PAIRS), ("lam_im", PAIRS), ("log_step", PAIRS),
          ("b_re", PAIRS * 32), ("b_im", PAIRS * 32), ("c_re", PAIRS * 32), ("c_im", PAIRS * 32),
          ("b_lat", LAT), ("g_qh", QK), ("g_kh", QK)]
NPL = sum(n for _, n in FIELDS)
CONSTS = [("ident", P), ("mask", 3 * P), ("cos", TB * HALF), ("sin", TB * HALF), ("before", P), ("ones", P),
          ("iota", P), ("r_b", E)]
NC_ = sum(n for _, n in CONSTS)

RING = 6
SLOT = 4096
MIX_SLOTS = 4
MIX_ITEMS = ["lat", "u", "gate0", "up", "gate1", "gate2", "gate3", "glu", "proj_a", "proj_s", "out0", "out1"]
N_MIX = len(MIX_ITEMS)
FFN_ITEMS = [("g", 0), ("u", 0)]
for _c in range(1, FFC):
    FFN_ITEMS += [("g", _c), ("u", _c), ("d", _c - 1)]
FFN_ITEMS += [("d", FFC - 1)]
N_FFN = len(FFN_ITEMS)
MOE_ITEMS = [("g", 0), ("u", 0)]
for _c in range(1, FEC):
    MOE_ITEMS += [("g", _c), ("u", _c), ("d", _c - 1)]
MOE_ITEMS += [("d", FEC - 1)]
N_EXP = len(MOE_ITEMS)
N_PAIR = 2 * N_EXP


class Signal:

    def __init__(self, ctx, nc, name, per_layer=0):
        self.sem, self.per = ctx.enter_context(nc.semaphore(name)), per_layer

    def at(self, layer, n):
        return layer * self.per + n


class Chain:

    def __init__(self, eng, sem):
        self.eng, self.sem, self.base, self.n = eng, sem, 0, 0

    def start(self, base):
        self.base, self.n = base, 0

    def add(self, ins):
        ins.then_inc(self.sem, 1)
        self.n += 1

    def sync(self):
        self.eng.wait_ge(self.sem, self.base + self.n)

    def link(self, ins):
        self.add(ins)
        self.sync()


DVE_MIX, DVE_FFN, DVE_ROUTE, DVE_PAIR = CHAIN_DVE = (152, 25, 25, 20)
ACT_MIX, ACT_FFN = CHAIN_ACT = (8, 0)
POOL_MIX = 127


def hybrid_trunk(nc, x_in, params, consts, w_in, w_uq, w_ukv, w_glu, w_pa, w_ps, w_out,
                 f_gate, f_up, f_down, router, m_gate, m_up, m_down, out):
    with ExitStack() as ctx:
        def sb(name, cols, dt=F32, parts=P):
            return ctx.enter_context(nc.sbuf_tensor(name, [parts, cols], dt))

        def sig(name, per=0):
            return Signal(ctx, nc, name, per)

        ring = sb("ring", RING * SLOT)
        x = sb("x", TB * D)[:, :].rearrange("p (b d) -> p b d", b=TB)
        hT = sb("hT", KD * SEQ)[:, :].rearrange("p (k t) -> p k t", k=KD)
        gates_t = sb("gates", 2 * KD * SEQ)
        gates = gates_t[:, :].rearrange("p (m t) -> p m t", m=2 * KD)
        uT = sb("uT", S5M * SEQ)[:, :].rearrange("p (m t) -> p m t", m=S5M)
        pl = sb("pl", NPL)
        cst = sb("cst", NC_)
        bT = sb("bT", S5M * 2 * P)[:, :].rearrange("p (m r s) -> p m r s", m=S5M, r=2)
        work = sb("work", 11 * 1024)
        early = sb("early", LAT * TB + 3 * SEQ)
        attnT = sb("attnT", 4 * SEQ)[:, :].rearrange("p (k t) -> p k t", k=4)
        stat = sb("stat", 200)
        small = sb("small", 24 * PAIRS)
        router_sb = sb("router_sb", KD * E)[:, :].rearrange("p (k e) -> p k e", k=KD)
        most_i = sb("most_i", 1, I32)
        psum = ctx.enter_context(nc.psum_tensor("psum", [P, 8, 512], F32))

        field, at = {}, 0
        for name, n in FIELDS:
            field[name] = pl[:, at:at + n]
            at += n
        const, at = {}, 0
        for name, n in CONSTS:
            const[name] = cst[:, at:at + n]
            at += n
        ident, mask = const["ident"], const["mask"]

        slots = [ring[:, s * SLOT:(s + 1) * SLOT] for s in range(RING)]
        lat = early[:, 0:TB * LAT].rearrange("p (b n) -> p b n", b=TB)
        qlT = early[:, TB * LAT:TB * LAT + 2 * SEQ].rearrange("p (k t) -> p k t", k=2)
        kvT = early[:, TB * LAT + 2 * SEQ:TB * LAT + 3 * SEQ]
        tail = ring[:, MIX_SLOTS * SLOT:RING * SLOT]
        qk_tok = tail[:, 0:2 * TB * H * QK].rearrange("p (w b h n) -> p w b h n", w=2, b=TB, h=H)
        q_tok, k_tok = qk_tok[:, 0], qk_tok[:, 1]
        at = 2 * TB * H * QK
        v_tok = tail[:, at:at + TB * H * VD].rearrange("p (b h n) -> p b h n", b=TB, h=H)
        at += TB * H * VD
        qkT_flat = tail[:, at:at + 2 * H * SEQ]
        qkT = qkT_flat.rearrange("p (h w t) -> p h w t", h=H, w=2)
        squares = qkT_flat[:, 0:TB * H * QK].rearrange("p (b h n) -> p b h n", b=TB, h=H)
        probs = tail[:, 0:H * 3 * P].rearrange("p (h n) -> p h n", h=H)
        probsT = qkT_flat[:, 0:H * 3 * P].rearrange("p (h n) -> p h n", h=H)
        assert at + 2 * H * SEQ == 2 * SLOT

        N4 = PQ * SEQ

        def wk(i, n=1):
            return work[:, i * N4:(i + n) * N4]

        def quads(a):
            return a.rearrange("p (q t) -> p q t", q=PQ)

        tab_c = [quads(wk(0)), quads(wk(1))]
        tab_s = [quads(wk(2)), quads(wk(3))]
        st_re = [wk(4), wk(5)]
        st_im = [wk(6), wk(7)]
        out_re = quads(wk(8))
        dve_tmp = wk(9)
        pool_tmp = quads(wk(10))

        def sm(i, n=1):
            return small[:, i * PAIRS:(i + n) * PAIRS]

        small_names = ["step", "theta", "turns", "absr", "sin", "cos", "decay", "er", "n_re", "n_im", "den", "f_re",
                       "f_im", "t1", "t2", "w_c", "w_s", "w_c2", "w_s2", "w_t"]
        S = {n: sm(i) for i, n in enumerate(small_names)}

        def st(at, n):
            return stat[:, at:at + n]

        ssq, std, rstd = st(0, TB), st(2, TB), st(4, TB)
        lat_ssq, lat_std_v, lat_rstd = st(6, 4), st(10, 4), st(14, 4)
        kr_ssq, hd_ssq, hd_std, hd_rstd = st(18, TB), st(20, 32), st(52, 32), st(84, 32)
        eps, half_pi, zero = st(116, 1), st(117, 1), st(118, 1)
        row_max, neg_max, row_sum, row_inv = st(120, 16), st(136, 16), st(152, 16), st(168, 16)
        diag = early[:, 0:TB * P].rearrange("p (b t) -> p b t", b=TB)
        powers = attnT.rearrange("p k (q t) -> p k q t", q=PAIRS)
        glu_sigma = wk(9).rearrange("p (m t) -> p m t", m=S5M)
        ssmT = wk(8).rearrange("p (m t) -> p m t", m=S5M)
        gates_w = gates.rearrange("p (w m) t -> p w m t", w=2)
        ff_sigma = wk(0)[:, 0:2 * SEQ].rearrange("p (i t) -> p i t", i=2)
        ff_actT = wk(1, 2).rearrange("p (i f t) -> p i f t", i=2, f=4)
        x_out = gates_t[:, 0:TB * D].rearrange("p (b d) -> p b d", b=TB)
        y_rows = gates_t[:, 2048:2048 + D]
        pick = gates_t[:, 3072:3072 + TB * P].rearrange("p (b j) -> p b j", b=TB)
        spread_tok = gates_t[:, 3328:3328 + TB * P].rearrange("p (b j) -> p b j", b=TB)
        spread = gates_t[:, 3584:3584 + TB * P].rearrange("p (b t) -> p b t", b=TB)
        rowsT = wk(0).rearrange("p (k j) -> p k j", k=KD)
        ex_sigma = wk(1).rearrange("p (i f) -> p i f", i=2)
        ex_a = wk(2).rearrange("p (i f) -> p i f", i=2)
        ex_aT = wk(3).rearrange("p (i k j) -> p i k j", i=2, k=4)
        rt = wk(4)

        def rv(i, dt=F32):
            v = rt[:, 16 * i:16 * i + 16]
            return (v.bitcast(dt) if dt is not F32 else v).rearrange("p (b e) -> p b e", b=TB)

        logits, top, top_i, top_f, sel, comb = rv(0), rv(1), rv(2, U32), rv(3), rv(4), rv(5)
        hot0, hot1, diff, ediff, den2, w_first, w_second = rv(6), rv(7), rv(8), rv(9), rv(10), rv(11), rv(12)
        place = rt[:, 16 * 13:16 * 15].rearrange("p (r b e) -> p r b e", r=2, b=TB)
        uq_loaded, consts_set = sig("uq_loaded", 16), sig("consts_set")
        slot_full = [sig(f"slot_full{s}") for s in range(RING)]
        x_loaded, consts_loaded, params_loaded = sig("x_loaded"), sig("consts_loaded"), sig("params_loaded", 16)
        router_loaded = sig("router_loaded")
        dve_chain, act_chain, pool_chain = sig("dve_chain"), sig("act_chain"), sig("pool_chain")
        x_ready, std_ready, diag_ready = sig("x_ready", 2), sig("std_ready", 2), sig("diag_ready", 2)
        hT_in_psum, hT_act, hT_dve = sig("hT_in_psum", 8), sig("hT_act", 8), sig("hT_dve", 8)
        step_exp, theta_ready, trig_ready = sig("step_exp", 1), sig("theta_ready", 1), sig("trig_ready", 1)
        bbar_ready, bbarT_in_psum, bbarT_ready = sig("bbar_ready", 1), sig("bbarT_in_psum", 1), sig("bbarT_ready", 1)
        table_ready, table_free = sig("table_ready", S5M), sig("table_free", S5M)
        lat_in_psum, lat_biased, lat_std, lat_ready = (sig("lat_in_psum", TB), sig("lat_biased", 1),
                                                       sig("lat_std", 1), sig("lat_ready", 1))
        u_in_psum, u_ready = sig("u_in_psum", S5M), sig("u_ready", S5M)
        gate_in_psum, gate_ready = sig("gate_in_psum", 2 * KD), sig("gate_ready", 2 * KD)
        bu_in_psum, bu_read = sig("bu_in_psum", S5M), sig("bu_read", S5M)
        scanned, states_ready = sig("scanned", S5M), sig("states_ready", S5M)
        y_in_psum, y_ready, gelu_ready = sig("y_in_psum", S5M), sig("y_ready", S5M), sig("gelu_ready", S5M)
        glu_in_psum, glu_sig, ssm_ready = sig("glu_in_psum", S5M), sig("glu_sig", S5M), sig("ssm_ready", S5M)
        latT_in_psum, latT_ready = sig("latT_in_psum", 2), sig("latT_ready", 3)
        qkv_in_psum, qkv_copied = sig("qkv_in_psum", 8), sig("qkv_copied", 8)
        head_ssq, head_std, qk_ready = sig("head_ssq", 1), sig("head_std", 1), sig("qk_ready", 1)
        qkT_in_psum, qkT_copied = sig("qkT_in_psum", H), sig("qkT_copied", H)
        scores_in_psum, scores_masked, max_ready = (sig("scores_in_psum", H), sig("scores_masked", H),
                                                    sig("max_ready", H))
        exp_ready, probs_ready = sig("exp_ready", H), sig("probs_ready", H)
        probsT_in_psum, probsT_copied = sig("probsT_in_psum", H), sig("probsT_copied", H)
        av_in_psum, attn_ready = sig("av_in_psum", H // 2), sig("attn_ready", H // 2)
        proj_in_psum, mix_ready, mixed_in_psum = sig("proj_in_psum", KD), sig("mix_ready", KD), sig("mixed_in_psum", 4)
        ff_in_psum, ff_sig, ff_act = sig("ff_in_psum"), sig("ff_sig"), sig("ff_act")
        ff_down, attn_projected = sig("ff_down"), sig("attn_projected", 1)
        logits_in_psum, top_ready, top_exp, chosen = sig("logits_in_psum"), sig("top_ready"), sig("top_exp"), sig("chosen")
        places_in_psum, places_ready, count_ready = sig("places_in_psum"), sig("places_ready"), sig("count_ready")
        pick_ready, rows_in_psum, rows_ready = sig("pick_ready"), sig("rows_in_psum"), sig("rows_ready")
        spreadT_in_psum, spread_ready = sig("spreadT_in_psum"), sig("spread_ready")
        ex_gate, ex_up, ex_down = sig("ex_gate"), sig("ex_up"), sig("ex_down")
        ex_sig, ex_act = sig("ex_sig"), sig("ex_act")
        actT_in_psum, actT_ready = sig("actT_in_psum"), sig("actT_ready")
        y_rows_ready = sig("y_rows_ready")
        spread_in_psum, spread_added = sig("spread_in_psum"), sig("spread_added")
        out_ready, stored = sig("out_ready"), sig("stored")

        mix_use = {i: (i % MIX_SLOTS, i // MIX_SLOTS + 1) for i in range(N_MIX)}
        ffn_use = {i: (i % RING, i // RING + 1) for i in range(N_FFN)}
        per_slot_layer = [N_MIX // MIX_SLOTS * (s < MIX_SLOTS) + N_FFN // RING for s in range(RING)]
        before_moe = [per_slot_layer[s] + N_MIX // MIX_SLOTS * (s < MIX_SLOTS) for s in range(RING)]
        per_slot_pair = N_PAIR // RING

        def mix_landed(eng, l, i):
            s, k = mix_use[i]
            eng.wait_ge(slot_full[s].sem, l * (16 * per_slot_layer[s]) + 16 * k)

        def ffn_landed(eng, i):
            s, k = ffn_use[i]
            eng.wait_ge(slot_full[s].sem, 16 * (N_MIX // MIX_SLOTS * (s < MIX_SLOTS) + k))

        def moe_landed(eng, turn, i):
            s, k = i % RING, i // RING + 1
            eng.wait_ge(slot_full[s].sem, turn * (16 * per_slot_pair) + 16 * (before_moe[s] + k))

        def slot_view(s, k, n):
            return slots[s][:, 0:k * n].rearrange("p (k n) -> p k n", k=k)

        def rows(w, k):
            return w.rearrange("(k p) n -> p k n", p=P)

        block = ctx.enter_context(nc.Block())

        @block.sync
        def _(sp):
            def layer_of(w, l):
                return w[bass.ds(l, 1)].rearrange("a r n -> (a r) n")

            def mixer_used(l, i):
                what = MIX_ITEMS[i]
                j = int(what[-1]) if what[-1].isdigit() else 0
                signal, n = {"lat": (lat_in_psum, TB), "u": (u_in_psum, S5M), "up": (qkv_in_psum, 8),
                             "gate": (gate_in_psum, 4 * j + 4), "glu": (glu_in_psum, S5M),
                             "proj_a": (attn_projected, 1), "proj_s": (proj_in_psum, KD),
                             "out": (mixed_in_psum, TB * (j + 1))}[what.rstrip("0123456789")]
                sp.wait_ge(signal.sem, signal.at(l, n))

            def ffn_used(i):
                what, c = FFN_ITEMS[i]
                if what == "d":
                    sp.wait_ge(ff_down.sem, c + 1)
                else:
                    sp.wait_ge(ff_in_psum.sem, min(4 * c + 4, FF // P))

            def expert_used(turn, i):
                half, (what, c) = i // N_EXP, MOE_ITEMS[i % N_EXP]
                signal = {"g": ex_gate, "u": ex_up, "d": ex_down}[what]
                sp.wait_ge(signal.sem, turn * (2 * FEC) + (half * FEC + c + 1))

            def load_mixer(l, i):
                what, s = MIX_ITEMS[i], i % MIX_SLOTS
                if what in ("lat", "u") or what.startswith("gate"):
                    c0, n = {"lat": (0, LAT), "u": (LAT, S5W)}.get(what) or (LAT + S5W + 512 * int(what[-1]), 512)
                    dst, src = slot_view(s, KD, n), rows(layer_of(w_in, l)[:, c0:c0 + n], KD)
                elif what == "up":
                    sp.dma_start(slots[s][:, 0:2 * H * QK].rearrange("p (k n) -> p k n", k=2),
                                 rows(layer_of(w_uq, l), 2)).then_inc(uq_loaded.sem, 16)
                    dst, src = slots[s][:, 2048:2048 + 2 * 512], layer_of(w_ukv, l)
                elif what == "glu":
                    dst, src = slot_view(s, S5M, S5W), rows(layer_of(w_glu, l), S5M)
                elif what in ("proj_a", "proj_s"):
                    dst, src = slot_view(s, 4, D), rows(layer_of(w_pa if what == "proj_a" else w_ps, l), 4)
                else:
                    c0 = 512 * int(what[-1])
                    dst, src = slot_view(s, KD, 512), rows(layer_of(w_out, l)[:, c0:c0 + 512], KD)
                sp.dma_start(dst, src).then_inc(slot_full[s].sem, 16)

            def load_ffn(i):
                (what, c), s = FFN_ITEMS[i], i % RING
                n = min(512, FF - 512 * c)
                if what == "d":
                    dst, src = slot_view(s, n // P, D), rows(f_down[0, 512 * c:512 * c + n, :], n // P)
                else:
                    dst = slot_view(s, KD, n)
                    src = rows((f_gate if what == "g" else f_up)[0, :, 512 * c:512 * c + n], KD)
                sp.dma_start(dst, src).then_inc(slot_full[s].sem, 16)

            def load_expert(pair, i):
                half, (what, c), s = i // N_EXP, MOE_ITEMS[i % N_EXP], i % RING
                e = bass.ds(pair * 2 + half, 1)
                if what == "d":
                    dst, src = slot_view(s, 4, D), m_down[e, 512 * c:512 * c + 512, :]
                else:
                    dst, src = slot_view(s, KD, 512), (m_gate if what == "g" else m_up)[e, :, 512 * c:512 * c + 512]
                sp.dma_start(dst, src.rearrange("a (k p) n -> p (a k) n", p=P)).then_inc(slot_full[s].sem, 16)

            for i in range(MIX_SLOTS):
                load_mixer(0, i)
            with sp.Fori(0, DEPTH) as l:
                for i in range(MIX_SLOTS, N_MIX):
                    mixer_used(l, i - MIX_SLOTS)
                    load_mixer(l, i)
                with sp.If(l < 1):
                    sp.wait_ge(attn_ready.sem, H // 2)
                    for i in range(N_FFN):
                        if i >= RING:
                            ffn_used(i - RING)
                        elif i < MIX_SLOTS:
                            mixer_used(0, N_MIX - MIX_SLOTS + i)
                        load_ffn(i)
                    for s in range(MIX_SLOTS):
                        ffn_used(N_FFN - RING + s)
                        load_mixer(1, s)
            sp.wait_ge(attn_ready.sem, DEPTH * (H // 2))
            for i in range(RING):
                if i < MIX_SLOTS:
                    mixer_used(1, N_MIX - MIX_SLOTS + i)
                load_expert(0, i)

            def experts(turn_0):
                def rest(pair):
                    for i in range(RING, N_PAIR):
                        expert_used(pair + turn_0, i - RING)
                        load_expert(pair, i)

                with sp.Fori(1, E // 2) as pair:
                    rest(pair - 1)
                    for i in range(RING):
                        expert_used(pair + (turn_0 - 1), N_PAIR - RING + i)
                        load_expert(pair, i)
                rest(E // 2 - 1)

            experts(0)
            sp.wait_ge(count_ready.sem, 1)
            most = sp.value_load(most_i[0:1, 0:1], min_val=0, max_val=SEQ)
            with sp.If(most > P):
                for i in range(RING):
                    expert_used(E // 2 - 1, N_PAIR - RING + i)
                    load_expert(0, i)
                experts(E // 2)
            sp.wait_ge(out_ready.sem, 1)
            sp.dma_start(out.rearrange("(b p) d -> p b d", p=P), x_out).then_inc(stored.sem, 16)
            sp.wait_ge(stored.sem, 16)

        @block.gpsimd
        def _(pool):
            g = nc.gpsimd
            c = Chain(pool, pool_chain.sem)
            low_c, low_s, high_c, high_s = (powers[:, i] for i in range(4))

            def over(v, n):
                return v.unsqueeze(2).broadcast_to([P, PAIRS, n])

            def doubled(tc, ts, n, wc, ws):
                t = pool_tmp.rearrange("p q (a b) -> p (q a) b", b=16)[:, 0:PAIRS, 0:n]
                new_c, new_s, old_c, old_s = tc[:, :, n:2 * n], ts[:, :, n:2 * n], tc[:, :, 0:n], ts[:, :, 0:n]
                c.add(g.tensor_tensor(new_c, old_c, over(wc, n), ALU.mult))
                c.link(g.tensor_tensor(t, old_s, over(ws, n), ALU.mult))
                c.add(g.tensor_tensor(new_c, new_c, t, ALU.subtract))
                c.link(g.tensor_tensor(new_s, old_s, over(wc, n), ALU.mult))
                c.link(g.tensor_tensor(t, old_c, over(ws, n), ALU.mult))
                c.link(g.tensor_tensor(new_s, new_s, t, ALU.add))

            def squared(wc, ws, out_c, out_s):
                c.add(g.tensor_tensor(out_c, wc, wc, ALU.mult))
                c.add(g.tensor_tensor(S["w_t"], ws, ws, ALU.mult))
                c.link(g.tensor_tensor(out_s, wc, ws, ALU.mult))
                c.add(g.tensor_tensor(out_c, out_c, S["w_t"], ALU.subtract))
                c.add(g.tensor_tensor(out_s, out_s, out_s, ALU.add))

            with pool.Fori(0, DEPTH) as l:
                c.start(l * POOL_MIX)
                pool.wait_ge(trig_ready.sem, trig_ready.at(l, 1))
                w = (S["cos"], S["sin"])
                spare = [(S["w_c"], S["w_s"]), (S["w_c2"], S["w_s2"])]
                squared(*w, *spare[0])
                for tc, ts in ((low_c, low_s), (high_c, high_s)):
                    c.add(g.memset(tc[:, :, 0:1], 1.0))
                    c.add(g.memset(ts[:, :, 0:1], 0.0))
                c.sync()
                for k in range(8):
                    tc, ts = (low_c, low_s) if k < 4 else (high_c, high_s)
                    doubled(tc, ts, 2 ** (k % 4), *w)
                    w = spare[k % 2]
                    if k < 6:
                        squared(*w, *spare[(k + 1) % 2])
                        c.sync()

                def table(m):
                    if m >= 2:
                        pool.wait_ge(bu_read.sem, bu_read.at(l, m - 1))
                    q = slice(PQ * m, PQ * m + PQ)
                    lo = [v[:, q].unsqueeze(2).broadcast_to([P, PQ, 16, 16]) for v in (low_c, low_s)]
                    hi = [v[:, q].unsqueeze(3).broadcast_to([P, PQ, 16, 16]) for v in (high_c, high_s)]
                    tc, ts, t = (v.rearrange("p q (a b) -> p q a b", b=16) for v in
                                 (tab_c[m % 2], tab_s[m % 2], pool_tmp))
                    c.add(g.tensor_tensor(tc, hi[0], lo[0], ALU.mult))
                    c.add(g.tensor_tensor(ts, hi[1], lo[0], ALU.mult))
                    c.link(g.tensor_tensor(t, hi[1], lo[1], ALU.mult))
                    c.link(g.tensor_tensor(tc, tc, t, ALU.subtract))
                    c.link(g.tensor_tensor(t, hi[0], lo[1], ALU.mult))
                    g.tensor_tensor(ts, ts, t, ALU.add).then_inc(table_ready.sem, 1)
                    pool.wait_ge(table_ready.sem, table_ready.at(l, m + 1))

                def turn_back(m):
                    i = m % 2
                    re, im = quads(st_re[i]), quads(st_im[i])
                    pool.wait_ge(scanned.sem, scanned.at(l, m + 1))
                    if m >= 1:
                        pool.wait_ge(y_in_psum.sem, y_in_psum.at(l, m))
                    c.add(g.tensor_tensor(out_re, re, tab_c[i], ALU.mult))
                    c.link(g.tensor_tensor(pool_tmp, im, tab_s[i], ALU.mult))
                    c.add(g.tensor_tensor(out_re, out_re, pool_tmp, ALU.subtract))
                    c.add(g.tensor_tensor(im, im, tab_c[i], ALU.mult))
                    c.link(g.tensor_tensor(re, re, tab_s[i], ALU.mult))
                    g.tensor_tensor(im, im, re, ALU.add).then_inc(states_ready.sem, 1)
                    pool.wait_ge(states_ready.sem, states_ready.at(l, m + 1))

                table(0)
                table(1)
                for m in range(S5M):
                    turn_back(m)
                    if m + 2 < S5M:
                        table(m + 2)
                assert c.n == POOL_MIX, c.n

        @block.scalar
        def _(act):
            a = nc.scalar
            c = Chain(act, act_chain.sem)
            act.dma_start(x, x_in.rearrange("(b p) d -> p b d", p=P)).then_inc(x_loaded.sem, 16)
            act.dma_start(pl[:, :], params[0]).then_inc(params_loaded.sem, 16)
            act.dma_start(cst[:, :], consts).then_inc(consts_loaded.sem, 16)
            act.dma_start(router_sb, router[0].rearrange("(k p) e -> p k e", p=P)).then_inc(router_loaded.sem, 16)
            junk = [tail[:, D * i:D * (i + 1)] for i in range(4)]

            def norm(l, k):
                act.wait_ge(x_ready.sem, x_ready.at(l, 1 + k))
                for b in range(TB):
                    c.add(a.activation((uT, attnT)[b].rearrange("p m t -> p (m t)"), x[:, b], ACT.Square, accum_out=ssq[:, b:b + 1]))
                c.sync()
                a.activation(std, ssq, ACT.Sqrt, scale=1.0 / D, bias=eps).then_inc(std_ready.sem, 1)

            def normed(l, k):
                gain = field["g_mix"] if k == 0 else field["g_ffn"]
                for j in (0, 2):
                    act.wait_ge(hT_in_psum.sem, hT_in_psum.at(l, 4 * k + j + 1))
                    for i in range(2):
                        kt = 2 * j + i
                        a.activation(hT[:, kt], psum[:, j, i * SEQ:(i + 1) * SEQ], ACT.Copy,
                                     scale=gain[:, kt:kt + 1]).then_inc(hT_act.sem, 1)

            act.wait_ge(consts_set.sem, 3)
            with act.Fori(0, DEPTH) as l:
                c.start(l * (ACT_MIX + ACT_FFN))
                norm(l, 0)
                act.wait_ge(params_loaded.sem, params_loaded.at(l, 16))
                a.activation(S["step"], field["log_step"], ACT.Exp).then_inc(step_exp.sem, 1)
                normed(l, 0)
                act.wait_ge(theta_ready.sem, theta_ready.at(l, 1))
                a.activation(S["decay"], S["er"], ACT.Exp)
                a.activation(S["sin"], S["theta"], ACT.Sin, bias=zero)
                a.activation(S["cos"], S["absr"], ACT.Sin, scale=-1.0, bias=half_pi).then_inc(trig_ready.sem, 1)
                act.wait_ge(lat_biased.sem, lat_biased.at(l, 1))
                for b in range(TB):
                    c.add(a.activation(junk[b][:, 0:QR], lat[:, b, 0:QR], ACT.Square, accum_out=lat_ssq[:, b:b + 1]))
                    c.add(a.activation(junk[2 + b][:, 0:KR], lat[:, b, QR:QR + KR], ACT.Square,
                                       accum_out=lat_ssq[:, 2 + b:3 + b]))
                c.sync()
                a.activation(lat_std_v[:, 0:2], lat_ssq[:, 0:2], ACT.Sqrt, scale=1.0 / QR, bias=eps)
                a.activation(lat_std_v[:, 2:4], lat_ssq[:, 2:4], ACT.Sqrt, scale=1.0 / KR,
                             bias=eps).then_inc(lat_std.sem, 1)
                act.wait_ge(bbarT_in_psum.sem, bbarT_in_psum.at(l, 1))
                for j in range(2):
                    ins = a.activation(bT[:, 2 * j:2 * j + 2], psum[:, 6 + j].rearrange(
                        "p (m r s) -> p m r s", m=2, r=2), ACT.Copy)
                ins.then_inc(bbarT_ready.sem, 1)
                for m in range(S5M):
                    act.wait_ge(u_in_psum.sem, u_in_psum.at(l, m + 1))
                    a.activation(uT[:, m], psum[:, 6 + m % 2, 0:SEQ], ACT.Identity,
                                 bias=field["b_u"][:, m:m + 1]).then_inc(u_ready.sem, 1)
                act.wait_ge(latT_in_psum.sem, latT_in_psum.at(l, 1))
                for k in range(2):
                    a.activation(qlT[:, k], psum[:, 4, k * SEQ:(k + 1) * SEQ], ACT.Copy,
                                 scale=field["g_q"][:, k:k + 1]).then_inc(latT_ready.sem, 1)
                act.wait_ge(latT_in_psum.sem, latT_in_psum.at(l, 2))
                a.activation(kvT, psum[:, 5, 0:SEQ], ACT.Copy, scale=field["g_kv"][:, 0:1]).then_inc(latT_ready.sem, 1)

                def gate(g):
                    act.wait_ge(gate_in_psum.sem, gate_in_psum.at(l, g + 1))
                    a.activation(gates[:, g], psum[:, 6 + g % 2, 0:SEQ], ACT.Sigmoid,
                                 bias=field["b_gate"][:, g:g + 1]).then_inc(gate_ready.sem, 1)

                def gelu(m):
                    act.wait_ge(y_ready.sem, y_ready.at(l, m + 1))
                    a.activation(uT[:, m], uT[:, m], ACT.Gelu_apprx_tanh).then_inc(gelu_ready.sem, 1)

                for g in range(4):
                    gate(g)
                for n in range(8):
                    act.wait_ge(qkv_in_psum.sem, qkv_in_psum.at(l, n + 1))
                    b, half = n % 4 // 2, n % 2
                    heads = slice(4 * half, 4 * half + 4)
                    if n < 4:
                        ins = a.activation(q_tok[:, b, heads], psum[:, 4 + n % 2, 0:4 * QK].rearrange(
                            "p (h n) -> p h n", h=4), ACT.Copy)
                    else:
                        kv = psum[:, 4 + n % 2].rearrange("p (h n) -> p h n", h=4)
                        a.activation(k_tok[:, b, heads, 0:NOPE], kv[:, :, 0:NOPE], ACT.Copy)
                        ins = a.activation(v_tok[:, b, heads], kv[:, :, NOPE:], ACT.Copy)
                    ins.then_inc(qkv_copied.sem, 1)
                act.wait_ge(head_ssq.sem, head_ssq.at(l, 1))
                a.activation(hd_std, hd_ssq, ACT.Sqrt, scale=1.0 / QK, bias=eps).then_inc(head_std.sem, 1)
                for g in range(4, 16):
                    gate(g)
                for m in range(S5M):
                    gelu(m)
                for h in range(H):
                    act.wait_ge(qkT_in_psum.sem, qkT_in_psum.at(l, h + 1))
                    a.activation(qkT[0:QK, h], psum[0:QK, h].rearrange("p (w t) -> p w t", w=2),
                                 ACT.Copy).then_inc(qkT_copied.sem, 1)
                for h in range(H):
                    act.wait_ge(max_ready.sem, max_ready.at(l, h + 1))
                    a.activation(probs[:, h, 0:P], probs[:, h, 0:P], ACT.Exp, scale=SCALE,
                                 bias=neg_max[:, 2 * h:2 * h + 1], accum_out=row_sum[:, 2 * h:2 * h + 1])
                    a.activation(probs[:, h, P:3 * P], probs[:, h, P:3 * P], ACT.Exp, scale=SCALE,
                                 bias=neg_max[:, 2 * h + 1:2 * h + 2],
                                 accum_out=row_sum[:, 2 * h + 1:2 * h + 2]).then_inc(exp_ready.sem, 1)
                for h in range(H):
                    act.wait_ge(probsT_in_psum.sem, probsT_in_psum.at(l, h + 1))
                    a.activation(probsT[:, h], psum[:, h, 0:3 * P], ACT.Copy).then_inc(probsT_copied.sem, 1)
                for m in range(S5M):
                    act.wait_ge(glu_in_psum.sem, glu_in_psum.at(l, m + 1))
                    a.activation(glu_sigma[:, m], psum[:, 2 * m + 1, 0:SEQ], ACT.Sigmoid,
                                 bias=field["b_glu"][:, m:m + 1]).then_inc(glu_sig.sem, 1)
                norm(l, 1)
                normed(l, 1)
                assert c.n == ACT_MIX, c.n
                with act.If(l < 1):
                    act.wait_ge(hT_dve.sem, 8)
                    act.wait_ge(hT_act.sem, 8)
                    act.dma_start(pl[:, :], params[1]).then_inc(params_loaded.sem, 16)
                    for f in range(FF // P):
                        act.wait_ge(ff_in_psum.sem, f + 1)
                        if f >= 2:
                            act.wait_ge(ff_act.sem, f - 1)
                        a.activation(ff_sigma[:, f % 2], psum[:, 4 + f % 4, 0:SEQ],
                                     ACT.Sigmoid).then_inc(ff_sig.sem, 1)

            act.wait_ge(top_ready.sem, 1)
            a.activation(ediff[:, :, 0:1], diff[:, :, 0:1], ACT.Exp).then_inc(top_exp.sem, 1)

            def experts(turn):
                for half in range(2):
                    def at(per, n):
                        return turn * (2 * per) + (half * per + n)

                    def sigma(ch):
                        act.wait_ge(ex_gate.sem, at(FEC, ch + 1))
                        if ch >= 2:
                            act.wait_ge(ex_act.sem, at(FEC, ch - 1))
                        a.activation(ex_sigma[:, ch % 2], psum[:, ch % 2], ACT.Sigmoid).then_inc(ex_sig.sem, 1)

                    def turned(ch):
                        act.wait_ge(actT_in_psum.sem, at(FEC, ch + 1))
                        a.activation(ex_aT[:, ch % 2], psum[:, 6].rearrange("p (k j) -> p k j", k=4),
                                     ACT.Copy).then_inc(actT_ready.sem, 1)

                    sigma(0)
                    for ch in range(1, FEC):
                        turned(ch - 1)
                        sigma(ch)
                    turned(FEC - 1)
                    act.wait_ge(ex_down.sem, at(FEC, FEC))
                    for j in range(2):
                        ins = a.activation(y_rows[:, 512 * j:512 * j + 512], psum[:, 4 + j], ACT.Copy)
                    ins.then_inc(y_rows_ready.sem, 1)

            with act.Fori(0, E // 2) as pair:
                experts(pair)
            act.wait_ge(count_ready.sem, 1)
            most = act.value_load(most_i[0:1, 0:1], min_val=0, max_val=SEQ)
            with act.If(most > P):
                with act.Fori(0, E // 2) as pair:
                    experts(pair + E // 2)

        @block.tensor
        def _(pe):
            t = nc.tensor

            pe.wait_ge(consts_loaded.sem, 16)

            def norm_transposes(l, k):
                pe.wait_ge(diag_ready.sem, diag_ready.at(l, k + 1))
                for kt in range(KD):
                    for b in range(TB):
                        at = (kt % 2) * SEQ + b * P
                        ins = t.matmul(psum[:, kt // 2, at:at + P], x[:, b, kt * P:(kt + 1) * P], diag[:, b],
                                       start=True, stop=True)
                    if kt % 2:
                        ins.then_inc(hT_in_psum.sem, 1)

            def wait_hT(l, k):
                pe.wait_ge(hT_act.sem, hT_act.at(l, 4 * k + 4))
                pe.wait_ge(hT_dve.sem, hT_dve.at(l, 4 * k + 4))

            with pe.Fori(0, DEPTH) as l:
                norm_transposes(l, 0)
                wait_hT(l, 0)
                mix_landed(pe, l, 0)
                w = slot_view(0, KD, LAT)
                for b in range(TB):
                    for kt in range(KD):
                        ins = t.matmul(psum[:, 4 + b, 0:LAT], hT[:, kt, b * P:(b + 1) * P], w[:, kt],
                                       start=kt == 0, stop=kt == KD - 1)
                    ins.then_inc(lat_in_psum.sem, 1)
                pe.wait_ge(bbar_ready.sem, bbar_ready.at(l, 1))
                for m in range(S5M):
                    for r, f in enumerate(("b_re", "b_im")):
                        at = (m % 2) * 2 * P + r * P
                        ins = t.transpose(psum[:, 6 + m // 2, at:at + P], field[f][:, m * P:(m + 1) * P], ident)
                ins.then_inc(bbarT_in_psum.sem, 1)
                pe.wait_ge(bbarT_ready.sem, bbarT_ready.at(l, 1))
                mix_landed(pe, l, 1)
                w = slot_view(1, KD, S5W)
                for m in range(S5M):
                    if m >= 2:
                        pe.wait_ge(u_ready.sem, u_ready.at(l, m - 1))
                    for kt in range(KD):
                        ins = t.matmul(psum[:, 6 + m % 2, 0:SEQ],
                                       w[:, kt, m * P:(m + 1) * P], hT[:, kt], start=kt == 0, stop=kt == KD - 1)
                    ins.then_inc(u_in_psum.sem, 1)
                pe.wait_ge(lat_ready.sem, lat_ready.at(l, 1))
                for k in range(2):
                    for b in range(TB):
                        ins = t.transpose(psum[:, 4, k * SEQ + b * P:k * SEQ + (b + 1) * P],
                                          lat[:, b, k * P:(k + 1) * P], ident)
                ins.then_inc(latT_in_psum.sem, 1)
                for b in range(TB):
                    ins = t.transpose(psum[:, 5, b * P:(b + 1) * P], lat[:, b, QR:QR + KR], ident)
                ins.then_inc(latT_in_psum.sem, 1)

                def input_states(m):
                    pe.wait_ge(u_ready.sem, u_ready.at(l, m + 1))
                    if m:
                        pe.wait_ge(bu_read.sem, bu_read.at(l, m))
                    for r in range(2):
                        for q in range(PQ):
                            rows_q = slice(32 * q, 32 * q + 32)
                            ins = t.matmul(psum[:, q, r * SEQ:(r + 1) * SEQ], bT[rows_q, m, r],
                                           uT[rows_q, m], start=True, stop=True)
                    ins.then_inc(bu_in_psum.sem, 1)

                def read_out(m):
                    pe.wait_ge(states_ready.sem, states_ready.at(l, m + 1))
                    if m >= 2:
                        pe.wait_ge(y_ready.sem, y_ready.at(l, m - 1))
                    im = quads(st_im[m % 2])
                    for q in range(PQ):
                        col = (PQ * m + q) * 32
                        o = psum[32 * q:32 * q + 32, 4 + m % 2, 0:SEQ]
                        t.matmul(o, field["c_re"][:, col:col + 32], out_re[:, q], start=True, stop=False)
                        ins = t.matmul(o, field["c_im"][:, col:col + 32], im[:, q], start=False, stop=True)
                    ins.then_inc(y_in_psum.sem, 1)

                def gate_products(j):
                    item = MIX_ITEMS.index(f"gate{j}")
                    mix_landed(pe, l, item)
                    w = slot_view(item % MIX_SLOTS, KD, 512)
                    for i in range(4):
                        g = 4 * j + i
                        if g >= 2:
                            pe.wait_ge(gate_ready.sem, gate_ready.at(l, g - 1))
                        else:
                            pe.wait_ge(u_ready.sem, u_ready.at(l, S5M))
                        for kt in range(KD):
                            ins = t.matmul(psum[:, 6 + g % 2, 0:SEQ], w[:, kt, i * P:(i + 1) * P], hT[:, kt],
                                           start=kt == 0, stop=kt == KD - 1)
                        ins.then_inc(gate_in_psum.sem, 1)

                input_states(0)
                gate_products(0)
                pe.wait_ge(latT_ready.sem, latT_ready.at(l, 3))
                item = MIX_ITEMS.index("up")
                mix_landed(pe, l, item)
                pe.wait_ge(uq_loaded.sem, uq_loaded.at(l, 16))
                s = item % MIX_SLOTS
                wq = slots[s][:, 0:2 * H * QK].rearrange("p (k n) -> p k n", k=2)
                for n in range(8):
                    b, half = n % 4 // 2, n % 2
                    if n >= 2:
                        pe.wait_ge(qkv_copied.sem, qkv_copied.at(l, n - 1))
                    if n < 4:
                        for k in range(2):
                            ins = t.matmul(psum[:, 4 + n % 2, 0:4 * QK], qlT[:, k, b * P:(b + 1) * P],
                                           wq[:, k, half * 4 * QK:(half + 1) * 4 * QK], start=k == 0, stop=k == 1)
                    else:
                        ins = t.matmul(psum[:, 4 + n % 2], kvT[:, b * P:(b + 1) * P],
                                       slots[s][:, 2048 + half * 512:2048 + half * 512 + 512], start=True, stop=True)
                    ins.then_inc(qkv_in_psum.sem, 1)
                input_states(1)
                gate_products(1)
                pe.wait_ge(qkv_copied.sem, qkv_copied.at(l, 8))
                read_out(0)
                input_states(2)
                gate_products(2)
                read_out(1)
                input_states(3)
                gate_products(3)
                read_out(2)
                read_out(3)
                pe.wait_ge(qk_ready.sem, qk_ready.at(l, 1))
                pe.wait_ge(bu_read.sem, bu_read.at(l, S5M))
                pe.wait_ge(y_ready.sem, y_ready.at(l, S5M))
                pe.wait_ge(gate_ready.sem, gate_ready.at(l, 2 * KD))
                for h in range(H):
                    for i, tok in enumerate((q_tok, k_tok)):
                        for b in range(TB):
                            ins = t.transpose(psum[0:QK, h, i * SEQ + b * P:i * SEQ + (b + 1) * P], tok[:, b, h],
                                              ident)
                    ins.then_inc(qkT_in_psum.sem, 1)
                for h in range(H):
                    pe.wait_ge(qkT_copied.sem, qkT_copied.at(l, h + 1))
                    t.matmul(psum[:, h, 0:P], qkT[0:QK, h, 0, 0:P], qkT[0:QK, h, 1, 0:P], start=True, stop=True)
                    t.matmul(psum[:, h, P:3 * P], qkT[0:QK, h, 0, P:2 * P], qkT[0:QK, h, 1],
                             start=True, stop=True).then_inc(scores_in_psum.sem, 1)
                for h in range(H):
                    pe.wait_ge(probs_ready.sem, probs_ready.at(l, h + 1))
                    for i in range(3):
                        ins = t.transpose(psum[:, h, i * P:(i + 1) * P], probs[:, h, i * P:(i + 1) * P], ident)
                    ins.then_inc(probsT_in_psum.sem, 1)
                for j in range(H // 2):
                    pe.wait_ge(probsT_copied.sem, probsT_copied.at(l, 2 * j + 2))
                    for i in range(2):
                        h = 2 * j + i
                        o = psum[VD * i:VD * i + VD, 2 * j]
                        t.matmul(o[:, 0:P], v_tok[:, 0, h], probsT[:, h, 0:P], start=True, stop=True)
                        t.matmul(o[:, P:2 * P], v_tok[:, 0, h], probsT[:, h, P:2 * P], start=True, stop=False)
                        ins = t.matmul(o[:, P:2 * P], v_tok[:, 1, h], probsT[:, h, 2 * P:3 * P],
                                       start=False, stop=True)
                    ins.then_inc(av_in_psum.sem, 1)
                item = MIX_ITEMS.index("glu")
                mix_landed(pe, l, item)
                pe.wait_ge(gelu_ready.sem, gelu_ready.at(l, S5M))
                w = slot_view(item % MIX_SLOTS, S5M, S5W)
                for m in range(S5M):
                    for kt in range(S5M):
                        ins = t.matmul(psum[:, 2 * m + 1, 0:SEQ], w[:, kt, m * P:(m + 1) * P], uT[:, kt],
                                       start=kt == 0, stop=kt == S5M - 1)
                    ins.then_inc(glu_in_psum.sem, 1)
                pe.wait_ge(glu_sig.sem, glu_sig.at(l, S5M))
                for i, (what, src) in enumerate((("proj_a", attnT), ("proj_s", ssmT))):
                    item = MIX_ITEMS.index(what)
                    mix_landed(pe, l, item)
                    if i == 0:
                        pe.wait_ge(attn_ready.sem, attn_ready.at(l, H // 2))
                    else:
                        pe.wait_ge(ssm_ready.sem, ssm_ready.at(l, S5M))
                    w = slot_view(item % MIX_SLOTS, 4, D)
                    for m in range(KD):
                        for kt in range(4):
                            ins = t.matmul(psum[:, m, i * SEQ:(i + 1) * SEQ], w[:, kt, m * P:(m + 1) * P], src[:, kt],
                                           start=kt == 0, stop=kt == 3)
                        if i:
                            ins.then_inc(proj_in_psum.sem, 1)
                    if i == 0:
                        ins.then_inc(attn_projected.sem, 1)
                pe.wait_ge(mix_ready.sem, mix_ready.at(l, KD))
                for c in range(2):
                    item = MIX_ITEMS.index(f"out{c}")
                    mix_landed(pe, l, item)
                    w = slot_view(item % MIX_SLOTS, KD, 512)
                    for b in range(TB):
                        for kt in range(KD):
                            ins = t.matmul(psum[:, 2 * c + b], gates[:, kt, b * P:(b + 1) * P], w[:, kt],
                                           start=kt == 0, stop=kt == KD - 1)
                        ins.then_inc(mixed_in_psum.sem, 1)
                norm_transposes(l, 1)
                wait_hT(l, 1)
                with pe.If(l < 1):
                    tiles = [min(4, FF // P - 4 * c) for c in range(FFC)]

                    def gate_up(c):
                        ig, iu = FFN_ITEMS.index(("g", c)), FFN_ITEMS.index(("u", c))
                        ffn_landed(pe, ig)
                        ffn_landed(pe, iu)
                        wg, wu = (slot_view(i % RING, KD, tiles[c] * P) for i in (ig, iu))
                        for f in range(tiles[c]):
                            n = 4 * c + f
                            if n >= 4:
                                pe.wait_ge(ff_act.sem, n - 3)
                            for i, w in enumerate((wg, wu)):
                                for kt in range(KD):
                                    ins = t.matmul(psum[:, 4 + n % 4, i * SEQ:(i + 1) * SEQ],
                                                   w[:, kt, f * P:(f + 1) * P], hT[:, kt],
                                                   start=kt == 0, stop=kt == KD - 1)
                            ins.then_inc(ff_in_psum.sem, 1)

                    def down(c):
                        item = FFN_ITEMS.index(("d", c))
                        ffn_landed(pe, item)
                        w = slot_view(item % RING, tiles[c], D)
                        for f in range(tiles[c]):
                            n = 4 * c + f
                            pe.wait_ge(ff_act.sem, n + 1)
                            for b in range(TB):
                                for j in range(2):
                                    ins = t.matmul(psum[:, 2 * b + j], ff_actT[:, c % 2, f, b * P:(b + 1) * P],
                                                   w[:, f, 512 * j:512 * j + 512], start=n == 0,
                                                   stop=n == FF // P - 1)
                        ins.then_inc(ff_down.sem, 1)

                    gate_up(0)
                    for c in range(1, FFC):
                        gate_up(c)
                        down(c - 1)
                    down(FFC - 1)

            pe.wait_ge(router_loaded.sem, 16)
            for b in range(TB):
                for kt in range(KD):
                    ins = t.matmul(psum[:, 4, b * E:(b + 1) * E], hT[:, kt, b * P:(b + 1) * P], router_sb[:, kt],
                                   start=kt == 0, stop=kt == KD - 1)
            ins.then_inc(logits_in_psum.sem, 1)
            pe.wait_ge(chosen.sem, 1)
            before, ones = const["before"], const["ones"]
            t.matmul(psum[:, 5, 0:E], before, sel[:, 0], start=True, stop=True)
            t.matmul(psum[:, 5, E:2 * E], before, sel[:, 1], start=True, stop=False)
            t.matmul(psum[:, 5, E:2 * E], ones, sel[:, 0], start=False, stop=True)
            t.matmul(psum[:, 5, 2 * E:3 * E], ones, sel[:, 0], start=True, stop=False)
            t.matmul(psum[:, 5, 2 * E:3 * E], ones, sel[:, 1], start=False, stop=True).then_inc(places_in_psum.sem, 1)

            def experts(turn):
                for half in range(2):
                    def at(per, n):
                        return turn * (2 * per) + (half * per + n)

                    def item(what, ch):
                        i = half * N_EXP + MOE_ITEMS.index((what, ch))
                        moe_landed(pe, turn, i)
                        return slot_view(i % RING, *((4, D) if what == "d" else (KD, 512)))

                    def product(what, ch):
                        w = item(what, ch)
                        bank = ch % 2 + (2 if what == "u" else 0)
                        for kt in range(KD):
                            ins = t.matmul(psum[:, bank], rowsT[:, kt], w[:, kt], start=kt == 0, stop=kt == KD - 1)
                        ins.then_inc((ex_up if what == "u" else ex_gate).sem, 1)

                    def turn_act(ch):
                        pe.wait_ge(ex_act.sem, at(FEC, ch + 1))
                        for k in range(4):
                            ins = t.transpose(psum[:, 6, k * P:(k + 1) * P], ex_a[:, ch % 2, k * P:(k + 1) * P],
                                              ident)
                        ins.then_inc(actT_in_psum.sem, 1)

                    def down(ch):
                        w = item("d", ch)
                        pe.wait_ge(actT_ready.sem, at(FEC, ch + 1))
                        for j in range(2):
                            for k in range(4):
                                ins = t.matmul(psum[:, 4 + j], ex_aT[:, ch % 2, k], w[:, k, 512 * j:512 * j + 512],
                                               start=ch == 0 and k == 0, stop=ch == FEC - 1 and k == 3)
                        ins.then_inc(ex_down.sem, 1)

                    pe.wait_ge(pick_ready.sem, at(1, 1))
                    for b in range(TB):
                        ins = t.transpose(psum[:, 1, b * P:(b + 1) * P], spread_tok[:, b], ident)
                    ins.then_inc(spreadT_in_psum.sem, 1)
                    for kt in range(KD):
                        for b in range(TB):
                            ins = t.matmul(psum[:, 6 + kt // 4, (kt % 4) * P:(kt % 4 + 1) * P],
                                           x[:, b, kt * P:(kt + 1) * P], pick[:, b], start=b == 0, stop=b == TB - 1)
                        if kt % 4 == 3:
                            ins.then_inc(rows_in_psum.sem, 1)
                    pe.wait_ge(spread_ready.sem, at(1, 1))
                    pe.wait_ge(rows_ready.sem, at(2, 2))
                    product("g", 0)
                    product("u", 0)
                    for ch in range(1, FEC):
                        product("g", ch)
                        turn_act(ch - 1)
                        product("u", ch)
                        down(ch - 1)
                    turn_act(FEC - 1)
                    down(FEC - 1)
                    pe.wait_ge(y_rows_ready.sem, at(1, 1))
                    for n in range(4):
                        if n >= 2:
                            pe.wait_ge(spread_added.sem, at(4, n - 1))
                        b, j = n // 2, n % 2
                        t.matmul(psum[:, 6 + n % 2], spread[:, b], y_rows[:, 512 * j:512 * j + 512],
                                 start=True, stop=True).then_inc(spread_in_psum.sem, 1)

            with pe.Fori(0, E // 2) as pair:
                experts(pair)
            pe.wait_ge(count_ready.sem, 1)
            most = pe.value_load(most_i[0:1, 0:1], min_val=0, max_val=SEQ)
            with pe.If(most > P):
                with pe.Fori(0, E // 2) as pair:
                    experts(pair + E // 2)

        @block.vector
        def _(dve):
            v = nc.vector
            c = Chain(dve, dve_chain.sem)

            def tt(o, a, b, op):
                return v.tensor_tensor(o, a, b, op)

            def row(f, n, shape):
                return field[f][:, 0:n].unsqueeze(1).broadcast_to(shape)

            def norm(l, k):
                dve.wait_ge(std_ready.sem, std_ready.at(l, k + 1))
                c.link(v.reciprocal(rstd, std))
                for b in range(TB):
                    ins = v.tensor_scalar(diag[:, b], ident, rstd[:, b:b + 1], None, ALU.mult)
                ins.then_inc(diag_ready.sem, 1)

            def normed(l, k):
                gain = field["g_mix"] if k == 0 else field["g_ffn"]
                for j in (1, 3):
                    dve.wait_ge(hT_in_psum.sem, hT_in_psum.at(l, 4 * k + j + 1))
                    for i in range(2):
                        kt = 2 * j + i
                        v.tensor_scalar(hT[:, kt], psum[:, j, i * SEQ:(i + 1) * SEQ], gain[:, kt:kt + 1], None,
                                        ALU.mult).then_inc(hT_dve.sem, 1)

            v.memset(eps, EPS).then_inc(consts_set.sem, 1)
            v.memset(half_pi, float(np.pi / 2)).then_inc(consts_set.sem, 1)
            v.memset(zero, 0.0).then_inc(consts_set.sem, 1)
            dve.wait_ge(consts_loaded.sem, 16)
            dve.wait_ge(x_loaded.sem, 16)
            dve.sem_inc(x_ready.sem, 1)
            with dve.Fori(0, DEPTH) as l:
                c.start(l * (DVE_MIX + DVE_FFN))
                norm(l, 0)
                dve.wait_ge(step_exp.sem, step_exp.at(l, 1))
                c.add(tt(S["er"], field["lam_re"], S["step"], ALU.mult))
                c.link(tt(S["theta"], field["lam_im"], S["step"], ALU.mult))
                c.link(v.tensor_scalar(S["turns"], S["theta"], float(1 / (2 * np.pi)), MAGIC, ALU.mult, ALU.add))
                c.link(v.tensor_scalar(S["turns"], S["turns"], MAGIC, None, ALU.subtract))
                for part in (PI2_A, PI2_B, PI2_C):
                    c.link(v.scalar_tensor_tensor(S["theta"], S["turns"], -part, S["theta"], ALU.mult, ALU.add))
                c.link(v.tensor_scalar(S["theta"], S["theta"], float(np.float32(3.1415925)), -float(np.float32(3.1415925)),
                                       ALU.min, ALU.max))
                c.link(v.tensor_scalar(S["t1"], S["theta"], -1.0, None, ALU.mult))
                tt(S["absr"], S["theta"], S["t1"], ALU.max).then_inc(theta_ready.sem, 1)
                normed(l, 0)
                dve.wait_ge(trig_ready.sem, trig_ready.at(l, 1))
                c.add(tt(S["n_re"], S["decay"], S["cos"], ALU.mult))
                c.add(tt(S["n_im"], S["decay"], S["sin"], ALU.mult))
                c.add(tt(S["den"], field["lam_re"], field["lam_re"], ALU.mult))
                c.link(tt(S["t1"], field["lam_im"], field["lam_im"], ALU.mult))
                c.add(v.tensor_scalar(S["n_re"], S["n_re"], 1.0, None, ALU.subtract))
                c.link(tt(S["den"], S["den"], S["t1"], ALU.add))
                c.add(v.reciprocal(S["den"], S["den"]))
                c.add(tt(S["f_re"], S["n_re"], field["lam_re"], ALU.mult))
                c.add(tt(S["t1"], S["n_im"], field["lam_im"], ALU.mult))
                c.add(tt(S["f_im"], S["n_im"], field["lam_re"], ALU.mult))
                c.link(tt(S["t2"], S["n_re"], field["lam_im"], ALU.mult))
                c.add(tt(S["f_re"], S["f_re"], S["t1"], ALU.add))
                c.link(tt(S["f_im"], S["f_im"], S["t2"], ALU.subtract))
                c.add(tt(S["f_re"], S["f_re"], S["den"], ALU.mult))
                c.link(tt(S["f_im"], S["f_im"], S["den"], ALU.mult))
                b_re, b_im = (field[f].rearrange("p (q n) -> p q n", q=PAIRS) for f in ("b_re", "b_im"))
                f_re, f_im = (S[f].unsqueeze(2).broadcast_to([P, PAIRS, 32]) for f in ("f_re", "f_im"))
                tmp = [dve_tmp[:, 512 * i:512 * i + 512].rearrange("p (q n) -> p q n", q=PAIRS) for i in range(2)]
                c.add(tt(tmp[0], b_im, f_im, ALU.mult))
                c.link(tt(tmp[1], b_re, f_im, ALU.mult))
                c.add(tt(b_re, b_re, f_re, ALU.mult))
                c.link(tt(b_im, b_im, f_re, ALU.mult))
                c.add(tt(b_re, b_re, tmp[0], ALU.subtract))
                tt(b_im, b_im, tmp[1], ALU.add).then_inc(bbar_ready.sem, 1)
                c.add(v.tensor_scalar(field["c_im"], field["c_im"], -1.0, None, ALU.mult))
                for b in range(TB):
                    dve.wait_ge(lat_in_psum.sem, lat_in_psum.at(l, b + 1))
                    ins = tt(lat[:, b], psum[:, 4 + b, 0:LAT], field["b_lat"], ALU.add)
                    if b == 0:
                        c.add(ins)
                ins.then_inc(lat_biased.sem, 1)
                dve.wait_ge(lat_std.sem, lat_std.at(l, 1))
                dve.wait_ge(lat_biased.sem, lat_biased.at(l, 1))
                c.link(v.reciprocal(lat_rstd, lat_std_v))
                for b in range(TB):
                    c.add(v.tensor_scalar(lat[:, b, 0:QR], lat[:, b, 0:QR], lat_rstd[:, b:b + 1], None, ALU.mult))
                    ins = v.tensor_scalar(lat[:, b, QR:QR + KR], lat[:, b, QR:QR + KR], lat_rstd[:, 2 + b:3 + b],
                                          None, ALU.mult)
                    if b == 0:
                        c.add(ins)
                ins.then_inc(lat_ready.sem, 1)

                def states(m):
                    i = m % 2
                    dve.wait_ge(bu_in_psum.sem, bu_in_psum.at(l, m + 1))
                    dve.wait_ge(table_ready.sem, table_ready.at(l, m + 1))
                    if m >= 2:
                        dve.wait_ge(y_in_psum.sem, y_in_psum.at(l, m - 1))
                    bu_re, bu_im = psum[:, 0:PQ, 0:SEQ], psum[:, 0:PQ, SEQ:2 * SEQ]
                    re, im, tmp = quads(st_re[i]), quads(st_im[i]), quads(dve_tmp)
                    c.add(tt(re, bu_re, tab_c[i], ALU.mult))
                    c.add(tt(im, bu_im, tab_c[i], ALU.mult))
                    c.link(tt(tmp, bu_im, tab_s[i], ALU.mult))
                    c.link(tt(re, re, tmp, ALU.add))
                    tt(tmp, bu_re, tab_s[i], ALU.mult).then_inc(bu_read.sem, 1)
                    dve.wait_ge(bu_read.sem, bu_read.at(l, m + 1))
                    c.link(tt(im, im, tmp, ALU.subtract))
                    for s in (re, im):
                        for q in range(PQ):
                            decay = S["decay"][:, PQ * m + q:PQ * m + q + 1].broadcast_to([P, SEQ])
                            ins = v.tensor_tensor_scan(s[:, q], decay, s[:, q], 0.0, ALU.mult, ALU.add)
                            if s is re or q < PQ - 1:
                                c.add(ins)
                    ins.then_inc(scanned.sem, 1)

                def skip(m):
                    dve.wait_ge(y_in_psum.sem, y_in_psum.at(l, m + 1))
                    v.scalar_tensor_tensor(uT[:, m], uT[:, m], field["s5_d"][:, m:m + 1], psum[:, 4 + m % 2, 0:SEQ],
                                           ALU.mult, ALU.add).then_inc(y_ready.sem, 1)

                states(0)
                cos, sin = (const[f].rearrange("p (b n) -> p b n", b=TB) for f in ("cos", "sin"))
                kr = lat[:, :, QR + KR:LAT]
                hq = [squares[:, :, :, 16 * i:16 * i + 16] for i in range(4)]
                flat = qkT_flat[:, 2048:2048 + 16 * 32]
                kg = flat[:, 0:TB * ROPE].rearrange("p (b n) -> p b n", b=TB)
                kt = flat[:, 64:64 + TB * ROPE].rearrange("p (b n) -> p b n", b=TB)
                krt = flat[:, 128:128 + TB * ROPE].rearrange("p (b n) -> p b n", b=TB)
                c.add(tt(kg, kr, row("g_kh", QK, [P, TB, QK])[:, :, NOPE:], ALU.mult))
                c.link(tt(kt, kr, kr, ALU.mult))
                c.link(v.tensor_reduce(kr_ssq, kt, AX_X, ALU.add))

                def rope(o, a, cos, sin, tmp):
                    a1, a2 = a[..., 0:HALF], a[..., HALF:]
                    c.add(tt(tmp[0], a1, cos, ALU.mult))
                    c.add(tt(tmp[1], a2, sin, ALU.mult))
                    c.add(tt(tmp[2], a2, cos, ALU.mult))
                    c.link(tt(tmp[3], a1, sin, ALU.mult))
                    c.add(tt(o[..., 0:HALF], tmp[0], tmp[1], ALU.subtract))
                    return tt(o[..., HALF:], tmp[2], tmp[3], ALU.add)

                t4 = [flat[:, 192 + 32 * i:224 + 32 * i].rearrange("p (b n) -> p b n", b=TB) for i in range(4)]
                c.link(rope(krt, kg, cos, sin, t4))
                dve.wait_ge(qkv_copied.sem, qkv_copied.at(l, 8))
                flat_h = squares.rearrange("p b h n -> p (b h) n")
                qf, kf = (w.rearrange("p b h n -> p (b h) n") for w in (q_tok, k_tok))
                c.link(tt(flat_h, qf, qf, ALU.mult))
                c.link(v.tensor_reduce(hd_ssq[:, 0:16], flat_h, AX_X, ALU.add))
                c.link(tt(flat_h[:, :, 0:NOPE], kf[:, :, 0:NOPE], kf[:, :, 0:NOPE], ALU.mult))
                c.link(v.tensor_reduce(hd_ssq[:, 16:32], flat_h[:, :, 0:NOPE], AX_X, ALU.add))
                k_ssq = hd_ssq[:, 16:32].rearrange("p (b h) -> p b h", b=TB)
                tt(k_ssq, k_ssq, kr_ssq.unsqueeze(2).broadcast_to([P, TB, H]), ALU.add).then_inc(head_ssq.sem, 1)
                dve.wait_ge(head_std.sem, head_std.at(l, 1))
                c.link(v.reciprocal(hd_rstd, hd_std))
                rq = hd_rstd[:, 0:16].unsqueeze(2)
                rk = hd_rstd[:, 16:32].unsqueeze(2)
                c.add(tt(qf, qf, rq.broadcast_to([P, TB * H, QK]), ALU.mult))
                c.add(tt(kf[:, :, 0:NOPE], kf[:, :, 0:NOPE], rk.broadcast_to([P, TB * H, NOPE]), ALU.mult))
                rkb = hd_rstd[:, 16:32].rearrange("p (b h) -> p b h", b=TB).unsqueeze(3)
                c.link(tt(k_tok[:, :, :, NOPE:], krt.unsqueeze(2).broadcast_to([P, TB, H, ROPE]),
                          rkb.broadcast_to([P, TB, H, ROPE]), ALU.mult))
                c.add(tt(kf[:, :, 0:NOPE], kf[:, :, 0:NOPE], row("g_kh", NOPE, [P, TB * H, NOPE]), ALU.mult))
                c.link(tt(qf, qf, row("g_qh", QK, [P, TB * H, QK]), ALU.mult))
                cos_h, sin_h = (w.unsqueeze(2).broadcast_to([P, TB, H, HALF]) for w in (cos, sin))
                t4 = [qkT_flat[:, 256 * i:256 * i + 256].rearrange("p (b h n) -> p b h n", b=TB, h=H)
                      for i in range(4)]
                rope(q_tok[:, :, :, NOPE:], q_tok[:, :, :, NOPE:], cos_h, sin_h, t4).then_inc(qk_ready.sem, 1)
                states(1)
                states(2)
                skip(0)
                states(3)
                skip(1)
                skip(2)
                skip(3)
                dve.wait_ge(qkT_in_psum.sem, qkT_in_psum.at(l, H))
                for h in range(H):
                    dve.wait_ge(scores_in_psum.sem, scores_in_psum.at(l, h + 1))
                    tt(probs[:, h], psum[:, h, 0:3 * P], mask, ALU.add).then_inc(scores_masked.sem, 1)
                    dve.wait_ge(scores_masked.sem, scores_masked.at(l, h + 1))
                    c.add(v.tensor_reduce(row_max[:, 2 * h:2 * h + 1], probs[:, h, 0:P], AX_X, ALU.max))
                    c.link(v.tensor_reduce(row_max[:, 2 * h + 1:2 * h + 2], probs[:, h, P:3 * P], AX_X, ALU.max))
                    v.tensor_scalar(neg_max[:, 2 * h:2 * h + 2], row_max[:, 2 * h:2 * h + 2], -SCALE, None,
                                    ALU.mult).then_inc(max_ready.sem, 1)
                for h in range(H):
                    dve.wait_ge(exp_ready.sem, exp_ready.at(l, h + 1))
                    c.link(v.reciprocal(row_inv[:, 2 * h:2 * h + 2], row_sum[:, 2 * h:2 * h + 2]))
                    c.add(v.tensor_scalar(probs[:, h, 0:P], probs[:, h, 0:P], row_inv[:, 2 * h:2 * h + 1], None,
                                          ALU.mult))
                    v.tensor_scalar(probs[:, h, P:3 * P], probs[:, h, P:3 * P], row_inv[:, 2 * h + 1:2 * h + 2], None,
                                    ALU.mult).then_inc(probs_ready.sem, 1)
                for j in range(H // 2):
                    dve.wait_ge(av_in_psum.sem, av_in_psum.at(l, j + 1))
                    v.tensor_copy(attnT[:, j], psum[:, 2 * j, 0:SEQ]).then_inc(attn_ready.sem, 1)
                for m in range(S5M):
                    dve.wait_ge(glu_sig.sem, glu_sig.at(l, m + 1))
                    tt(ssmT[:, m], uT[:, m], glu_sigma[:, m], ALU.mult).then_inc(ssm_ready.sem, 1)
                for m in range(KD):
                    dve.wait_ge(proj_in_psum.sem, proj_in_psum.at(l, m + 1))
                    both = gates_w[:, :, m]
                    c.link(tt(both, both, psum[:, m].rearrange("p (w t) -> p w t", w=2), ALU.mult))
                    tt(gates[:, m], gates[:, m], gates[:, KD + m], ALU.add).then_inc(mix_ready.sem, 1)
                for n in range(4):
                    dve.wait_ge(mixed_in_psum.sem, mixed_in_psum.at(l, n + 1))
                    xs = x[:, n % 2, 512 * (n // 2):512 * (n // 2) + 512]
                    ins = tt(xs, xs, psum[:, n], ALU.add)
                    if n < 3:
                        c.add(ins)
                ins.then_inc(x_ready.sem, 1)
                norm(l, 1)
                normed(l, 1)
                assert c.n == DVE_MIX, c.n
                with dve.If(l < 1):
                    c.start(DVE_MIX)
                    for f in range(FF // P):
                        dve.wait_ge(ff_sig.sem, f + 1)
                        ins = tt(ff_sigma[:, f % 2], ff_sigma[:, f % 2], psum[:, 4 + f % 4, 0:SEQ], ALU.mult)
                        c.link(ins)
                        tt(ff_actT[:, f // 4 % 2, f % 4], ff_sigma[:, f % 2], psum[:, 4 + f % 4, SEQ:2 * SEQ],
                           ALU.mult).then_inc(ff_act.sem, 1)
                    dve.wait_ge(ff_down.sem, FFC)
                    for n in range(4):
                        xs = x[:, n // 2, 512 * (n % 2):512 * (n % 2) + 512]
                        ins = tt(xs, xs, psum[:, n], ALU.add)
                        if n < 3:
                            c.add(ins)
                    ins.then_inc(x_ready.sem, 1)
                    assert c.n == DVE_FFN, c.n

            c.start(DEPTH * DVE_MIX + DVE_FFN)
            dve.wait_ge(logits_in_psum.sem, 1)
            c.link(tt(logits, psum[:, 4, 0:TB * E].rearrange("p (b e) -> p b e", b=TB),
                      const["r_b"].unsqueeze(1).broadcast_to([P, TB, E]), ALU.add))
            for b in range(TB):
                c.add(v.max(top[:, b], logits[:, b]))
            c.sync()
            for b in range(TB):
                c.add(v.max_index(top_i[:, b], top[:, b], logits[:, b]))
            tt(diff[:, :, 0:1], top[:, :, 1:2], top[:, :, 0:1], ALU.subtract).then_inc(top_ready.sem, 1)
            c.sync()
            c.link(v.tensor_copy(top_f, top_i))
            dve.wait_ge(top_exp.sem, 1)
            c.link(v.tensor_scalar(den2[:, :, 0:1], ediff[:, :, 0:1], 1.0, None, ALU.add))
            c.link(v.reciprocal(w_first[:, :, 0:1], den2[:, :, 0:1]))
            c.link(tt(w_second[:, :, 0:1], ediff[:, :, 0:1], w_first[:, :, 0:1], ALU.mult))
            iota = const["iota"]
            for b in range(TB):
                i0, i1 = top_f[:, b, 0:1], top_f[:, b, 1:2]
                c.add(v.tensor_scalar(hot0[:, b], iota[:, 0:E], i0, None, ALU.is_equal))
                c.link(v.tensor_scalar(hot1[:, b], iota[:, 0:E], i1, None, ALU.is_equal))
                c.link(tt(sel[:, b], hot0[:, b], hot1[:, b], ALU.add))
                c.add(v.tensor_scalar(hot0[:, b], hot0[:, b], w_first[:, b, 0:1], None, ALU.mult))
                c.link(v.tensor_scalar(hot1[:, b], hot1[:, b], w_second[:, b, 0:1], None, ALU.mult))
                ins = tt(comb[:, b], hot0[:, b], hot1[:, b], ALU.add)
                if b == 0:
                    c.add(ins)
            ins.then_inc(chosen.sem, 1)
            c.add(v.tensor_copy(x_out, x))
            dve.wait_ge(places_in_psum.sem, 1)
            dve.wait_ge(chosen.sem, 1)
            c.add(v.tensor_reduce(diff[:, 0, 1:2], psum[:, 5, 2 * E:3 * E], AX_X, ALU.max))
            c.link(v.scalar_tensor_tensor(place[:, 0], psum[:, 5, 0:2 * E].rearrange("p (b e) -> p b e", b=TB), 1.0,
                                          sel, ALU.add, ALU.mult))
            v.tensor_copy(most_i[:, 0:1], diff[:, 0, 1:2]).then_inc(count_ready.sem, 1)
            c.add(v.tensor_scalar(place[:, 1], place[:, 0], 1.0 + P, None, ALU.subtract))
            c.link(v.tensor_scalar(place[:, 0], place[:, 0], 1.0, None, ALU.subtract))
            assert c.n == DVE_ROUTE, c.n

            def experts(pair, turn, r):
                c.start(turn * DVE_PAIR + (DEPTH * DVE_MIX + DVE_FFN + DVE_ROUTE))
                for half in range(2):
                    def at(per, n):
                        return turn * (2 * per) + (half * per + n)

                    e = bass.ds(pair * 2 + half, 1)
                    for b in range(TB):
                        c.add(v.tensor_scalar(pick[:, b], iota, place[:, r, b, e], rstd[:, b:b + 1],
                                              ALU.is_equal, ALU.mult))
                        ins = v.tensor_scalar(spread_tok[:, b], iota, place[:, r, b, e], comb[:, b, e],
                                              ALU.is_equal, ALU.mult)
                        if b == 0:
                            c.add(ins)
                    ins.then_inc(pick_ready.sem, 1)
                    dve.wait_ge(spreadT_in_psum.sem, at(1, 1))
                    v.tensor_copy(spread.rearrange("p b t -> p (b t)"), psum[:, 1, 0:TB * P]).then_inc(
                        spread_ready.sem, 1)
                    for j in range(2):
                        dve.wait_ge(rows_in_psum.sem, at(2, j + 1))
                        gain = field["g_ffn"][:, 4 * j:4 * j + 4].unsqueeze(2).broadcast_to([P, 4, P])
                        tt(rowsT[:, 4 * j:4 * j + 4], psum[:, 6 + j].rearrange("p (k j) -> p k j", k=4), gain,
                           ALU.mult).then_inc(rows_ready.sem, 1)
                    for ch in range(FEC):
                        dve.wait_ge(ex_sig.sem, at(FEC, ch + 1))
                        if ch >= 2:
                            dve.wait_ge(actT_in_psum.sem, at(FEC, ch - 1))
                        c.link(tt(ex_sigma[:, ch % 2], ex_sigma[:, ch % 2], psum[:, ch % 2], ALU.mult))
                        dve.wait_ge(ex_up.sem, at(FEC, ch + 1))
                        tt(ex_a[:, ch % 2], ex_sigma[:, ch % 2], psum[:, 2 + ch % 2], ALU.mult).then_inc(
                            ex_act.sem, 1)
                    for n in range(4):
                        b, j = n // 2, n % 2
                        dve.wait_ge(spread_in_psum.sem, at(4, n + 1))
                        xs = x_out[:, b, 512 * j:512 * j + 512]
                        tt(xs, xs, psum[:, 6 + n % 2], ALU.add).then_inc(spread_added.sem, 1)
                assert c.n == DVE_PAIR, c.n

            with dve.Fori(0, E // 2) as pair:
                experts(pair, pair, 0)
            dve.wait_ge(count_ready.sem, 1)
            most = dve.value_load(most_i[0:1, 0:1], min_val=0, max_val=SEQ)
            with dve.If(most > P):
                with dve.Fori(0, E // 2) as pair:
                    experts(pair, pair + E // 2, 1)
            dve.drain().then_inc(out_ready.sem, 1)


def _packed(i):
    def channels(a):
        return a.reshape(DEPTH, -1, P).transpose(0, 2, 1)

    def pairs(a):
        return a.reshape(DEPTH, PAIRS, 2 * STATES).transpose(0, 2, 1)

    def two_groups(a):
        a = a.reshape(DEPTH, PAIRS, 2, STATES, CH)
        wide = np.zeros((DEPTH, PAIRS, 2, STATES, 2, CH), a.dtype)
        for g in range(2):
            wide[:, :, g, :, g] = a[:, :, g]
        return wide.reshape(DEPTH, PAIRS, P, 32).transpose(0, 2, 1, 3).reshape(DEPTH, P, PAIRS * 32)

    def spread(a):
        return np.broadcast_to(a[:, None, :], (DEPTH, P, a.shape[1]))

    b_in = i["b_in"]
    step = np.broadcast_to(i["s5_log_step"][:, :, None], (DEPTH, GROUPS, STATES))
    values = {
        "g_mix": channels(i["ln_mix_g"]), "g_ffn": channels(i["ln_ffn_g"]), "b_u": channels(b_in[:, LAT:LAT + S5W]),
        "b_gate": channels(b_in[:, LAT + S5W:]), "s5_d": channels(i["s5_d"]), "b_glu": channels(i["b_glu"]),
        "g_q": channels(i["q_norm_g"]), "g_kv": channels(i["kv_norm_g"]), "lam_re": pairs(i["s5_lam_re"]),
        "lam_im": pairs(i["s5_lam_im"]), "log_step": pairs(step), "b_re": two_groups(i["s5_b_re"]),
        "b_im": two_groups(i["s5_b_im"]), "c_re": two_groups(i["s5_c_re"].transpose(0, 1, 3, 2)),
        "c_im": two_groups(i["s5_c_im"].transpose(0, 1, 3, 2)), "b_lat": spread(b_in[:, :LAT]),
        "g_qh": spread(i["q_head_g"]), "g_kh": spread(i["k_head_g"]),
    }
    return np.ascontiguousarray(np.concatenate([values[n] for n, _ in FIELDS], 2))


def _constants(router_b):
    rows = np.arange(P)
    causal = np.where(rows[None, :] <= rows[:, None], 0.0, NEG)
    inv = np.power(np.float32(10000.0), -np.arange(0, ROPE, 2, dtype=np.float32) / np.float32(ROPE))
    angle = (np.arange(SEQ, dtype=np.float32)[:, None] * inv[None, :]).reshape(TB, P, HALF).transpose(1, 0, 2)
    values = {"ident": np.eye(P), "mask": np.concatenate([causal, np.zeros((P, P)), causal], 1),
              "cos": np.cos(angle).reshape(P, -1), "sin": np.sin(angle).reshape(P, -1),
              "before": rows[:, None] < rows[None, :], "ones": np.ones((P, P)),
              "iota": np.broadcast_to(rows[None, :], (P, P)), "r_b": np.broadcast_to(router_b, (P, E))}
    return np.concatenate([values[n].astype(np.float32) for n, _ in CONSTS], 1)


def kernel(**inputs):
    import concourse.bacc as bacc
    from concourse.bass_utils import run_bass_kernel_spmd

    nc = bacc.Bacc("TRN2", target_bir_lowering=False, num_devices=1)
    i = {n: np.asarray(a) for n, a in inputs.items()}
    given = {"x": i["x"].reshape(SEQ, D), "params": _packed(i), "consts": _constants(i["router_b"])}
    for n in ("w_in", "w_uq", "w_ukv", "w_glu", "w_proj_attn", "w_proj_ssm", "w_out", "ffn_w_gate", "ffn_w_up",
              "ffn_w_down", "router_w"):
        given[n] = i[n]
    for n in ("moe_w_gate", "moe_w_up", "moe_w_down"):
        given[n] = i[n][0]
    arrays = {f"{n}_dram": np.ascontiguousarray(a) for n, a in given.items()}
    args = [nc.dram_tensor(n, a.shape, mybir.dt.from_np(a.dtype), kind="ExternalInput").ap()
            for n, a in arrays.items()]
    out = nc.dram_tensor("out_dram", (SEQ, D), F32, kind="ExternalOutput").ap()
    hybrid_trunk(nc, *args, out)
    r = run_bass_kernel_spmd(nc, [arrays], core_ids=[0])
    return r.results[0]["out_dram"].reshape(1, SEQ, D)
```

```python
from contextlib import ExitStack

import numpy as np

import concourse.bass as bass
from concourse import mybir

F32 = mybir.dt.float32
F32R = mybir.dt.float32r
I32 = mybir.dt.int32
U32 = mybir.dt.uint32
ALU = mybir.AluOpType
ACT = mybir.ActivationFunctionType
AX_X = mybir.AxisListType.X

P = 128
D = 1024
KD = D // P
SEQ = 256
TB = SEQ // P
DEPTH = 2
H = 8
NOPE = 64
ROPE = 32
HALF = ROPE // 2
QK = NOPE + ROPE
VD = 64
QR = 256
KR = 128
LAT = QR + KR + ROPE
S5W = 512
S5M = S5W // P
GROUPS = 32
STATES = 64
CH = 16
PAIRS = GROUPS // 2
PQ = PAIRS // S5M
FF = 2816
FFC = 6
E = 8
FE = 3584
FEC = FE // 512
EPS = 1e-6
NEG = -1e30
SCALE = QK ** -0.5
PI2_A = 6.28125
PI2_B = float(np.float32(2 * np.pi - 6.28125).astype(np.float16))
PI2_C = float(2 * np.pi - PI2_A - PI2_B)
MAGIC = 1.5 * 2 ** 23

FIELDS = [("g_mix", KD), ("g_ffn", KD), ("b_u", S5M), ("b_gate", 2 * KD), ("s5_d", S5M), ("b_glu", S5M),
          ("g_q", QR // P), ("g_kv", KR // P), ("lam_re", PAIRS), ("lam_im", PAIRS), ("log_step", PAIRS),
          ("b_re", PAIRS * 32), ("b_im", PAIRS * 32), ("c_re", PAIRS * 32), ("c_im", PAIRS * 32),
          ("b_lat", LAT), ("g_qh", QK), ("g_kh", QK)]
NPL = sum(n for _, n in FIELDS)
CONSTS = [("ident", P), ("mask", 3 * P), ("cos", TB * HALF), ("sin", TB * HALF), ("before", P), ("ones", P),
          ("iota", P), ("r_b", E)]
NC_ = sum(n for _, n in CONSTS)

RING = 6
SLOT = 4096
MIX_SLOTS = 4
MIX_ITEMS = ["lat", "u", "gate0", "up", "gate1", "gate2", "gate3", "glu", "proj_a", "proj_s", "out0", "out1"]
N_MIX = len(MIX_ITEMS)
FFN_ITEMS = [(_w, _c) for _c in range(FFC) for _w in "gud"]
N_FFN = len(FFN_ITEMS)
MOE_ITEMS = [("g", 0), ("u", 0)]
for _c in range(1, FEC):
    MOE_ITEMS += [("g", _c), ("u", _c), ("d", _c - 1)]
MOE_ITEMS += [("d", FEC - 1)]
N_EXP = len(MOE_ITEMS)
N_PAIR = 2 * N_EXP
UNIT = 1024
UNITS = SLOT // UNIT
UNIT_BUFS = 7
FF_TILES = FF // P
FF_UNITS = []
for _n in range(FF_TILES + 2):
    FF_UNITS += [(_w, _n) for _w in "gu" if _n < FF_TILES] + [("d", _n - 2)] * (_n >= 2)
N_FF_UNITS = len(FF_UNITS)


class Signal:

    def __init__(self, ctx, nc, name, per_layer=0):
        self.sem, self.per = ctx.enter_context(nc.semaphore(name)), per_layer

    def at(self, layer, n):
        return layer * self.per + n


class Chain:

    def __init__(self, eng, sem):
        self.eng, self.sem, self.base, self.n = eng, sem, 0, 0

    def start(self, base):
        self.base, self.n = base, 0

    def add(self, ins):
        ins.then_inc(self.sem, 1)
        self.n += 1

    def sync(self):
        self.eng.wait_ge(self.sem, self.base + self.n)

    def link(self, ins):
        self.add(ins)
        self.sync()


DVE_MIX, DVE_FFN, DVE_ROUTE, DVE_PAIR = CHAIN_DVE = (152, 25, 30, 14)
ACT_MIX, ACT_FFN = CHAIN_ACT = (8, 0)
POOL_MIX = 127


def hybrid_trunk(nc, x_in, params, consts, w_in, w_uq, w_ukv, w_glu, w_pa, w_ps, w_out,
                 f_gate, f_up, f_down, router, m_gate, m_up, m_down, out):
    with ExitStack() as ctx:
        def sb(name, cols, dt=F32, parts=P):
            return ctx.enter_context(nc.sbuf_tensor(name, [parts, cols], dt))

        def sig(name, per=0):
            return Signal(ctx, nc, name, per)

        ring = sb("ring", RING * SLOT)
        x = sb("x", TB * D)[:, :].rearrange("p (b d) -> p b d", b=TB)
        cst = sb("cst", NC_)
        stat = sb("stat", 240)
        router_sb = sb("router_sb", KD * E)[:, :].rearrange("p (k e) -> p k e", k=KD)
        most_i = sb("most_i", 8, I32)
        area_at = (nc.sbuf_base + 31) // 32 * 32
        area_cols = (nc.sbuf_usable_end - area_at) // 4 // 8 * 8 - 8
        sb("area", area_cols)
        taken = [0]

        def sb(name, cols, dt=F32):
            at, taken[0] = taken[0], taken[0] + (cols + 7) // 8 * 8
            assert taken[0] <= area_cols, (name, taken[0], area_cols)
            return nc.alloc_sbuf_tensor_at(name, [P, cols], dt, offset=area_at + 4 * at)

        pl = sb("pl", NPL)
        at_split = taken[0]
        w_hi = sb("w_hi", UNIT_BUFS * UNIT, F32R)[:, :].rearrange("p (i n) -> p i n", i=UNIT_BUFS)
        w_lo = sb("w_lo", UNIT_BUFS * UNIT, F32R)[:, :].rearrange("p (i n) -> p i n", i=UNIT_BUFS)
        at_hT = taken[0]
        taken[0] = at_split
        work = sb("work", 11 * 1024)
        uT = sb("uT", S5M * SEQ)[:, :].rearrange("p (m t) -> p m t", m=S5M)
        bT = sb("bT", S5M * 2 * P)[:, :].rearrange("p (m r s) -> p m r s", m=S5M, r=2)
        attnT = sb("attnT", 4 * SEQ)[:, :].rearrange("p (k t) -> p k t", k=4)
        assert taken[0] <= at_hT
        taken[0] = at_hT
        hT = sb("hT", KD * SEQ)[:, :].rearrange("p (k t) -> p k t", k=KD)
        at_gates = taken[0]
        gates_t = sb("gates", 2 * KD * SEQ)
        gates = gates_t[:, :].rearrange("p (m t) -> p m t", m=2 * KD)
        early = sb("early", LAT * TB + 3 * SEQ)
        small = sb("small", 24 * PAIRS)
        taken[0] = at_hT
        hT_hi = sb("hT_hi", KD * SEQ, F32R)[:, :].rearrange("p (k t) -> p k t", k=KD)
        hT_lo = sb("hT_lo", KD * SEQ, F32R)[:, :].rearrange("p (k t) -> p k t", k=KD)
        ff_sigma = sb("ff_sigma", 2 * SEQ)[:, :].rearrange("p (i t) -> p i t", i=2)
        ff_a = sb("ff_a", 2 * SEQ)[:, :].rearrange("p (i t) -> p i t", i=2)
        ff_hi = sb("ff_hi", 4 * SEQ, F32R)[:, :].rearrange("p (i t) -> p i t", i=4)
        ff_lo = sb("ff_lo", 4 * SEQ, F32R)[:, :].rearrange("p (i t) -> p i t", i=4)
        taken[0] = 0
        x_out = sb("x_out", TB * D)[:, :].rearrange("p (b d) -> p b d", b=TB)
        rt = sb("rt", 320)
        spread = sb("spread", TB * P)[:, :].rearrange("p (b t) -> p b t", b=TB)
        assert taken[0] <= at_split
        taken[0] = at_hT
        y_rows = sb("y_rows", D)
        pick = sb("pick", TB * P)[:, :].rearrange("p (b j) -> p b j", b=TB)
        spread_tok = sb("spread_tok", TB * P)[:, :].rearrange("p (b j) -> p b j", b=TB)
        rows_f = sb("rows_f", D)[:, :].rearrange("p (k j) -> p k j", k=KD)
        rows_hi = sb("rows_hi", D, F32R)[:, :].rearrange("p (k j) -> p k j", k=KD)
        rows_lo = sb("rows_lo", D, F32R)[:, :].rearrange("p (k j) -> p k j", k=KD)
        ex_sigma = sb("ex_sigma", 512)[:, :]
        ex_a = sb("ex_a", 2 * 512)[:, :].rearrange("p (i f) -> p i f", i=2)
        aT_hi = sb("aT_hi", 2 * 512, F32R)[:, :].rearrange("p (i n) -> p i n", i=2)
        aT_lo = sb("aT_lo", 2 * 512, F32R)[:, :].rearrange("p (i n) -> p i n", i=2)
        psum = ctx.enter_context(nc.psum_tensor("psum", [P, 8, 512], F32))

        field, at = {}, 0
        for name, n in FIELDS:
            field[name] = pl[:, at:at + n]
            at += n
        const, at = {}, 0
        for name, n in CONSTS:
            const[name] = cst[:, at:at + n]
            at += n
        ident, mask = const["ident"], const["mask"]

        slots = [ring[:, s * SLOT:(s + 1) * SLOT] for s in range(RING)]
        lat = early[:, 0:TB * LAT].rearrange("p (b n) -> p b n", b=TB)
        qlT = early[:, TB * LAT:TB * LAT + 2 * SEQ].rearrange("p (k t) -> p k t", k=2)
        kvT = early[:, TB * LAT + 2 * SEQ:TB * LAT + 3 * SEQ]
        tail = ring[:, MIX_SLOTS * SLOT:RING * SLOT]
        qk_tok = tail[:, 0:2 * TB * H * QK].rearrange("p (w b h n) -> p w b h n", w=2, b=TB, h=H)
        q_tok, k_tok = qk_tok[:, 0], qk_tok[:, 1]
        at = 2 * TB * H * QK
        v_tok = tail[:, at:at + TB * H * VD].rearrange("p (b h n) -> p b h n", b=TB, h=H)
        at += TB * H * VD
        qkT_flat = tail[:, at:at + 2 * H * SEQ]
        qkT = qkT_flat.rearrange("p (h w t) -> p h w t", h=H, w=2)
        squares = qkT_flat[:, 0:TB * H * QK].rearrange("p (b h n) -> p b h n", b=TB, h=H)
        probs = tail[:, 0:H * 3 * P].rearrange("p (h n) -> p h n", h=H)
        probsT = qkT_flat[:, 0:H * 3 * P].rearrange("p (h n) -> p h n", h=H)
        assert at + 2 * H * SEQ == 2 * SLOT

        N4 = PQ * SEQ

        def wk(i, n=1):
            return work[:, i * N4:(i + n) * N4]

        def quads(a):
            return a.rearrange("p (q t) -> p q t", q=PQ)

        tab_c = [quads(wk(0)), quads(wk(1))]
        tab_s = [quads(wk(2)), quads(wk(3))]
        st_re = [wk(4), wk(5)]
        st_im = [wk(6), wk(7)]
        out_re = quads(wk(8))
        dve_tmp = wk(9)
        pool_tmp = quads(wk(10))

        def sm(i, n=1):
            return small[:, i * PAIRS:(i + n) * PAIRS]

        small_names = ["step", "theta", "turns", "absr", "sin", "cos", "decay", "er", "n_re", "n_im", "den", "f_re",
                       "f_im", "t1", "t2", "w_c", "w_s", "w_c2", "w_s2", "w_t"]
        S = {n: sm(i) for i, n in enumerate(small_names)}

        def st(at, n):
            return stat[:, at:at + n]

        ssq, std, rstd = st(0, TB), st(2, TB), st(4, TB)
        lat_ssq, lat_std_v, lat_rstd = st(6, 4), st(10, 4), st(14, 4)
        kr_ssq, hd_ssq, hd_std, hd_rstd = st(18, TB), st(20, 32), st(52, 32), st(84, 32)
        eps, half_pi, zero = st(116, 1), st(117, 1), st(118, 1)
        row_max, neg_max, row_sum, row_inv = st(120, 16), st(136, 16), st(152, 16), st(168, 16)
        diag = early[:, 0:TB * P].rearrange("p (b t) -> p b t", b=TB)
        powers = attnT.rearrange("p k (q t) -> p k q t", q=PAIRS)
        glu_sigma = wk(9).rearrange("p (m t) -> p m t", m=S5M)
        ssmT = wk(8).rearrange("p (m t) -> p m t", m=S5M)
        gates_w = gates.rearrange("p (w m) t -> p w m t", w=2)
        def rv(i, dt=F32):
            v = rt[:, 16 * i:16 * i + 16]
            return (v.bitcast(dt) if dt is not F32 else v).rearrange("p (b e) -> p b e", b=TB)

        logits, top, top_i, top_f, sel, comb = rv(0), rv(1), rv(2, U32), rv(3), rv(4), rv(5)
        hot0, hot1, diff, ediff, den2, w_first, w_second = rv(6), rv(7), rv(8), rv(9), rv(10), rv(11), rv(12)
        N_ALL = 2 * E + 1
        place = rt[:, 208:208 + TB * N_ALL].rearrange("p (b e) -> p b e", b=TB)
        weight = rt[:, 256:256 + TB * N_ALL].rearrange("p (b e) -> p b e", b=TB)
        g_rows = st(200, KD)
        uq_loaded, consts_set = sig("uq_loaded", 16), sig("consts_set")
        slot_full = [sig(f"slot_full{s}") for s in range(RING)]
        x_loaded, consts_loaded, params_loaded = sig("x_loaded"), sig("consts_loaded"), sig("params_loaded", 16)
        router_loaded = sig("router_loaded")
        dve_chain, act_chain, pool_chain = sig("dve_chain"), sig("act_chain"), sig("pool_chain")
        x_ready, std_ready, diag_ready = sig("x_ready", 2), sig("std_ready", 2), sig("diag_ready", 2)
        hT_in_psum, hT_act, hT_dve = sig("hT_in_psum", 8), sig("hT_act", 12), sig("hT_dve", 12)
        step_exp, theta_ready, trig_ready = sig("step_exp", 1), sig("theta_ready", 1), sig("trig_ready", 1)
        bbar_ready, bbarT_in_psum, bbarT_ready = sig("bbar_ready", 1), sig("bbarT_in_psum", 1), sig("bbarT_ready", 1)
        table_ready, table_free = sig("table_ready", S5M), sig("table_free", S5M)
        lat_in_psum, lat_biased, lat_std, lat_ready = (sig("lat_in_psum", TB), sig("lat_biased", 1),
                                                       sig("lat_std", 1), sig("lat_ready", 1))
        u_in_psum, u_ready = sig("u_in_psum", S5M), sig("u_ready", S5M)
        gate_in_psum, gate_ready = sig("gate_in_psum", 2 * KD), sig("gate_ready", 2 * KD)
        bu_in_psum, bu_read = sig("bu_in_psum", S5M), sig("bu_read", S5M)
        scanned, states_ready = sig("scanned", S5M), sig("states_ready", S5M)
        y_in_psum, y_ready, gelu_ready = sig("y_in_psum", S5M), sig("y_ready", S5M), sig("gelu_ready", S5M)
        glu_in_psum, glu_sig, ssm_ready = sig("glu_in_psum", S5M), sig("glu_sig", S5M), sig("ssm_ready", S5M)
        latT_in_psum, latT_ready = sig("latT_in_psum", 2), sig("latT_ready", 3)
        qkv_in_psum, qkv_copied = sig("qkv_in_psum", 8), sig("qkv_copied", 8)
        head_ssq, head_std, qk_ready = sig("head_ssq", 1), sig("head_std", 1), sig("qk_ready", 1)
        qkT_in_psum, qkT_copied = sig("qkT_in_psum", H), sig("qkT_copied", H)
        scores_in_psum, scores_masked, max_ready = (sig("scores_in_psum", H), sig("scores_masked", H),
                                                    sig("max_ready", H))
        exp_ready, probs_ready = sig("exp_ready", H), sig("probs_ready", H)
        probsT_in_psum, probsT_copied = sig("probsT_in_psum", H), sig("probsT_copied", H)
        av_in_psum, attn_ready = sig("av_in_psum", H // 2), sig("attn_ready", H // 2)
        proj_in_psum, mix_ready, mixed_in_psum = sig("proj_in_psum", KD), sig("mix_ready", KD), sig("mixed_in_psum", 4)
        ff_sig, ff_act, ff_hi_ready, ff_lo_ready = sig("ff_sig"), sig("ff_act"), sig("ff_hi_ready"), sig("ff_lo_ready")
        attn_projected = sig("attn_projected", 1)
        logits_in_psum, top_ready, top_exp, chosen = sig("logits_in_psum"), sig("top_ready"), sig("top_exp"), sig("chosen")
        places_in_psum, places_ready, count_ready = sig("places_in_psum"), sig("places_ready"), sig("count_ready")
        pick_ready, rows_in_psum = sig("pick_ready"), sig("rows_in_psum")
        spreadT_in_psum, spread_ready = sig("spreadT_in_psum"), sig("spread_ready")
        hi_ready, lo_ready, unit_used = sig("hi_ready"), sig("lo_ready"), sig("unit_used")
        rows_f_ready, rows_hi_ready, rows_lo_ready = sig("rows_f_ready"), sig("rows_hi_ready"), sig("rows_lo_ready")
        aT_hi_ready, aT_lo_ready = sig("aT_hi_ready"), sig("aT_lo_ready")
        ex_sig, ex_act = sig("ex_sig"), sig("ex_act")
        actT_in_psum = sig("actT_in_psum")
        y_rows_ready, y_rows_ready_dve = sig("y_rows_ready"), sig("y_rows_ready_dve")
        spread_in_psum, spread_added = sig("spread_in_psum"), sig("spread_added")
        out_ready, stored = sig("out_ready"), sig("stored")

        mix_use = {i: (i % MIX_SLOTS, i // MIX_SLOTS + 1) for i in range(N_MIX)}
        ffn_use = {i: (i % RING, i // RING + 1) for i in range(N_FFN)}
        per_slot_layer = [N_MIX // MIX_SLOTS * (s < MIX_SLOTS) + N_FFN // RING for s in range(RING)]
        before_moe = [per_slot_layer[s] + N_MIX // MIX_SLOTS * (s < MIX_SLOTS) for s in range(RING)]
        per_slot_pair = N_PAIR // RING

        def mix_landed(eng, l, i):
            s, k = mix_use[i]
            eng.wait_ge(slot_full[s].sem, l * (16 * per_slot_layer[s]) + 16 * k)

        def ffn_landed(eng, i):
            s, k = ffn_use[i]
            eng.wait_ge(slot_full[s].sem, 16 * (N_MIX // MIX_SLOTS * (s < MIX_SLOTS) + k))

        def moe_landed(eng, turn, i):
            s, k = i % RING, i // RING + 1
            eng.wait_ge(slot_full[s].sem, turn * (16 * per_slot_pair) + 16 * (before_moe[s] + k))

        assert (N_PAIR * UNITS) % UNIT_BUFS == 0

        def buf(n):
            return (N_FF_UNITS + n) % UNIT_BUFS

        def ff_unit(what, tile):
            c, f = tile // 4, tile % 4
            slot = slots[FFN_ITEMS.index((what, c)) % RING]
            width = min(4, FF_TILES - 4 * c) * P
            if what == "d":
                src = slot[:, f * D:(f + 1) * D]
            else:
                src = slot[:, 0:KD * width].rearrange("p (k n) -> p k n", k=KD)[:, :, f * P:(f + 1) * P]
            return FF_UNITS.index((what, tile)), src

        def unit(n):
            return ring[:, (n // UNITS % RING) * SLOT + n % UNITS * UNIT:][:, 0:UNIT]

        def item_unit(half, what, ch):
            return (half * N_EXP + MOE_ITEMS.index((what, ch))) * UNITS

        def per_pair(turn, n):
            return turn * (N_PAIR * UNITS) + (N_FF_UNITS + n)

        def ahead(eng, pair, turn, half, split):
            first = (half + 1) * N_EXP * UNITS
            if half == 0:
                for part in range(UNITS):
                    split(turn, first + part)
            else:
                with eng.If(pair < E // 2 - 1):
                    for part in range(UNITS):
                        split(turn, first + part)

        def slot_view(s, k, n):
            return slots[s][:, 0:k * n].rearrange("p (k n) -> p k n", k=k)

        def rows(w, k):
            return w.rearrange("(k p) n -> p k n", p=P)

        block = ctx.enter_context(nc.Block())

        @block.sync
        def _(sp):
            def layer_of(w, l):
                return w[bass.ds(l, 1)].rearrange("a r n -> (a r) n")

            def mixer_used(l, i):
                what = MIX_ITEMS[i]
                j = int(what[-1]) if what[-1].isdigit() else 0
                signal, n = {"lat": (lat_in_psum, TB), "u": (u_in_psum, S5M), "up": (qkv_in_psum, 8),
                             "gate": (gate_in_psum, 4 * j + 4), "glu": (glu_in_psum, S5M),
                             "proj_a": (attn_projected, 1), "proj_s": (proj_in_psum, KD),
                             "out": (mixed_in_psum, TB * (j + 1))}[what.rstrip("0123456789")]
                sp.wait_ge(signal.sem, signal.at(l, n))

            def ffn_used(i):
                what, c = FFN_ITEMS[i]
                last = FF_UNITS.index((what, min(4 * c + 3, FF_TILES - 1)))
                sp.wait_ge(lo_ready.sem, last + 1)

            def expert_used(turn, i):
                sp.wait_ge(lo_ready.sem, per_pair(turn, UNITS * (i + 1)))

            def load_mixer(l, i):
                what, s = MIX_ITEMS[i], i % MIX_SLOTS
                if what in ("lat", "u") or what.startswith("gate"):
                    c0, n = {"lat": (0, LAT), "u": (LAT, S5W)}.get(what) or (LAT + S5W + 512 * int(what[-1]), 512)
                    dst, src = slot_view(s, KD, n), rows(layer_of(w_in, l)[:, c0:c0 + n], KD)
                elif what == "up":
                    sp.dma_start(slots[s][:, 0:2 * H * QK].rearrange("p (k n) -> p k n", k=2),
                                 rows(layer_of(w_uq, l), 2)).then_inc(uq_loaded.sem, 16)
                    dst, src = slots[s][:, 2048:2048 + 2 * 512], layer_of(w_ukv, l)
                elif what == "glu":
                    dst, src = slot_view(s, S5M, S5W), rows(layer_of(w_glu, l), S5M)
                elif what in ("proj_a", "proj_s"):
                    dst, src = slot_view(s, 4, D), rows(layer_of(w_pa if what == "proj_a" else w_ps, l), 4)
                else:
                    c0 = 512 * int(what[-1])
                    dst, src = slot_view(s, KD, 512), rows(layer_of(w_out, l)[:, c0:c0 + 512], KD)
                sp.dma_start(dst, src).then_inc(slot_full[s].sem, 16)

            def load_ffn(i):
                (what, c), s = FFN_ITEMS[i], i % RING
                n = min(512, FF - 512 * c)
                if what == "d":
                    dst, src = slot_view(s, n // P, D), rows(f_down[0, 512 * c:512 * c + n, :], n // P)
                else:
                    dst = slot_view(s, KD, n)
                    src = rows((f_gate if what == "g" else f_up)[0, :, 512 * c:512 * c + n], KD)
                sp.dma_start(dst, src).then_inc(slot_full[s].sem, 16)

            def load_expert(pair, i):
                half, (what, c), s = i // N_EXP, MOE_ITEMS[i % N_EXP], i % RING
                e = bass.ds(pair * 2 + half, 1)
                if what == "d":
                    dst, src = slot_view(s, 4, D), m_down[e, 512 * c:512 * c + 512, :]
                else:
                    dst, src = slot_view(s, KD, 512), (m_gate if what == "g" else m_up)[e, :, 512 * c:512 * c + 512]
                sp.dma_start(dst, src.rearrange("a (k p) n -> p (a k) n", p=P)).then_inc(slot_full[s].sem, 16)

            sp.dma_start(x, x_in.rearrange("(b p) d -> p b d", p=P)).then_inc(x_loaded.sem, 16)
            sp.dma_start(cst[:, :], consts).then_inc(consts_loaded.sem, 16)
            sp.dma_start(pl[:, :], params[0]).then_inc(params_loaded.sem, 16)
            for i in range(MIX_SLOTS):
                load_mixer(0, i)
            with sp.Fori(0, DEPTH) as l:
                for i in range(MIX_SLOTS, N_MIX):
                    mixer_used(l, i - MIX_SLOTS)
                    load_mixer(l, i)
                with sp.If(l < 1):
                    sp.wait_ge(attn_ready.sem, H // 2)
                    for i in range(N_FFN):
                        if i >= RING:
                            ffn_used(i - RING)
                        elif i < MIX_SLOTS:
                            mixer_used(0, N_MIX - MIX_SLOTS + i)
                        load_ffn(i)
                    for s in range(MIX_SLOTS):
                        ffn_used(N_FFN - RING + s)
                        load_mixer(1, s)
            sp.wait_ge(attn_ready.sem, DEPTH * (H // 2))
            for i in range(RING):
                if i < MIX_SLOTS:
                    mixer_used(1, N_MIX - MIX_SLOTS + i)
                load_expert(0, i)

            def experts(turn_0):
                def rest(pair):
                    for i in range(RING, N_PAIR):
                        expert_used(pair + turn_0, i - RING)
                        load_expert(pair, i)

                with sp.Fori(1, E // 2) as pair:
                    rest(pair - 1)
                    for i in range(RING):
                        expert_used(pair + (turn_0 - 1), N_PAIR - RING + i)
                        load_expert(pair, i)
                rest(E // 2 - 1)

            experts(0)
            sp.wait_ge(count_ready.sem, 1)
            most = sp.value_load(most_i[0:1, 0:1], min_val=0, max_val=SEQ)
            with sp.If(most > P):
                for i in range(RING):
                    expert_used(E // 2 - 1, N_PAIR - RING + i)
                    load_expert(0, i)
                experts(E // 2)
            sp.wait_ge(out_ready.sem, 1)
            sp.dma_start(out.rearrange("(b p) d -> p b d", p=P), x_out).then_inc(stored.sem, 16)
            sp.wait_ge(stored.sem, 16)

        @block.gpsimd
        def _(pool):
            g = nc.gpsimd
            c = Chain(pool, pool_chain.sem)
            low_c, low_s, high_c, high_s = (powers[:, i] for i in range(4))

            def over(v, n):
                return v.unsqueeze(2).broadcast_to([P, PAIRS, n])

            def doubled(tc, ts, n, wc, ws):
                t = pool_tmp.rearrange("p q (a b) -> p (q a) b", b=16)[:, 0:PAIRS, 0:n]
                new_c, new_s, old_c, old_s = tc[:, :, n:2 * n], ts[:, :, n:2 * n], tc[:, :, 0:n], ts[:, :, 0:n]
                c.add(g.tensor_tensor(new_c, old_c, over(wc, n), ALU.mult))
                c.link(g.tensor_tensor(t, old_s, over(ws, n), ALU.mult))
                c.add(g.tensor_tensor(new_c, new_c, t, ALU.subtract))
                c.link(g.tensor_tensor(new_s, old_s, over(wc, n), ALU.mult))
                c.link(g.tensor_tensor(t, old_c, over(ws, n), ALU.mult))
                c.link(g.tensor_tensor(new_s, new_s, t, ALU.add))

            def squared(wc, ws, out_c, out_s):
                c.add(g.tensor_tensor(out_c, wc, wc, ALU.mult))
                c.add(g.tensor_tensor(S["w_t"], ws, ws, ALU.mult))
                c.link(g.tensor_tensor(out_s, wc, ws, ALU.mult))
                c.add(g.tensor_tensor(out_c, out_c, S["w_t"], ALU.subtract))
                c.add(g.tensor_tensor(out_s, out_s, out_s, ALU.add))

            with pool.Fori(0, DEPTH) as l:
                c.start(l * POOL_MIX)
                pool.wait_ge(trig_ready.sem, trig_ready.at(l, 1))
                w = (S["cos"], S["sin"])
                spare = [(S["w_c"], S["w_s"]), (S["w_c2"], S["w_s2"])]
                squared(*w, *spare[0])
                for tc, ts in ((low_c, low_s), (high_c, high_s)):
                    c.add(g.memset(tc[:, :, 0:1], 1.0))
                    c.add(g.memset(ts[:, :, 0:1], 0.0))
                c.sync()
                for k in range(8):
                    tc, ts = (low_c, low_s) if k < 4 else (high_c, high_s)
                    doubled(tc, ts, 2 ** (k % 4), *w)
                    w = spare[k % 2]
                    if k < 6:
                        squared(*w, *spare[(k + 1) % 2])
                        c.sync()

                def table(m):
                    if m >= 2:
                        pool.wait_ge(bu_read.sem, bu_read.at(l, m - 1))
                    q = slice(PQ * m, PQ * m + PQ)
                    lo = [v[:, q].unsqueeze(2).broadcast_to([P, PQ, 16, 16]) for v in (low_c, low_s)]
                    hi = [v[:, q].unsqueeze(3).broadcast_to([P, PQ, 16, 16]) for v in (high_c, high_s)]
                    tc, ts, t = (v.rearrange("p q (a b) -> p q a b", b=16) for v in
                                 (tab_c[m % 2], tab_s[m % 2], pool_tmp))
                    c.add(g.tensor_tensor(tc, hi[0], lo[0], ALU.mult))
                    c.add(g.tensor_tensor(ts, hi[1], lo[0], ALU.mult))
                    c.link(g.tensor_tensor(t, hi[1], lo[1], ALU.mult))
                    c.link(g.tensor_tensor(tc, tc, t, ALU.subtract))
                    c.link(g.tensor_tensor(t, hi[0], lo[1], ALU.mult))
                    g.tensor_tensor(ts, ts, t, ALU.add).then_inc(table_ready.sem, 1)
                    pool.wait_ge(table_ready.sem, table_ready.at(l, m + 1))

                def turn_back(m):
                    i = m % 2
                    re, im = quads(st_re[i]), quads(st_im[i])
                    pool.wait_ge(scanned.sem, scanned.at(l, m + 1))
                    if m >= 1:
                        pool.wait_ge(y_in_psum.sem, y_in_psum.at(l, m))
                    c.add(g.tensor_tensor(out_re, re, tab_c[i], ALU.mult))
                    c.link(g.tensor_tensor(pool_tmp, im, tab_s[i], ALU.mult))
                    c.add(g.tensor_tensor(out_re, out_re, pool_tmp, ALU.subtract))
                    c.add(g.tensor_tensor(im, im, tab_c[i], ALU.mult))
                    c.link(g.tensor_tensor(re, re, tab_s[i], ALU.mult))
                    g.tensor_tensor(im, im, re, ALU.add).then_inc(states_ready.sem, 1)
                    pool.wait_ge(states_ready.sem, states_ready.at(l, m + 1))

                table(0)
                table(1)
                for m in range(S5M):
                    turn_back(m)
                    if m + 2 < S5M:
                        table(m + 2)
                assert c.n == POOL_MIX, c.n

        @block.scalar
        def _(act):
            a = nc.scalar
            c = Chain(act, act_chain.sem)
            act.wait_ge(params_loaded.sem, 16)
            act.dma_start(router_sb, router[0].rearrange("(k p) e -> p k e", p=P)).then_inc(router_loaded.sem, 16)
            junk = [tail[:, D * i:D * (i + 1)] for i in range(4)]

            def norm(l, k):
                act.wait_ge(x_ready.sem, x_ready.at(l, 1 + k))
                for b in range(TB):
                    c.add(a.activation((uT, attnT)[b].rearrange("p m t -> p (m t)"), x[:, b], ACT.Square, accum_out=ssq[:, b:b + 1]))
                c.sync()
                a.activation(std, ssq, ACT.Sqrt, scale=1.0 / D, bias=eps).then_inc(std_ready.sem, 1)

            def normed(l):
                for j in (0, 2):
                    act.wait_ge(hT_in_psum.sem, hT_in_psum.at(l, j + 1))
                    for i in range(2):
                        kt = 2 * j + i
                        a.activation(hT[:, kt], psum[:, j, i * SEQ:(i + 1) * SEQ], ACT.Copy,
                                     scale=field["g_mix"][:, kt:kt + 1]).then_inc(hT_act.sem, 1)

            def normed_split(l):
                for kt in range(KD):
                    j, i = kt // 2, kt % 2
                    act.wait_ge(hT_in_psum.sem, hT_in_psum.at(l, 4 + j + 1))
                    a.activation(hT_hi[:, kt], psum[:, j, i * SEQ:(i + 1) * SEQ], ACT.Copy,
                                 scale=field["g_ffn"][:, kt:kt + 1]).then_inc(hT_act.sem, 1)

            act.wait_ge(consts_set.sem, 3)
            with act.Fori(0, DEPTH) as l:
                c.start(l * (ACT_MIX + ACT_FFN))
                norm(l, 0)
                act.wait_ge(params_loaded.sem, params_loaded.at(l, 16))
                a.activation(S["step"], field["log_step"], ACT.Exp).then_inc(step_exp.sem, 1)
                normed(l)
                act.wait_ge(theta_ready.sem, theta_ready.at(l, 1))
                a.activation(S["decay"], S["er"], ACT.Exp)
                a.activation(S["sin"], S["theta"], ACT.Sin, bias=zero)
                a.activation(S["cos"], S["absr"], ACT.Sin, scale=-1.0, bias=half_pi).then_inc(trig_ready.sem, 1)
                act.wait_ge(lat_biased.sem, lat_biased.at(l, 1))
                for b in range(TB):
                    c.add(a.activation(junk[b][:, 0:QR], lat[:, b, 0:QR], ACT.Square, accum_out=lat_ssq[:, b:b + 1]))
                    c.add(a.activation(junk[2 + b][:, 0:KR], lat[:, b, QR:QR + KR], ACT.Square,
                                       accum_out=lat_ssq[:, 2 + b:3 + b]))
                c.sync()
                a.activation(lat_std_v[:, 0:2], lat_ssq[:, 0:2], ACT.Sqrt, scale=1.0 / QR, bias=eps)
                a.activation(lat_std_v[:, 2:4], lat_ssq[:, 2:4], ACT.Sqrt, scale=1.0 / KR,
                             bias=eps).then_inc(lat_std.sem, 1)
                act.wait_ge(bbarT_in_psum.sem, bbarT_in_psum.at(l, 1))
                for j in range(2):
                    ins = a.activation(bT[:, 2 * j:2 * j + 2], psum[:, 6 + j].rearrange(
                        "p (m r s) -> p m r s", m=2, r=2), ACT.Copy)
                ins.then_inc(bbarT_ready.sem, 1)
                for m in range(S5M):
                    act.wait_ge(u_in_psum.sem, u_in_psum.at(l, m + 1))
                    a.activation(uT[:, m], psum[:, 6 + m % 2, 0:SEQ], ACT.Identity,
                                 bias=field["b_u"][:, m:m + 1]).then_inc(u_ready.sem, 1)
                act.wait_ge(latT_in_psum.sem, latT_in_psum.at(l, 1))
                for k in range(2):
                    a.activation(qlT[:, k], psum[:, 4, k * SEQ:(k + 1) * SEQ], ACT.Copy,
                                 scale=field["g_q"][:, k:k + 1]).then_inc(latT_ready.sem, 1)
                act.wait_ge(latT_in_psum.sem, latT_in_psum.at(l, 2))
                a.activation(kvT, psum[:, 5, 0:SEQ], ACT.Copy, scale=field["g_kv"][:, 0:1]).then_inc(latT_ready.sem, 1)

                def gate(g):
                    act.wait_ge(gate_in_psum.sem, gate_in_psum.at(l, g + 1))
                    a.activation(gates[:, g], psum[:, 6 + g % 2, 0:SEQ], ACT.Sigmoid,
                                 bias=field["b_gate"][:, g:g + 1]).then_inc(gate_ready.sem, 1)

                def gelu(m):
                    act.wait_ge(y_ready.sem, y_ready.at(l, m + 1))
                    a.activation(uT[:, m], uT[:, m], ACT.Gelu_apprx_tanh).then_inc(gelu_ready.sem, 1)

                for g in range(4):
                    gate(g)
                for n in range(8):
                    act.wait_ge(qkv_in_psum.sem, qkv_in_psum.at(l, n + 1))
                    b, half = n % 4 // 2, n % 2
                    heads = slice(4 * half, 4 * half + 4)
                    if n < 4:
                        ins = a.activation(q_tok[:, b, heads], psum[:, 4 + n % 2, 0:4 * QK].rearrange(
                            "p (h n) -> p h n", h=4), ACT.Copy)
                    else:
                        kv = psum[:, 4 + n % 2].rearrange("p (h n) -> p h n", h=4)
                        a.activation(k_tok[:, b, heads, 0:NOPE], kv[:, :, 0:NOPE], ACT.Copy)
                        ins = a.activation(v_tok[:, b, heads], kv[:, :, NOPE:], ACT.Copy)
                    ins.then_inc(qkv_copied.sem, 1)
                act.wait_ge(head_ssq.sem, head_ssq.at(l, 1))
                a.activation(hd_std, hd_ssq, ACT.Sqrt, scale=1.0 / QK, bias=eps).then_inc(head_std.sem, 1)
                for g in range(4, 16):
                    gate(g)
                for m in range(S5M):
                    gelu(m)
                for h in range(H):
                    act.wait_ge(qkT_in_psum.sem, qkT_in_psum.at(l, h + 1))
                    a.activation(qkT[0:QK, h], psum[0:QK, h].rearrange("p (w t) -> p w t", w=2),
                                 ACT.Copy).then_inc(qkT_copied.sem, 1)
                for h in range(H):
                    act.wait_ge(max_ready.sem, max_ready.at(l, h + 1))
                    a.activation(probs[:, h, 0:P], probs[:, h, 0:P], ACT.Exp, scale=SCALE,
                                 bias=neg_max[:, 2 * h:2 * h + 1], accum_out=row_sum[:, 2 * h:2 * h + 1])
                    a.activation(probs[:, h, P:3 * P], probs[:, h, P:3 * P], ACT.Exp, scale=SCALE,
                                 bias=neg_max[:, 2 * h + 1:2 * h + 2],
                                 accum_out=row_sum[:, 2 * h + 1:2 * h + 2]).then_inc(exp_ready.sem, 1)
                for h in range(H):
                    act.wait_ge(probsT_in_psum.sem, probsT_in_psum.at(l, h + 1))
                    a.activation(probsT[:, h], psum[:, h, 0:3 * P], ACT.Copy).then_inc(probsT_copied.sem, 1)
                for m in range(S5M):
                    act.wait_ge(glu_in_psum.sem, glu_in_psum.at(l, m + 1))
                    a.activation(glu_sigma[:, m], psum[:, 2 * m + 1, 0:SEQ], ACT.Sigmoid,
                                 bias=field["b_glu"][:, m:m + 1]).then_inc(glu_sig.sem, 1)
                norm(l, 1)
                normed_split(l)
                assert c.n == ACT_MIX, c.n
                with act.If(l < 1):
                    act.wait_ge(hT_dve.sem, 12)
                    act.wait_ge(hT_act.sem, 12)
                    act.dma_start(pl[:, :], params[1]).then_inc(params_loaded.sem, 16)

                    def split(what, tile):
                        n, src = ff_unit(what, tile)
                        if tile % 4 == 0:
                            ffn_landed(act, FFN_ITEMS.index((what, tile // 4)))
                        act.wait_ge(unit_used.sem, n + 1)
                        dst = w_hi[:, n % UNIT_BUFS]
                        if what != "d":
                            dst = dst.rearrange("p (k n) -> p k n", k=KD)
                        a.activation(dst, src, ACT.Copy).then_inc(hi_ready.sem, 1)

                    for n in range(FF_TILES + 2):
                        if n < FF_TILES:
                            split("g", n)
                        if 1 <= n <= FF_TILES:
                            act.wait_ge(unit_used.sem, FF_UNITS.index(("g", n - 1)) + 1 + UNIT_BUFS)
                            if n >= 3:
                                act.wait_ge(ff_act.sem, n - 2)
                            a.activation(ff_sigma[:, (n - 1) % 2], psum[:, 4 + (n - 1) % 2, 0:SEQ],
                                         ACT.Sigmoid).then_inc(ff_sig.sem, 1)
                        if n < FF_TILES:
                            split("u", n)
                        if 1 <= n <= FF_TILES:
                            act.wait_ge(ff_act.sem, n)
                            a.activation(ff_hi[:, (n - 1) % 4], ff_a[:, (n - 1) % 2],
                                         ACT.Copy).then_inc(ff_hi_ready.sem, 1)
                        if n >= 2:
                            split("d", n - 2)

            act.wait_ge(top_ready.sem, 1)
            a.activation(ediff[:, :, 0:1], diff[:, :, 0:1], ACT.Exp).then_inc(top_exp.sem, 1)

            def rows_split(n):
                act.wait_ge(rows_f_ready.sem, n)
                a.activation(rows_hi, rows_f, ACT.Copy).then_inc(rows_hi_ready.sem, 1)

            rows_split(1)

            def split(turn, n):
                i, m = n // UNITS % N_PAIR, n % (N_PAIR * UNITS)
                if n % UNITS == 0:
                    moe_landed(act, turn + n // (N_PAIR * UNITS), i)
                act.wait_ge(unit_used.sem, per_pair(turn, n + 1))
                a.activation(w_hi[:, buf(m)], unit(m), ACT.Copy).then_inc(hi_ready.sem, 1)

            def experts(pair, turn):
                for half in range(2):
                    def at(per, n):
                        return turn * (2 * per) + (half * per + n)

                    def sigma(ch):
                        act.wait_ge(unit_used.sem, per_pair(turn, item_unit(half, "g", ch) + UNITS + UNIT_BUFS))
                        if ch >= 1 or half == 1:
                            act.wait_ge(ex_act.sem, at(FEC, ch))
                        a.activation(ex_sigma, psum[:, ch % 2], ACT.Sigmoid).then_inc(ex_sig.sem, 1)

                    def turned(ch):
                        act.wait_ge(actT_in_psum.sem, at(FEC, ch + 1))
                        a.activation(aT_hi[:, ch % 2], psum[:, 6], ACT.Copy).then_inc(aT_hi_ready.sem, 1)

                    for ch in range(FEC):
                        for part in range(UNITS):
                            if ch:
                                split(turn, item_unit(half, "g", ch) + part)
                            if ch == 1 and part == 1:
                                sigma(0)
                        for part in range(UNITS):
                            split(turn, item_unit(half, "u", ch) + part)
                            if ch and part == 2:
                                turned(ch - 1)
                        for part in range(UNITS if ch else 0):
                            split(turn, item_unit(half, "d", ch - 1) + part)
                            if part == 2:
                                sigma(ch)
                    for part in range(UNITS):
                        split(turn, item_unit(half, "d", FEC - 1) + part)
                        if part == 1:
                            rows_split(at(1, 2))
                            turned(FEC - 1)
                    ahead(act, pair, turn, half, split)
                    act.wait_ge(unit_used.sem, per_pair(turn, (half + 1) * N_EXP * UNITS + UNIT_BUFS))
                    a.activation(y_rows[:, 0:512], psum[:, 4], ACT.Copy).then_inc(y_rows_ready.sem, 1)

            for part in range(UNITS):
                split(0, part)
            with act.Fori(0, E // 2) as pair:
                experts(pair, pair)
            act.wait_ge(count_ready.sem, 1)
            most = act.value_load(most_i[0:1, 0:1], min_val=0, max_val=SEQ)
            with act.If(most > P):
                for part in range(UNITS):
                    split(E // 2, part)
                with act.Fori(0, E // 2) as pair:
                    experts(pair, pair + E // 2)

        @block.tensor
        def _(pe):
            t = nc.tensor

            pe.sem_inc(unit_used.sem, UNIT_BUFS)
            pe.wait_ge(consts_loaded.sem, 16)

            def norm_transposes(l, k):
                pe.wait_ge(diag_ready.sem, diag_ready.at(l, k + 1))
                for kt in range(KD):
                    for b in range(TB):
                        at = (kt % 2) * SEQ + b * P
                        ins = t.matmul(psum[:, kt // 2, at:at + P], x[:, b, kt * P:(kt + 1) * P], diag[:, b],
                                       start=True, stop=True)
                    if kt % 2:
                        ins.then_inc(hT_in_psum.sem, 1)

            def wait_hT(l, k):
                pe.wait_ge(hT_act.sem, hT_act.at(l, 12 if k else 4))
                pe.wait_ge(hT_dve.sem, hT_dve.at(l, 12 if k else 4))

            with pe.Fori(0, DEPTH) as l:
                norm_transposes(l, 0)
                wait_hT(l, 0)
                mix_landed(pe, l, 0)
                w = slot_view(0, KD, LAT)
                for b in range(TB):
                    for kt in range(KD):
                        ins = t.matmul(psum[:, 4 + b, 0:LAT], hT[:, kt, b * P:(b + 1) * P], w[:, kt],
                                       start=kt == 0, stop=kt == KD - 1)
                    ins.then_inc(lat_in_psum.sem, 1)
                pe.wait_ge(bbar_ready.sem, bbar_ready.at(l, 1))
                for m in range(S5M):
                    for r, f in enumerate(("b_re", "b_im")):
                        at = (m % 2) * 2 * P + r * P
                        ins = t.transpose(psum[:, 6 + m // 2, at:at + P], field[f][:, m * P:(m + 1) * P], ident)
                ins.then_inc(bbarT_in_psum.sem, 1)
                pe.wait_ge(bbarT_ready.sem, bbarT_ready.at(l, 1))
                mix_landed(pe, l, 1)
                w = slot_view(1, KD, S5W)
                for m in range(S5M):
                    if m >= 2:
                        pe.wait_ge(u_ready.sem, u_ready.at(l, m - 1))
                    for kt in range(KD):
                        ins = t.matmul(psum[:, 6 + m % 2, 0:SEQ],
                                       w[:, kt, m * P:(m + 1) * P], hT[:, kt], start=kt == 0, stop=kt == KD - 1)
                    ins.then_inc(u_in_psum.sem, 1)
                pe.wait_ge(lat_ready.sem, lat_ready.at(l, 1))
                for k in range(2):
                    for b in range(TB):
                        ins = t.transpose(psum[:, 4, k * SEQ + b * P:k * SEQ + (b + 1) * P],
                                          lat[:, b, k * P:(k + 1) * P], ident)
                ins.then_inc(latT_in_psum.sem, 1)
                for b in range(TB):
                    ins = t.transpose(psum[:, 5, b * P:(b + 1) * P], lat[:, b, QR:QR + KR], ident)
                ins.then_inc(latT_in_psum.sem, 1)

                def input_states(m):
                    pe.wait_ge(u_ready.sem, u_ready.at(l, m + 1))
                    if m:
                        pe.wait_ge(bu_read.sem, bu_read.at(l, m))
                    for r in range(2):
                        for q in range(PQ):
                            rows_q = slice(32 * q, 32 * q + 32)
                            ins = t.matmul(psum[:, q, r * SEQ:(r + 1) * SEQ], bT[rows_q, m, r],
                                           uT[rows_q, m], start=True, stop=True)
                    ins.then_inc(bu_in_psum.sem, 1)

                def read_out(m):
                    pe.wait_ge(states_ready.sem, states_ready.at(l, m + 1))
                    if m >= 2:
                        pe.wait_ge(y_ready.sem, y_ready.at(l, m - 1))
                    im = quads(st_im[m % 2])
                    for q in range(PQ):
                        col = (PQ * m + q) * 32
                        o = psum[32 * q:32 * q + 32, 4 + m % 2, 0:SEQ]
                        t.matmul(o, field["c_re"][:, col:col + 32], out_re[:, q], start=True, stop=False)
                        ins = t.matmul(o, field["c_im"][:, col:col + 32], im[:, q], start=False, stop=True)
                    ins.then_inc(y_in_psum.sem, 1)

                def gate_products(j):
                    item = MIX_ITEMS.index(f"gate{j}")
                    mix_landed(pe, l, item)
                    w = slot_view(item % MIX_SLOTS, KD, 512)
                    for i in range(4):
                        g = 4 * j + i
                        if g >= 2:
                            pe.wait_ge(gate_ready.sem, gate_ready.at(l, g - 1))
                        else:
                            pe.wait_ge(u_ready.sem, u_ready.at(l, S5M))
                        for kt in range(KD):
                            ins = t.matmul(psum[:, 6 + g % 2, 0:SEQ], w[:, kt, i * P:(i + 1) * P], hT[:, kt],
                                           start=kt == 0, stop=kt == KD - 1)
                        ins.then_inc(gate_in_psum.sem, 1)

                input_states(0)
                gate_products(0)
                pe.wait_ge(latT_ready.sem, latT_ready.at(l, 3))
                item = MIX_ITEMS.index("up")
                mix_landed(pe, l, item)
                pe.wait_ge(uq_loaded.sem, uq_loaded.at(l, 16))
                s = item % MIX_SLOTS
                wq = slots[s][:, 0:2 * H * QK].rearrange("p (k n) -> p k n", k=2)
                for n in range(8):
                    b, half = n % 4 // 2, n % 2
                    if n >= 2:
                        pe.wait_ge(qkv_copied.sem, qkv_copied.at(l, n - 1))
                    if n < 4:
                        for k in range(2):
                            ins = t.matmul(psum[:, 4 + n % 2, 0:4 * QK], qlT[:, k, b * P:(b + 1) * P],
                                           wq[:, k, half * 4 * QK:(half + 1) * 4 * QK], start=k == 0, stop=k == 1)
                    else:
                        ins = t.matmul(psum[:, 4 + n % 2], kvT[:, b * P:(b + 1) * P],
                                       slots[s][:, 2048 + half * 512:2048 + half * 512 + 512], start=True, stop=True)
                    ins.then_inc(qkv_in_psum.sem, 1)
                input_states(1)
                gate_products(1)
                pe.wait_ge(qkv_copied.sem, qkv_copied.at(l, 8))
                read_out(0)
                input_states(2)
                gate_products(2)
                read_out(1)
                input_states(3)
                gate_products(3)
                read_out(2)
                read_out(3)
                pe.wait_ge(qk_ready.sem, qk_ready.at(l, 1))
                pe.wait_ge(bu_read.sem, bu_read.at(l, S5M))
                pe.wait_ge(y_ready.sem, y_ready.at(l, S5M))
                pe.wait_ge(gate_ready.sem, gate_ready.at(l, 2 * KD))
                for h in range(H):
                    for i, tok in enumerate((q_tok, k_tok)):
                        for b in range(TB):
                            ins = t.transpose(psum[0:QK, h, i * SEQ + b * P:i * SEQ + (b + 1) * P], tok[:, b, h],
                                              ident)
                    ins.then_inc(qkT_in_psum.sem, 1)
                for h in range(H):
                    pe.wait_ge(qkT_copied.sem, qkT_copied.at(l, h + 1))
                    t.matmul(psum[:, h, 0:P], qkT[0:QK, h, 0, 0:P], qkT[0:QK, h, 1, 0:P], start=True, stop=True)
                    t.matmul(psum[:, h, P:3 * P], qkT[0:QK, h, 0, P:2 * P], qkT[0:QK, h, 1],
                             start=True, stop=True).then_inc(scores_in_psum.sem, 1)
                for h in range(H):
                    pe.wait_ge(probs_ready.sem, probs_ready.at(l, h + 1))
                    for i in range(3):
                        ins = t.transpose(psum[:, h, i * P:(i + 1) * P], probs[:, h, i * P:(i + 1) * P], ident)
                    ins.then_inc(probsT_in_psum.sem, 1)
                for j in range(H // 2):
                    pe.wait_ge(probsT_copied.sem, probsT_copied.at(l, 2 * j + 2))
                    for i in range(2):
                        h = 2 * j + i
                        o = psum[VD * i:VD * i + VD, 2 * j]
                        t.matmul(o[:, 0:P], v_tok[:, 0, h], probsT[:, h, 0:P], start=True, stop=True)
                        t.matmul(o[:, P:2 * P], v_tok[:, 0, h], probsT[:, h, P:2 * P], start=True, stop=False)
                        ins = t.matmul(o[:, P:2 * P], v_tok[:, 1, h], probsT[:, h, 2 * P:3 * P],
                                       start=False, stop=True)
                    ins.then_inc(av_in_psum.sem, 1)
                item = MIX_ITEMS.index("glu")
                mix_landed(pe, l, item)
                pe.wait_ge(gelu_ready.sem, gelu_ready.at(l, S5M))
                w = slot_view(item % MIX_SLOTS, S5M, S5W)
                for m in range(S5M):
                    for kt in range(S5M):
                        ins = t.matmul(psum[:, 2 * m + 1, 0:SEQ], w[:, kt, m * P:(m + 1) * P], uT[:, kt],
                                       start=kt == 0, stop=kt == S5M - 1)
                    ins.then_inc(glu_in_psum.sem, 1)
                pe.wait_ge(glu_sig.sem, glu_sig.at(l, S5M))
                for i, (what, src) in enumerate((("proj_a", attnT), ("proj_s", ssmT))):
                    item = MIX_ITEMS.index(what)
                    mix_landed(pe, l, item)
                    if i == 0:
                        pe.wait_ge(attn_ready.sem, attn_ready.at(l, H // 2))
                    else:
                        pe.wait_ge(ssm_ready.sem, ssm_ready.at(l, S5M))
                    w = slot_view(item % MIX_SLOTS, 4, D)
                    for m in range(KD):
                        for kt in range(4):
                            ins = t.matmul(psum[:, m, i * SEQ:(i + 1) * SEQ], w[:, kt, m * P:(m + 1) * P], src[:, kt],
                                           start=kt == 0, stop=kt == 3)
                        if i:
                            ins.then_inc(proj_in_psum.sem, 1)
                    if i == 0:
                        ins.then_inc(attn_projected.sem, 1)
                pe.wait_ge(mix_ready.sem, mix_ready.at(l, KD))
                for c in range(2):
                    item = MIX_ITEMS.index(f"out{c}")
                    mix_landed(pe, l, item)
                    w = slot_view(item % MIX_SLOTS, KD, 512)
                    for b in range(TB):
                        for kt in range(KD):
                            ins = t.matmul(psum[:, 2 * c + b], gates[:, kt, b * P:(b + 1) * P], w[:, kt],
                                           start=kt == 0, stop=kt == KD - 1)
                        ins.then_inc(mixed_in_psum.sem, 1)
                norm_transposes(l, 1)
                wait_hT(l, 1)
                with pe.If(l < 1):
                    def pair_of(what, tile):
                        n, _ = ff_unit(what, tile)
                        pe.wait_ge(lo_ready.sem, n + 1)
                        return w_hi[:, n % UNIT_BUFS], w_lo[:, n % UNIT_BUFS]

                    for n in range(FF_TILES + 2):
                        if n < FF_TILES:
                            if n >= 2:
                                pe.wait_ge(ff_act.sem, n - 1)
                            for i, what in enumerate("gu"):
                                wh, wl = pair_of(what, n)
                                o = psum[:, 4 + 2 * i + n % 2, 0:SEQ]
                                for kt in range(KD):
                                    at_w = slice(kt * P, (kt + 1) * P)
                                    t.matmul(o, wh[:, at_w], hT_hi[:, kt], start=kt == 0, stop=False)
                                    t.matmul(o, wh[:, at_w], hT_lo[:, kt], start=False, stop=False)
                                    ins = t.matmul(o, wl[:, at_w], hT_hi[:, kt], start=False, stop=kt == KD - 1)
                                ins.then_inc(unit_used.sem, 1)
                        if n >= 2:
                            m = n - 2
                            wh, wl = pair_of("d", m)
                            pe.wait_ge(ff_lo_ready.sem, m + 1)
                            for b in range(TB):
                                ah, al = (a[:, m % 4, b * P:(b + 1) * P] for a in (ff_hi, ff_lo))
                                for a, w in ((ah, wh), (ah, wl), (al, wh)):
                                    for j in range(2):
                                        ins = t.matmul(psum[:, 2 * b + j], a, w[:, 512 * j:512 * j + 512],
                                                       start=m == 0 and a is ah and w is wh,
                                                       stop=m == FF_TILES - 1 and a is al)
                            ins.then_inc(unit_used.sem, 1)

            pe.wait_ge(router_loaded.sem, 16)
            for b in range(TB):
                for i, part in enumerate((hT_hi, hT_lo)):
                    for kt in range(KD):
                        ins = t.matmul(psum[:, 4, b * E:(b + 1) * E], part[:, kt, b * P:(b + 1) * P].bitcast(F32),
                                       router_sb[:, kt], start=i + kt == 0, stop=i == 1 and kt == KD - 1)
            ins.then_inc(logits_in_psum.sem, 1)
            pe.wait_ge(chosen.sem, 1)
            before, ones = const["before"], const["ones"]
            t.matmul(psum[:, 5, 0:E], before, sel[:, 0], start=True, stop=True)
            t.matmul(psum[:, 5, E:2 * E], before, sel[:, 1], start=True, stop=False)
            t.matmul(psum[:, 5, E:2 * E], ones, sel[:, 0], start=False, stop=True)
            t.matmul(psum[:, 5, 2 * E:3 * E], ones, sel[:, 0], start=True, stop=False)
            t.matmul(psum[:, 5, 2 * E:3 * E], ones, sel[:, 1], start=False, stop=True).then_inc(places_in_psum.sem, 1)

            def gather(n):
                pe.wait_ge(pick_ready.sem, n)
                for kt in range(KD):
                    for b in range(TB):
                        ins = t.matmul(psum[:, 1 + 2 * (kt // 4), (kt % 4) * P:(kt % 4 + 1) * P],
                                       x[:, b, kt * P:(kt + 1) * P], pick[:, b], start=b == 0, stop=b == TB - 1)
                    if kt % 4 == 3:
                        ins.then_inc(rows_in_psum.sem, 1)

            gather(1)

            def experts(turn):
                for half in range(2):
                    def at(per, n):
                        return turn * (2 * per) + (half * per + n)

                    def units(what, ch, steps, products):
                        first = item_unit(half, what, ch)
                        for part in range(UNITS):
                            n = first + part
                            pe.wait_ge(lo_ready.sem, per_pair(turn, n + 1))
                            wh, wl = w_hi[:, buf(n)], w_lo[:, buf(n)]
                            for k in range(part * steps, (part + 1) * steps):
                                ins = products(k, k - part * steps, wh, wl)
                            ins.then_inc(unit_used.sem, 1)

                    def product(what, ch):
                        bank = ch % 2 + (2 if what == "u" else 0)
                        o = psum[:, bank]

                        def step(k, i, wh, wl):
                            at_w = slice(512 * i, 512 * i + 512)
                            t.matmul(o, rows_hi[:, k], wh[:, at_w], start=k == 0, stop=False)
                            t.matmul(o, rows_hi[:, k], wl[:, at_w], start=False, stop=False)
                            return t.matmul(o, rows_lo[:, k], wh[:, at_w], start=False, stop=k == KD - 1)

                        units(what, ch, KD // UNITS, step)

                    def turn_act(ch):
                        pe.wait_ge(ex_act.sem, at(FEC, ch + 1))
                        for k in range(4):
                            ins = t.transpose(psum[:, 6, k * P:(k + 1) * P], ex_a[:, ch % 2, k * P:(k + 1) * P],
                                              ident)
                        ins.then_inc(actT_in_psum.sem, 1)

                    def down(ch):
                        pe.wait_ge(aT_lo_ready.sem, at(FEC, ch + 1))

                        def step(k, i, wh, wl):
                            ah, al = (a[:, ch % 2, k * P:(k + 1) * P] for a in (aT_hi, aT_lo))
                            first, last = ch == 0 and k == 0, ch == FEC - 1 and k == 3
                            for j in range(2):
                                at_w = slice(D * i + 512 * j, D * i + 512 * j + 512)
                                t.matmul(psum[:, 4 + j], ah, wh[:, at_w], start=first, stop=False)
                                t.matmul(psum[:, 4 + j], ah, wl[:, at_w], start=False, stop=False)
                            for j in range(2):
                                at_w = slice(D * i + 512 * j, D * i + 512 * j + 512)
                                ins = t.matmul(psum[:, 4 + j], al, wh[:, at_w], start=False, stop=last)
                            return ins

                        units("d", ch, 4 // UNITS, step)

                    pe.wait_ge(rows_lo_ready.sem, at(1, 1))
                    for ch in range(FEC):
                        product("g", ch)
                        if ch:
                            turn_act(ch - 1)
                        product("u", ch)
                        if ch == 1:
                            for b in range(TB):
                                ins = t.transpose(psum[:, 7, b * P:(b + 1) * P], spread_tok[:, b], ident)
                            ins.then_inc(spreadT_in_psum.sem, 1)
                        if ch:
                            down(ch - 1)
                    gather(at(1, 2))
                    turn_act(FEC - 1)
                    down(FEC - 1)
                    pe.wait_ge(spread_ready.sem, at(1, 1))
                    pe.wait_ge(y_rows_ready.sem, at(1, 1))
                    for n in range(4):
                        if n == 1:
                            pe.wait_ge(y_rows_ready_dve.sem, at(1, 1))
                        if n >= 2:
                            pe.wait_ge(spread_added.sem, at(4, n - 1))
                        b, j = n // 2, n % 2
                        t.matmul(psum[:, 7 - n % 2], spread[:, b], y_rows[:, 512 * j:512 * j + 512],
                                 start=True, stop=True).then_inc(spread_in_psum.sem, 1)

            with pe.Fori(0, E // 2) as pair:
                experts(pair)
            pe.wait_ge(count_ready.sem, 1)
            most = pe.value_load(most_i[0:1, 0:1], min_val=0, max_val=SEQ)
            with pe.If(most > P):
                with pe.Fori(0, E // 2) as pair:
                    experts(pair + E // 2)

        @block.vector
        def _(dve):
            v = nc.vector
            c = Chain(dve, dve_chain.sem)

            def tt(o, a, b, op):
                return v.tensor_tensor(o, a, b, op)

            def row(f, n, shape):
                return field[f][:, 0:n].unsqueeze(1).broadcast_to(shape)

            def norm(l, k):
                dve.wait_ge(std_ready.sem, std_ready.at(l, k + 1))
                c.link(v.reciprocal(rstd, std))
                for b in range(TB):
                    ins = v.tensor_scalar(diag[:, b], ident, rstd[:, b:b + 1], None, ALU.mult)
                ins.then_inc(diag_ready.sem, 1)

            def normed(l):
                for j in (1, 3):
                    dve.wait_ge(hT_in_psum.sem, hT_in_psum.at(l, j + 1))
                    for i in range(2):
                        kt = 2 * j + i
                        v.tensor_scalar(hT[:, kt], psum[:, j, i * SEQ:(i + 1) * SEQ], field["g_mix"][:, kt:kt + 1],
                                        None, ALU.mult).then_inc(hT_dve.sem, 1)

            def normed_split(l):
                for j in range(4):
                    dve.wait_ge(hT_act.sem, hT_act.at(l, 4 + 2 * j + 2))
                    for i in range(2):
                        kt = 2 * j + i
                        v.scalar_tensor_tensor(hT_lo[:, kt], psum[:, j, i * SEQ:(i + 1) * SEQ],
                                               field["g_ffn"][:, kt:kt + 1], hT_hi[:, kt].bitcast(F32),
                                               ALU.mult, ALU.subtract).then_inc(hT_dve.sem, 1)

            v.memset(eps, EPS).then_inc(consts_set.sem, 1)
            v.memset(half_pi, float(np.pi / 2)).then_inc(consts_set.sem, 1)
            v.memset(zero, 0.0).then_inc(consts_set.sem, 1)
            dve.wait_ge(consts_loaded.sem, 16)
            dve.wait_ge(x_loaded.sem, 16)
            dve.sem_inc(x_ready.sem, 1)
            with dve.Fori(0, DEPTH) as l:
                c.start(l * (DVE_MIX + DVE_FFN))
                norm(l, 0)
                dve.wait_ge(step_exp.sem, step_exp.at(l, 1))
                c.add(tt(S["er"], field["lam_re"], S["step"], ALU.mult))
                c.link(tt(S["theta"], field["lam_im"], S["step"], ALU.mult))
                c.link(v.tensor_scalar(S["turns"], S["theta"], float(1 / (2 * np.pi)), MAGIC, ALU.mult, ALU.add))
                c.link(v.tensor_scalar(S["turns"], S["turns"], MAGIC, None, ALU.subtract))
                for part in (PI2_A, PI2_B, PI2_C):
                    c.link(v.scalar_tensor_tensor(S["theta"], S["turns"], -part, S["theta"], ALU.mult, ALU.add))
                c.link(v.tensor_scalar(S["theta"], S["theta"], float(np.float32(3.1415925)), -float(np.float32(3.1415925)),
                                       ALU.min, ALU.max))
                c.link(v.tensor_scalar(S["t1"], S["theta"], -1.0, None, ALU.mult))
                tt(S["absr"], S["theta"], S["t1"], ALU.max).then_inc(theta_ready.sem, 1)
                normed(l)
                dve.wait_ge(trig_ready.sem, trig_ready.at(l, 1))
                c.add(tt(S["n_re"], S["decay"], S["cos"], ALU.mult))
                c.add(tt(S["n_im"], S["decay"], S["sin"], ALU.mult))
                c.add(tt(S["den"], field["lam_re"], field["lam_re"], ALU.mult))
                c.link(tt(S["t1"], field["lam_im"], field["lam_im"], ALU.mult))
                c.add(v.tensor_scalar(S["n_re"], S["n_re"], 1.0, None, ALU.subtract))
                c.link(tt(S["den"], S["den"], S["t1"], ALU.add))
                c.add(v.reciprocal(S["den"], S["den"]))
                c.add(tt(S["f_re"], S["n_re"], field["lam_re"], ALU.mult))
                c.add(tt(S["t1"], S["n_im"], field["lam_im"], ALU.mult))
                c.add(tt(S["f_im"], S["n_im"], field["lam_re"], ALU.mult))
                c.link(tt(S["t2"], S["n_re"], field["lam_im"], ALU.mult))
                c.add(tt(S["f_re"], S["f_re"], S["t1"], ALU.add))
                c.link(tt(S["f_im"], S["f_im"], S["t2"], ALU.subtract))
                c.add(tt(S["f_re"], S["f_re"], S["den"], ALU.mult))
                c.link(tt(S["f_im"], S["f_im"], S["den"], ALU.mult))
                b_re, b_im = (field[f].rearrange("p (q n) -> p q n", q=PAIRS) for f in ("b_re", "b_im"))
                f_re, f_im = (S[f].unsqueeze(2).broadcast_to([P, PAIRS, 32]) for f in ("f_re", "f_im"))
                tmp = [dve_tmp[:, 512 * i:512 * i + 512].rearrange("p (q n) -> p q n", q=PAIRS) for i in range(2)]
                c.add(tt(tmp[0], b_im, f_im, ALU.mult))
                c.link(tt(tmp[1], b_re, f_im, ALU.mult))
                c.add(tt(b_re, b_re, f_re, ALU.mult))
                c.link(tt(b_im, b_im, f_re, ALU.mult))
                c.add(tt(b_re, b_re, tmp[0], ALU.subtract))
                tt(b_im, b_im, tmp[1], ALU.add).then_inc(bbar_ready.sem, 1)
                c.add(v.tensor_scalar(field["c_im"], field["c_im"], -1.0, None, ALU.mult))
                for b in range(TB):
                    dve.wait_ge(lat_in_psum.sem, lat_in_psum.at(l, b + 1))
                    ins = tt(lat[:, b], psum[:, 4 + b, 0:LAT], field["b_lat"], ALU.add)
                    if b == 0:
                        c.add(ins)
                ins.then_inc(lat_biased.sem, 1)
                dve.wait_ge(lat_std.sem, lat_std.at(l, 1))
                dve.wait_ge(lat_biased.sem, lat_biased.at(l, 1))
                c.link(v.reciprocal(lat_rstd, lat_std_v))
                for b in range(TB):
                    c.add(v.tensor_scalar(lat[:, b, 0:QR], lat[:, b, 0:QR], lat_rstd[:, b:b + 1], None, ALU.mult))
                    ins = v.tensor_scalar(lat[:, b, QR:QR + KR], lat[:, b, QR:QR + KR], lat_rstd[:, 2 + b:3 + b],
                                          None, ALU.mult)
                    if b == 0:
                        c.add(ins)
                ins.then_inc(lat_ready.sem, 1)

                def states(m):
                    i = m % 2
                    dve.wait_ge(bu_in_psum.sem, bu_in_psum.at(l, m + 1))
                    dve.wait_ge(table_ready.sem, table_ready.at(l, m + 1))
                    if m >= 2:
                        dve.wait_ge(y_in_psum.sem, y_in_psum.at(l, m - 1))
                    bu_re, bu_im = psum[:, 0:PQ, 0:SEQ], psum[:, 0:PQ, SEQ:2 * SEQ]
                    re, im, tmp = quads(st_re[i]), quads(st_im[i]), quads(dve_tmp)
                    c.add(tt(re, bu_re, tab_c[i], ALU.mult))
                    c.add(tt(im, bu_im, tab_c[i], ALU.mult))
                    c.link(tt(tmp, bu_im, tab_s[i], ALU.mult))
                    c.link(tt(re, re, tmp, ALU.add))
                    tt(tmp, bu_re, tab_s[i], ALU.mult).then_inc(bu_read.sem, 1)
                    dve.wait_ge(bu_read.sem, bu_read.at(l, m + 1))
                    c.link(tt(im, im, tmp, ALU.subtract))
                    for s in (re, im):
                        for q in range(PQ):
                            decay = S["decay"][:, PQ * m + q:PQ * m + q + 1].broadcast_to([P, SEQ])
                            ins = v.tensor_tensor_scan(s[:, q], decay, s[:, q], 0.0, ALU.mult, ALU.add)
                            if s is re or q < PQ - 1:
                                c.add(ins)
                    ins.then_inc(scanned.sem, 1)

                def skip(m):
                    dve.wait_ge(y_in_psum.sem, y_in_psum.at(l, m + 1))
                    v.scalar_tensor_tensor(uT[:, m], uT[:, m], field["s5_d"][:, m:m + 1], psum[:, 4 + m % 2, 0:SEQ],
                                           ALU.mult, ALU.add).then_inc(y_ready.sem, 1)

                states(0)
                cos, sin = (const[f].rearrange("p (b n) -> p b n", b=TB) for f in ("cos", "sin"))
                kr = lat[:, :, QR + KR:LAT]
                hq = [squares[:, :, :, 16 * i:16 * i + 16] for i in range(4)]
                flat = qkT_flat[:, 2048:2048 + 16 * 32]
                kg = flat[:, 0:TB * ROPE].rearrange("p (b n) -> p b n", b=TB)
                kt = flat[:, 64:64 + TB * ROPE].rearrange("p (b n) -> p b n", b=TB)
                krt = flat[:, 128:128 + TB * ROPE].rearrange("p (b n) -> p b n", b=TB)
                c.add(tt(kg, kr, row("g_kh", QK, [P, TB, QK])[:, :, NOPE:], ALU.mult))
                c.link(tt(kt, kr, kr, ALU.mult))
                c.link(v.tensor_reduce(kr_ssq, kt, AX_X, ALU.add))

                def rope(o, a, cos, sin, tmp):
                    a1, a2 = a[..., 0:HALF], a[..., HALF:]
                    c.add(tt(tmp[0], a1, cos, ALU.mult))
                    c.add(tt(tmp[1], a2, sin, ALU.mult))
                    c.add(tt(tmp[2], a2, cos, ALU.mult))
                    c.link(tt(tmp[3], a1, sin, ALU.mult))
                    c.add(tt(o[..., 0:HALF], tmp[0], tmp[1], ALU.subtract))
                    return tt(o[..., HALF:], tmp[2], tmp[3], ALU.add)

                t4 = [flat[:, 192 + 32 * i:224 + 32 * i].rearrange("p (b n) -> p b n", b=TB) for i in range(4)]
                c.link(rope(krt, kg, cos, sin, t4))
                dve.wait_ge(qkv_copied.sem, qkv_copied.at(l, 8))
                flat_h = squares.rearrange("p b h n -> p (b h) n")
                qf, kf = (w.rearrange("p b h n -> p (b h) n") for w in (q_tok, k_tok))
                c.link(tt(flat_h, qf, qf, ALU.mult))
                c.link(v.tensor_reduce(hd_ssq[:, 0:16], flat_h, AX_X, ALU.add))
                c.link(tt(flat_h[:, :, 0:NOPE], kf[:, :, 0:NOPE], kf[:, :, 0:NOPE], ALU.mult))
                c.link(v.tensor_reduce(hd_ssq[:, 16:32], flat_h[:, :, 0:NOPE], AX_X, ALU.add))
                k_ssq = hd_ssq[:, 16:32].rearrange("p (b h) -> p b h", b=TB)
                tt(k_ssq, k_ssq, kr_ssq.unsqueeze(2).broadcast_to([P, TB, H]), ALU.add).then_inc(head_ssq.sem, 1)
                dve.wait_ge(head_std.sem, head_std.at(l, 1))
                c.link(v.reciprocal(hd_rstd, hd_std))
                rq = hd_rstd[:, 0:16].unsqueeze(2)
                rk = hd_rstd[:, 16:32].unsqueeze(2)
                c.add(tt(qf, qf, rq.broadcast_to([P, TB * H, QK]), ALU.mult))
                c.add(tt(kf[:, :, 0:NOPE], kf[:, :, 0:NOPE], rk.broadcast_to([P, TB * H, NOPE]), ALU.mult))
                rkb = hd_rstd[:, 16:32].rearrange("p (b h) -> p b h", b=TB).unsqueeze(3)
                c.link(tt(k_tok[:, :, :, NOPE:], krt.unsqueeze(2).broadcast_to([P, TB, H, ROPE]),
                          rkb.broadcast_to([P, TB, H, ROPE]), ALU.mult))
                c.add(tt(kf[:, :, 0:NOPE], kf[:, :, 0:NOPE], row("g_kh", NOPE, [P, TB * H, NOPE]), ALU.mult))
                c.link(tt(qf, qf, row("g_qh", QK, [P, TB * H, QK]), ALU.mult))
                cos_h, sin_h = (w.unsqueeze(2).broadcast_to([P, TB, H, HALF]) for w in (cos, sin))
                t4 = [qkT_flat[:, 256 * i:256 * i + 256].rearrange("p (b h n) -> p b h n", b=TB, h=H)
                      for i in range(4)]
                rope(q_tok[:, :, :, NOPE:], q_tok[:, :, :, NOPE:], cos_h, sin_h, t4).then_inc(qk_ready.sem, 1)
                states(1)
                states(2)
                skip(0)
                states(3)
                skip(1)
                skip(2)
                skip(3)
                dve.wait_ge(qkT_in_psum.sem, qkT_in_psum.at(l, H))
                for h in range(H):
                    dve.wait_ge(scores_in_psum.sem, scores_in_psum.at(l, h + 1))
                    tt(probs[:, h], psum[:, h, 0:3 * P], mask, ALU.add).then_inc(scores_masked.sem, 1)
                    dve.wait_ge(scores_masked.sem, scores_masked.at(l, h + 1))
                    c.add(v.tensor_reduce(row_max[:, 2 * h:2 * h + 1], probs[:, h, 0:P], AX_X, ALU.max))
                    c.link(v.tensor_reduce(row_max[:, 2 * h + 1:2 * h + 2], probs[:, h, P:3 * P], AX_X, ALU.max))
                    v.tensor_scalar(neg_max[:, 2 * h:2 * h + 2], row_max[:, 2 * h:2 * h + 2], -SCALE, None,
                                    ALU.mult).then_inc(max_ready.sem, 1)
                for h in range(H):
                    dve.wait_ge(exp_ready.sem, exp_ready.at(l, h + 1))
                    c.link(v.reciprocal(row_inv[:, 2 * h:2 * h + 2], row_sum[:, 2 * h:2 * h + 2]))
                    c.add(v.tensor_scalar(probs[:, h, 0:P], probs[:, h, 0:P], row_inv[:, 2 * h:2 * h + 1], None,
                                          ALU.mult))
                    v.tensor_scalar(probs[:, h, P:3 * P], probs[:, h, P:3 * P], row_inv[:, 2 * h + 1:2 * h + 2], None,
                                    ALU.mult).then_inc(probs_ready.sem, 1)
                for j in range(H // 2):
                    dve.wait_ge(av_in_psum.sem, av_in_psum.at(l, j + 1))
                    v.tensor_copy(attnT[:, j], psum[:, 2 * j, 0:SEQ]).then_inc(attn_ready.sem, 1)
                for m in range(S5M):
                    dve.wait_ge(glu_sig.sem, glu_sig.at(l, m + 1))
                    tt(ssmT[:, m], uT[:, m], glu_sigma[:, m], ALU.mult).then_inc(ssm_ready.sem, 1)
                for m in range(KD):
                    dve.wait_ge(proj_in_psum.sem, proj_in_psum.at(l, m + 1))
                    both = gates_w[:, :, m]
                    c.link(tt(both, both, psum[:, m].rearrange("p (w t) -> p w t", w=2), ALU.mult))
                    tt(gates[:, m], gates[:, m], gates[:, KD + m], ALU.add).then_inc(mix_ready.sem, 1)
                for n in range(4):
                    dve.wait_ge(mixed_in_psum.sem, mixed_in_psum.at(l, n + 1))
                    xs = x[:, n % 2, 512 * (n // 2):512 * (n // 2) + 512]
                    ins = tt(xs, xs, psum[:, n], ALU.add)
                    if n < 3:
                        c.add(ins)
                ins.then_inc(x_ready.sem, 1)
                norm(l, 1)
                normed_split(l)
                assert c.n == DVE_MIX, c.n
                with dve.If(l < 1):
                    c.start(DVE_MIX)

                    def split(what, tile):
                        n, src = ff_unit(what, tile)
                        hi, lo = w_hi[:, n % UNIT_BUFS].bitcast(F32), w_lo[:, n % UNIT_BUFS]
                        if what != "d":
                            hi, lo = (w.rearrange("p (k n) -> p k n", k=KD) for w in (hi, lo))
                        dve.wait_ge(hi_ready.sem, n + 1)
                        tt(lo, src, hi, ALU.subtract).then_inc(lo_ready.sem, 1)

                    for n in range(FF_TILES + 2):
                        m = n - 1
                        if n < FF_TILES:
                            split("g", n)
                        if 0 <= m < FF_TILES:
                            gate_ps, up_ps = (psum[:, i + m % 2, 0:SEQ] for i in (4, 6))
                            dve.wait_ge(ff_sig.sem, m + 1)
                            if m >= 2:
                                dve.wait_ge(ff_hi_ready.sem, m - 1)
                            c.link(tt(ff_a[:, m % 2], ff_sigma[:, m % 2], gate_ps, ALU.mult))
                            dve.wait_ge(unit_used.sem, FF_UNITS.index(("u", m)) + 1 + UNIT_BUFS)
                            tt(ff_a[:, m % 2], ff_a[:, m % 2], up_ps, ALU.mult).then_inc(ff_act.sem, 1)
                        if n < FF_TILES:
                            split("u", n)
                        if n >= 2:
                            split("d", n - 2)
                        if 0 <= m < FF_TILES:
                            dve.wait_ge(ff_hi_ready.sem, m + 1)
                            tt(ff_lo[:, m % 4], ff_a[:, m % 2], ff_hi[:, m % 4].bitcast(F32),
                               ALU.subtract).then_inc(ff_lo_ready.sem, 1)
                    dve.wait_ge(unit_used.sem, N_FF_UNITS + UNIT_BUFS)
                    for n in range(4):
                        xs = x[:, n // 2, 512 * (n % 2):512 * (n % 2) + 512]
                        ins = tt(xs, xs, psum[:, n], ALU.add)
                        if n < 3:
                            c.add(ins)
                    ins.then_inc(x_ready.sem, 1)
                    assert c.n == DVE_FFN, c.n

            c.start(DEPTH * DVE_MIX + DVE_FFN)
            dve.wait_ge(logits_in_psum.sem, 1)
            c.link(tt(logits, psum[:, 4, 0:TB * E].rearrange("p (b e) -> p b e", b=TB),
                      const["r_b"].unsqueeze(1).broadcast_to([P, TB, E]), ALU.add))
            for b in range(TB):
                c.add(v.max(top[:, b], logits[:, b]))
            c.sync()
            for b in range(TB):
                c.add(v.max_index(top_i[:, b], top[:, b], logits[:, b]))
            tt(diff[:, :, 0:1], top[:, :, 1:2], top[:, :, 0:1], ALU.subtract).then_inc(top_ready.sem, 1)
            c.sync()
            c.link(v.tensor_copy(top_f, top_i))
            dve.wait_ge(top_exp.sem, 1)
            c.link(v.tensor_scalar(den2[:, :, 0:1], ediff[:, :, 0:1], 1.0, None, ALU.add))
            c.link(v.reciprocal(w_first[:, :, 0:1], den2[:, :, 0:1]))
            c.link(tt(w_second[:, :, 0:1], ediff[:, :, 0:1], w_first[:, :, 0:1], ALU.mult))
            iota = const["iota"]
            for b in range(TB):
                i0, i1 = top_f[:, b, 0:1], top_f[:, b, 1:2]
                c.add(v.tensor_scalar(hot0[:, b], iota[:, 0:E], i0, None, ALU.is_equal))
                c.link(v.tensor_scalar(hot1[:, b], iota[:, 0:E], i1, None, ALU.is_equal))
                c.link(tt(sel[:, b], hot0[:, b], hot1[:, b], ALU.add))
                c.add(v.tensor_scalar(hot0[:, b], hot0[:, b], w_first[:, b, 0:1], None, ALU.mult))
                c.link(v.tensor_scalar(hot1[:, b], hot1[:, b], w_second[:, b, 0:1], None, ALU.mult))
                ins = tt(comb[:, b], hot0[:, b], hot1[:, b], ALU.add)
                if b == 0:
                    c.add(ins)
            ins.then_inc(chosen.sem, 1)
            c.link(v.tensor_copy(g_rows, field["g_ffn"]))
            c.add(v.tensor_copy(x_out, x))
            dve.wait_ge(places_in_psum.sem, 1)
            dve.wait_ge(chosen.sem, 1)
            c.add(v.tensor_reduce(diff[:, 0, 1:2], psum[:, 5, 2 * E:3 * E], AX_X, ALU.max))
            c.link(v.scalar_tensor_tensor(place[:, :, 0:E], psum[:, 5, 0:2 * E].rearrange("p (b e) -> p b e", b=TB), 1.0,
                                          sel, ALU.add, ALU.mult))
            v.tensor_copy(most_i[:, 0:1], diff[:, 0, 1:2]).then_inc(count_ready.sem, 1)
            c.add(v.tensor_scalar(place[:, :, E:2 * E], place[:, :, 0:E], 1.0 + P, None, ALU.subtract))
            c.sync()
            c.add(v.tensor_scalar(place[:, :, 0:E], place[:, :, 0:E], 1.0, None, ALU.subtract))
            c.add(v.memset(place[:, :, 2 * E:], -1.0))
            c.add(v.memset(weight[:, :, 2 * E:], 0.0))
            c.add(v.tensor_copy(weight[:, :, 0:E], comb))
            c.link(v.tensor_copy(weight[:, :, E:2 * E], comb))
            assert c.n == DVE_ROUTE, c.n

            def choose(g, n):
                if isinstance(n, int):
                    assert n == 1
                else:
                    dve.wait_ge(spreadT_in_psum.sem, n - 1)
                    dve.wait_ge(rows_in_psum.sem, (n - 1) * 2)
                for b in range(TB):
                    v.tensor_scalar(pick[:, b], iota, place[:, b, g], rstd[:, b:b + 1], ALU.is_equal, ALU.mult)
                    ins = v.tensor_scalar(spread_tok[:, b], iota, place[:, b, g], weight[:, b, g],
                                          ALU.is_equal, ALU.mult)
                ins.then_inc(pick_ready.sem, 1)

            def take_rows(n):
                for j in range(2):
                    dve.wait_ge(rows_in_psum.sem, n * 2 - 1 + j)
                    gain = g_rows[:, 4 * j:4 * j + 4].unsqueeze(2).broadcast_to([P, 4, P])
                    ins = tt(rows_f[:, 4 * j:4 * j + 4], psum[:, 1 + 2 * j].rearrange("p (k j) -> p k j", k=4), gain,
                             ALU.mult)
                ins.then_inc(rows_f_ready.sem, 1)
                dve.wait_ge(rows_hi_ready.sem, n)
                tt(rows_lo, rows_f, rows_hi.bitcast(F32), ALU.subtract).then_inc(rows_lo_ready.sem, 1)

            choose(slice(0, 1), 1)
            take_rows(1)

            def split(turn, n):
                m = n % (N_PAIR * UNITS)
                dve.wait_ge(hi_ready.sem, per_pair(turn, n + 1))
                tt(w_lo[:, buf(m)], unit(m), w_hi[:, buf(m)].bitcast(F32),
                   ALU.subtract).then_inc(lo_ready.sem, 1)

            def experts(pair, turn):
                c.start(turn * DVE_PAIR + (DEPTH * DVE_MIX + DVE_FFN + DVE_ROUTE))
                for half in range(2):
                    def at(per, n):
                        return turn * (2 * per) + (half * per + n)

                    def act_of(ch):
                        dve.wait_ge(ex_sig.sem, at(FEC, ch + 1))
                        if ch >= 2:
                            dve.wait_ge(actT_in_psum.sem, at(FEC, ch - 1))
                        c.link(tt(ex_a[:, ch % 2], ex_sigma, psum[:, ch % 2], ALU.mult))
                        dve.wait_ge(unit_used.sem, per_pair(turn, item_unit(half, "u", ch) + UNITS + UNIT_BUFS))
                        tt(ex_a[:, ch % 2], ex_a[:, ch % 2], psum[:, 2 + ch % 2], ALU.mult).then_inc(ex_act.sem, 1)

                    def rest_of_act(ch):
                        dve.wait_ge(aT_hi_ready.sem, at(FEC, ch + 1))
                        tt(aT_lo[:, ch % 2], psum[:, 6], aT_hi[:, ch % 2].bitcast(F32), ALU.subtract).then_inc(
                            aT_lo_ready.sem, 1)

                    for ch in range(FEC):
                        for part in range(UNITS):
                            if ch:
                                split(turn, item_unit(half, "g", ch) + part)
                            if ch and part == 1:
                                act_of(ch - 1)
                        for part in range(UNITS):
                            split(turn, item_unit(half, "u", ch) + part)
                            if ch and part == 2:
                                rest_of_act(ch - 1)
                        if ch == 2:
                            dve.wait_ge(spreadT_in_psum.sem, at(1, 1))
                            v.tensor_copy(spread.rearrange("p b t -> p (b t)"), psum[:, 7, 0:TB * P]).then_inc(
                                spread_ready.sem, 1)
                        if ch == 3:
                            choose(bass.ds(turn * 2 + (half + 1), 1), at(1, 2))
                        for part in range(UNITS if ch else 0):
                            split(turn, item_unit(half, "d", ch - 1) + part)
                    for part in range(UNITS):
                        split(turn, item_unit(half, "d", FEC - 1) + part)
                        if part == 0:
                            act_of(FEC - 1)
                        if part == 1:
                            take_rows(at(1, 2))
                            rest_of_act(FEC - 1)
                    ahead(dve, pair, turn, half, split)
                    dve.wait_ge(unit_used.sem, per_pair(turn, (half + 1) * N_EXP * UNITS + UNIT_BUFS))
                    v.tensor_copy(y_rows[:, 512:], psum[:, 5]).then_inc(y_rows_ready_dve.sem, 1)
                    for n in range(4):
                        b, j = n // 2, n % 2
                        dve.wait_ge(spread_in_psum.sem, at(4, n + 1))
                        xs = x_out[:, b, 512 * j:512 * j + 512]
                        tt(xs, xs, psum[:, 7 - n % 2], ALU.add).then_inc(spread_added.sem, 1)
                assert c.n == DVE_PAIR, c.n

            for part in range(UNITS):
                split(0, part)
            with dve.Fori(0, E // 2) as pair:
                experts(pair, pair)
            dve.wait_ge(count_ready.sem, 1)
            most = dve.value_load(most_i[0:1, 0:1], min_val=0, max_val=SEQ)
            with dve.If(most > P):
                for part in range(UNITS):
                    split(E // 2, part)
                with dve.Fori(0, E // 2) as pair:
                    experts(pair, pair + E // 2)
            dve.drain().then_inc(out_ready.sem, 1)


def _packed(i):
    def channels(a):
        return a.reshape(DEPTH, -1, P).transpose(0, 2, 1)

    def pairs(a):
        return a.reshape(DEPTH, PAIRS, 2 * STATES).transpose(0, 2, 1)

    def two_groups(a):
        a = a.reshape(DEPTH, PAIRS, 2, STATES, CH)
        wide = np.zeros((DEPTH, PAIRS, 2, STATES, 2, CH), a.dtype)
        for g in range(2):
            wide[:, :, g, :, g] = a[:, :, g]
        return wide.reshape(DEPTH, PAIRS, P, 32).transpose(0, 2, 1, 3).reshape(DEPTH, P, PAIRS * 32)

    def spread(a):
        return np.broadcast_to(a[:, None, :], (DEPTH, P, a.shape[1]))

    b_in = i["b_in"]
    step = np.broadcast_to(i["s5_log_step"][:, :, None], (DEPTH, GROUPS, STATES))
    values = {
        "g_mix": channels(i["ln_mix_g"]), "g_ffn": channels(i["ln_ffn_g"]), "b_u": channels(b_in[:, LAT:LAT + S5W]),
        "b_gate": channels(b_in[:, LAT + S5W:]), "s5_d": channels(i["s5_d"]), "b_glu": channels(i["b_glu"]),
        "g_q": channels(i["q_norm_g"]), "g_kv": channels(i["kv_norm_g"]), "lam_re": pairs(i["s5_lam_re"]),
        "lam_im": pairs(i["s5_lam_im"]), "log_step": pairs(step), "b_re": two_groups(i["s5_b_re"]),
        "b_im": two_groups(i["s5_b_im"]), "c_re": two_groups(i["s5_c_re"].transpose(0, 1, 3, 2)),
        "c_im": two_groups(i["s5_c_im"].transpose(0, 1, 3, 2)), "b_lat": spread(b_in[:, :LAT]),
        "g_qh": spread(i["q_head_g"]), "g_kh": spread(i["k_head_g"]),
    }
    return np.ascontiguousarray(np.concatenate([values[n] for n, _ in FIELDS], 2))


def _constants(router_b):
    rows = np.arange(P)
    causal = np.where(rows[None, :] <= rows[:, None], 0.0, NEG)
    inv = np.power(np.float32(10000.0), -np.arange(0, ROPE, 2, dtype=np.float32) / np.float32(ROPE))
    angle = (np.arange(SEQ, dtype=np.float32)[:, None] * inv[None, :]).reshape(TB, P, HALF).transpose(1, 0, 2)
    values = {"ident": np.eye(P), "mask": np.concatenate([causal, np.zeros((P, P)), causal], 1),
              "cos": np.cos(angle).reshape(P, -1), "sin": np.sin(angle).reshape(P, -1),
              "before": rows[:, None] < rows[None, :], "ones": np.ones((P, P)),
              "iota": np.broadcast_to(rows[None, :], (P, P)), "r_b": np.broadcast_to(router_b, (P, E))}
    return np.concatenate([values[n].astype(np.float32) for n, _ in CONSTS], 1)


def kernel(**inputs):
    import concourse.bacc as bacc
    from concourse.bass_utils import run_bass_kernel_spmd

    nc = bacc.Bacc("TRN2", target_bir_lowering=False, num_devices=1)
    i = {n: np.asarray(a) for n, a in inputs.items()}
    given = {"x": i["x"].reshape(SEQ, D), "params": _packed(i), "consts": _constants(i["router_b"])}
    for n in ("w_in", "w_uq", "w_ukv", "w_glu", "w_proj_attn", "w_proj_ssm", "w_out", "ffn_w_gate", "ffn_w_up",
              "ffn_w_down", "router_w"):
        given[n] = i[n]
    for n in ("moe_w_gate", "moe_w_up", "moe_w_down"):
        given[n] = i[n][0]
    arrays = {f"{n}_dram": np.ascontiguousarray(a) for n, a in given.items()}
    args = [nc.dram_tensor(n, a.shape, mybir.dt.from_np(a.dtype), kind="ExternalInput").ap()
            for n, a in arrays.items()]
    out = nc.dram_tensor("out_dram", (SEQ, D), F32, kind="ExternalOutput").ap()
    hybrid_trunk(nc, *args, out)
    r = run_bass_kernel_spmd(nc, [arrays], core_ids=[0])
    return r.results[0]["out_dram"].reshape(1, SEQ, D)
```

```python
from contextlib import ExitStack

import numpy as np

import concourse.bass as bass
from concourse import mybir

F32 = mybir.dt.float32
F32R = mybir.dt.float32r
I32 = mybir.dt.int32
U32 = mybir.dt.uint32
ALU = mybir.AluOpType
ACT = mybir.ActivationFunctionType
AX_X = mybir.AxisListType.X

P = 128
D = 1024
KD = D // P
SEQ = 256
TB = SEQ // P
DEPTH = 2
H = 8
NOPE = 64
ROPE = 32
HALF = ROPE // 2
QK = NOPE + ROPE
VD = 64
QR = 256
KR = 128
LAT = QR + KR + ROPE
S5W = 512
S5M = S5W // P
GROUPS = 32
STATES = 64
CH = 16
PAIRS = GROUPS // 2
PQ = PAIRS // S5M
FF = 2816
FFC = 6
E = 8
FE = 3584
FEC = FE // 512
EPS = 1e-6
NEG = -1e30
SCALE = QK ** -0.5
HEADS = (0, 1, 2, 3, 6, 7, 4, 5)
PI2_A = 6.28125
PI2_B = float(np.float32(2 * np.pi - 6.28125).astype(np.float16))
PI2_C = float(2 * np.pi - PI2_A - PI2_B)
MAGIC = 1.5 * 2 ** 23

FIELDS = [("g_mix", KD), ("g_ffn", KD), ("b_u", S5M), ("b_gate", 2 * KD), ("s5_d", S5M), ("b_glu", S5M),
          ("g_q", QR // P), ("g_kv", KR // P), ("lam_re", PAIRS), ("lam_im", PAIRS), ("log_step", PAIRS),
          ("b_re", PAIRS * 32), ("b_im", PAIRS * 32), ("c_re", PAIRS * 32), ("c_im", PAIRS * 32),
          ("b_lat", LAT), ("g_qh", QK), ("g_kh", QK)]
NPL = sum(n for _, n in FIELDS)
CONSTS = [("ident", P), ("mask", P), ("cos", TB * HALF), ("sin", TB * HALF), ("before", P), ("ones", P),
          ("iota", P), ("r_b", E)]
NC_ = sum(n for _, n in CONSTS)

RING = 6
SLOT = 4096
MIX_SLOTS = 4
MIX_ITEMS = ["u", "lat", "gate0", "up", "gate1", "gate2", "gate3", "glu", "proj_a", "proj_s", "out0", "out1"]
N_MIX = len(MIX_ITEMS)
FFN_ITEMS = [(_w, _c) for _c in range(FFC) for _w in "gud"]
N_FFN = len(FFN_ITEMS)
MOE_ITEMS = [("g", 0), ("u", 0)]
for _c in range(1, FEC):
    MOE_ITEMS += [("g", _c), ("u", _c), ("d", _c - 1)]
MOE_ITEMS += [("d", FEC - 1)]
N_EXP = len(MOE_ITEMS)
N_PAIR = 2 * N_EXP
UNIT = 1024
UNITS = SLOT // UNIT
UNIT_BUFS = 7
FF_TILES = FF // P
FF_UNITS = []
for _n in range(FF_TILES + 2):
    FF_UNITS += [(_w, _n) for _w in "gu" if _n < FF_TILES] + [("d", _n - 2)] * (_n >= 2)
N_FF_UNITS = len(FF_UNITS)


class Signal:

    def __init__(self, ctx, nc, name, per_layer=0):
        self.sem, self.per = ctx.enter_context(nc.semaphore(name)), per_layer

    def at(self, layer, n):
        return layer * self.per + n


class Chain:

    def __init__(self, eng, sem):
        self.eng, self.sem, self.base, self.n = eng, sem, 0, 0

    def start(self, base):
        self.base, self.n = base, 0

    def add(self, ins):
        ins.then_inc(self.sem, 1)
        self.n += 1

    def sync(self):
        self.eng.wait_ge(self.sem, self.base + self.n)

    def link(self, ins):
        self.add(ins)
        self.sync()


DVE_MIX, DVE_FFN, DVE_ROUTE, DVE_PAIR = (174, 22, 30, 14)
ACT_MIX = 8
POOL_MIX = 102


def hybrid_trunk(nc, x_in, params, consts, w_in, w_uq, w_ukv, w_glu, w_pa, w_ps, w_out,
                 f_gate, f_up, f_down, router, m_gate, m_up, m_down, out):
    with ExitStack() as ctx:
        def sb(name, cols, dt=F32, parts=P):
            return ctx.enter_context(nc.sbuf_tensor(name, [parts, cols], dt))

        def sig(name, per=0):
            return Signal(ctx, nc, name, per)

        ring_at = (nc.sbuf_base + 31) // 32 * 32
        ring = sb("ring", RING * SLOT)
        slot_lo = [nc.alloc_sbuf_tensor_at(f"slot_lo{s}", [P, SLOT], F32R, offset=ring_at + 4 * SLOT * s)
                   for s in range(MIX_SLOTS)]
        x = sb("x", TB * D)[:, :].rearrange("p (b d) -> p b d", b=TB)
        cst = sb("cst", NC_)
        stat = sb("stat", 240)
        router_sb = sb("router_sb", KD * E)[:, :].rearrange("p (k e) -> p k e", k=KD)
        most_i = sb("most_i", 8, I32)
        area_at = (nc.sbuf_base + 31) // 32 * 32
        area_cols = (nc.sbuf_usable_end - area_at) // 4 // 8 * 8 - 8
        sb("area", area_cols)
        taken = [0]

        def sb(name, cols, dt=F32):
            at, taken[0] = taken[0], taken[0] + (cols + 7) // 8 * 8
            assert taken[0] <= area_cols, (name, taken[0], area_cols)
            return nc.alloc_sbuf_tensor_at(name, [P, cols], dt, offset=area_at + 4 * at)

        pl = sb("pl", NPL)
        at_split = taken[0]
        w_hi = sb("w_hi", UNIT_BUFS * UNIT, F32R)[:, :].rearrange("p (i n) -> p i n", i=UNIT_BUFS)
        w_lo = sb("w_lo", UNIT_BUFS * UNIT, F32R)[:, :].rearrange("p (i n) -> p i n", i=UNIT_BUFS)
        at_hT = taken[0]
        taken[0] = at_split
        work = sb("work", 11 * 1024)
        taken[0] = at_split
        work_hi = sb("work_hi", 11 * 1024, F32R)
        uT = sb("uT", S5M * SEQ)[:, :].rearrange("p (m t) -> p m t", m=S5M)
        bT = sb("bT", S5M * 2 * P)[:, :].rearrange("p (m r s) -> p m r s", m=S5M, r=2)
        at_attn = taken[0]
        attnT = sb("attnT", 4 * SEQ)[:, :].rearrange("p (k t) -> p k t", k=4)
        taken[0] = at_attn
        attn_lo = sb("attn_lo", 4 * SEQ, F32R)[:, :].rearrange("p (k t) -> p k t", k=4)
        assert taken[0] <= at_hT
        taken[0] = at_hT
        hT = sb("hT", KD * SEQ)[:, :].rearrange("p (k t) -> p k t", k=KD)
        at_gates = taken[0]
        gates_t = sb("gates", 2 * KD * SEQ)
        gates = gates_t[:, :].rearrange("p (m t) -> p m t", m=2 * KD)
        taken[0] = at_gates
        mixed_parts = sb("mixed_parts", 2 * KD * SEQ, F32R)[:, :].rearrange("p (m t) -> p m t", m=2 * KD)
        early = sb("early", LAT * TB + 3 * SEQ)
        small = sb("small", 24 * PAIRS)
        taken[0] = at_hT
        hT_hi = sb("hT_hi", KD * SEQ, F32R)[:, :].rearrange("p (k t) -> p k t", k=KD)
        hT_lo = sb("hT_lo", KD * SEQ, F32R)[:, :].rearrange("p (k t) -> p k t", k=KD)
        ff_sigma = sb("ff_sigma", 2 * SEQ)[:, :].rearrange("p (i t) -> p i t", i=2)
        ff_a = sb("ff_a", 2 * SEQ)[:, :].rearrange("p (i t) -> p i t", i=2)
        ff_hi = sb("ff_hi", 4 * SEQ, F32R)[:, :].rearrange("p (i t) -> p i t", i=4)
        ff_lo = sb("ff_lo", 4 * SEQ, F32R)[:, :].rearrange("p (i t) -> p i t", i=4)
        taken[0] = 0
        x_out = sb("x_out", TB * D)[:, :].rearrange("p (b d) -> p b d", b=TB)
        rt = sb("rt", 320)
        spread = sb("spread", TB * P)[:, :].rearrange("p (b t) -> p b t", b=TB)
        assert taken[0] <= at_split
        taken[0] = at_hT
        y_rows = sb("y_rows", D)
        pick = sb("pick", TB * P)[:, :].rearrange("p (b j) -> p b j", b=TB)
        spread_tok = sb("spread_tok", TB * P)[:, :].rearrange("p (b j) -> p b j", b=TB)
        rows_f = sb("rows_f", D)[:, :].rearrange("p (k j) -> p k j", k=KD)
        rows_hi = sb("rows_hi", D, F32R)[:, :].rearrange("p (k j) -> p k j", k=KD)
        rows_lo = sb("rows_lo", D, F32R)[:, :].rearrange("p (k j) -> p k j", k=KD)
        ex_sigma = sb("ex_sigma", 512)[:, :]
        ex_a = sb("ex_a", 2 * 512)[:, :].rearrange("p (i f) -> p i f", i=2)
        aT_hi = sb("aT_hi", 2 * 512, F32R)[:, :].rearrange("p (i n) -> p i n", i=2)
        aT_lo = sb("aT_lo", 2 * 512, F32R)[:, :].rearrange("p (i n) -> p i n", i=2)
        psum = ctx.enter_context(nc.psum_tensor("psum", [P, 8, 512], F32))

        field, at = {}, 0
        for name, n in FIELDS:
            field[name] = pl[:, at:at + n]
            at += n
        const, at = {}, 0
        for name, n in CONSTS:
            const[name] = cst[:, at:at + n]
            at += n
        ident, mask = const["ident"], const["mask"]

        slots = [ring[:, s * SLOT:(s + 1) * SLOT] for s in range(RING)]
        lat = early[:, 0:TB * LAT].rearrange("p (b n) -> p b n", b=TB)
        qlT = early[:, TB * LAT:TB * LAT + 2 * SEQ].rearrange("p (k t) -> p k t", k=2)
        kvT = early[:, TB * LAT + 2 * SEQ:TB * LAT + 3 * SEQ]
        tail = ring[:, MIX_SLOTS * SLOT:RING * SLOT]
        qk_tok = tail[:, 0:2 * TB * H * QK].rearrange("p (w b h n) -> p w b h n", w=2, b=TB, h=H)
        q_tok, k_tok = qk_tok[:, 0], qk_tok[:, 1]
        at = 2 * TB * H * QK
        v_tok = tail[:, at:at + TB * H * VD].rearrange("p (b h n) -> p b h n", b=TB, h=H)
        at += TB * H * VD
        qkT_flat = tail[:, at:at + 2 * H * SEQ]
        qkT = qkT_flat.rearrange("p (h w t) -> p h w t", h=H, w=2)
        squares = qkT_flat[:, 0:TB * H * QK].rearrange("p (b h n) -> p b h n", b=TB, h=H)
        probs = tail[:, 0:H * 3 * P].rearrange("p (h n) -> p h n", h=H)
        probsT = qkT_flat[:, 0:H * 3 * P].rearrange("p (h n) -> p h n", h=H)
        assert at + 2 * H * SEQ == 2 * SLOT

        N4 = PQ * SEQ

        def wk(i, n=1):
            return work[:, i * N4:(i + n) * N4]

        def quads(a):
            return a.rearrange("p (q t) -> p q t", q=PQ)

        tab_c = [quads(wk(0)), quads(wk(1))]
        tab_s = [quads(wk(2)), quads(wk(3))]
        st_re = [wk(4), wk(5)]
        st_im = [wk(6), wk(7)]
        turn_tmp = [quads(wk(8)), quads(wk(9))]
        dve_tmp = wk(9)
        pool_tmp = quads(wk(10))

        def sm(i, n=1):
            return small[:, i * PAIRS:(i + n) * PAIRS]

        small_names = ["step", "theta", "turns", "absr", "sin", "cos", "decay", "er", "n_re", "n_im", "den", "f_re",
                       "f_im", "t1", "t2", "w_c", "w_s", "w_c2", "w_s2", "w_t"]
        S = {n: sm(i) for i, n in enumerate(small_names)}

        def st(at, n):
            return stat[:, at:at + n]

        ssq, std, rstd = st(0, TB), st(2, TB), st(4, TB)
        lat_ssq, lat_std_v, lat_rstd = st(6, 4), st(10, 4), st(14, 4)
        kr_ssq, hd_ssq, hd_std, hd_rstd = st(18, TB), st(20, 32), st(52, 32), st(84, 32)
        eps, half_pi, zero = st(116, 1), st(117, 1), st(118, 1)
        row_max, neg_max, row_sum, row_inv = st(120, 16), st(136, 16), st(152, 16), st(168, 16)
        diag = early[:, 0:TB * P].rearrange("p (b t) -> p b t", b=TB)
        powers = attnT.rearrange("p k (q t) -> p k q t", q=PAIRS)
        glu_sigma = wk(9).rearrange("p (m t) -> p m t", m=S5M)
        ssmT = wk(8).rearrange("p (m t) -> p m t", m=S5M)
        mix_hi = work_hi[:, 0:2 * SLOT].rearrange("p (i n) -> p i n", i=2)
        attn_hi, ssm_hi = hT_hi[:, 0:4], hT_hi[:, 4:8]
        ssm_lo = work_hi[:, 8 * N4:9 * N4].rearrange("p (m t) -> p m t", m=S5M)
        mixed_lo, mixed_hi = mixed_parts[:, 0:KD], mixed_parts[:, KD:]
        gates_w = gates.rearrange("p (w m) t -> p w m t", w=2)
        def rv(i, dt=F32):
            v = rt[:, 16 * i:16 * i + 16]
            return (v.bitcast(dt) if dt is not F32 else v).rearrange("p (b e) -> p b e", b=TB)

        logits, top, top_i, top_f, sel, comb = rv(0), rv(1), rv(2, U32), rv(3), rv(4), rv(5)
        hot0, hot1, diff, ediff, den2, w_first, w_second = rv(6), rv(7), rv(8), rv(9), rv(10), rv(11), rv(12)
        N_ALL = 2 * E + 1
        place = rt[:, 208:208 + TB * N_ALL].rearrange("p (b e) -> p b e", b=TB)
        weight = rt[:, 256:256 + TB * N_ALL].rearrange("p (b e) -> p b e", b=TB)
        g_rows = st(200, KD)
        uq_loaded, consts_set = sig("uq_loaded", 16), sig("consts_set")
        slot_full = [sig(f"slot_full{s}") for s in range(RING)]
        x_loaded, consts_loaded, params_loaded = sig("x_loaded"), sig("consts_loaded"), sig("params_loaded", 16)
        router_loaded = sig("router_loaded")
        dve_chain, act_chain, pool_chain = sig("dve_chain"), sig("act_chain"), sig("pool_chain")
        x_ready, std_ready, diag_ready = (sig(n, 2 * TB) for n in ("x_ready", "std_ready", "diag_ready"))
        hT_in_psum, hT_act, hT_dve = sig("hT_in_psum", 8), sig("hT_act", 12), sig("hT_dve", 12)
        step_exp, theta_ready, trig_ready = sig("step_exp", 1), sig("theta_ready", 1), sig("trig_ready", 1)
        bbar_ready, bbarT_in_psum, bbarT_ready = sig("bbar_ready", 1), sig("bbarT_in_psum", 1), sig("bbarT_ready", 1)
        powers_ready, table_ready = sig("powers_ready", 1), sig("table_ready", S5M - 1)
        lat_in_psum, lat_biased, lat_std, lat_ready = (sig("lat_in_psum", TB), sig("lat_biased", 1),
                                                       sig("lat_std", 1), sig("lat_ready", 1))
        u_in_psum, u_ready = sig("u_in_psum", S5M), sig("u_ready", S5M)
        gate_in_psum, gate_ready = sig("gate_in_psum", 2 * KD), sig("gate_ready", 2 * KD)
        bu_in_psum, bu_read = sig("bu_in_psum", S5M), sig("bu_read", S5M)
        states_ready = sig("states_ready", S5M)
        y_in_psum, y_ready, gelu_ready = sig("y_in_psum", S5M), sig("y_ready", S5M), sig("gelu_ready", S5M)
        glu_in_psum, glu_sig, ssm_ready = sig("glu_in_psum", S5M), sig("glu_sig", S5M), sig("ssm_ready", S5M)
        latT_in_psum, latT_ready = sig("latT_in_psum", 2), sig("latT_ready", 3)
        qkv_in_psum, qkv_copied = sig("qkv_in_psum", 8), sig("qkv_copied", 8)
        head_sq, q_ssq = sig("head_sq", 2), sig("q_ssq", 1)
        head_ssq, head_std, qk_ready = sig("head_ssq", 1), sig("head_std", 1), sig("qk_ready", 1)
        qkT_in_psum, qkT_copied = sig("qkT_in_psum", H), sig("qkT_copied", H)
        scores_in_psum, max_ready = sig("scores_in_psum", H), sig("max_ready", H)
        exp_ready, probs_ready = sig("exp_ready", H), sig("probs_ready", H)
        probsT_in_psum, probsT_copied = sig("probsT_in_psum", H), sig("probsT_copied", H)
        av_in_psum, attn_ready = sig("av_in_psum", H // 2), sig("attn_ready", H // 2)
        proj_in_psum, mix_ready, mixed_in_psum = sig("proj_in_psum", KD), sig("mix_ready", KD), sig("mixed_in_psum", 4)
        ff_sig, ff_act, ff_hi_ready, ff_lo_ready = sig("ff_sig"), sig("ff_act"), sig("ff_hi_ready"), sig("ff_lo_ready")
        mix_w_hi, proj_w_lo, out0_w_lo, out1_w_lo = (sig("mix_w_hi", 4 * UNITS), sig("proj_w_lo", 2 * UNITS),
                                                     sig("out0_w_lo", UNITS), sig("out1_w_lo", UNITS))
        attn_hi_ready, attn_lo_ready, ssm_hi_ready, ssm_lo_ready = (
            sig(n, 4) for n in ("attn_hi_ready", "attn_lo_ready", "ssm_hi_ready", "ssm_lo_ready"))
        mixed, mixed_hi_ready = sig("mixed", KD), sig("mixed_hi_ready", KD)
        attn_projected = sig("attn_projected", 1)
        logits_in_psum, top_ready, top_exp, chosen = sig("logits_in_psum"), sig("top_ready"), sig("top_exp"), sig("chosen")
        places_in_psum, count_ready = sig("places_in_psum"), sig("count_ready")
        pick_ready, rows_in_psum = sig("pick_ready"), sig("rows_in_psum")
        spreadT_in_psum, spread_ready = sig("spreadT_in_psum"), sig("spread_ready")
        hi_ready, lo_ready, unit_used = sig("hi_ready"), sig("lo_ready"), sig("unit_used")
        rows_f_ready, rows_hi_ready, rows_lo_ready = sig("rows_f_ready"), sig("rows_hi_ready"), sig("rows_lo_ready")
        aT_hi_ready, aT_lo_ready = sig("aT_hi_ready"), sig("aT_lo_ready")
        ex_sig, ex_act = sig("ex_sig"), sig("ex_act")
        actT_in_psum = sig("actT_in_psum")
        y_rows_ready, y_rows_ready_dve = sig("y_rows_ready"), sig("y_rows_ready_dve")
        spread_in_psum, spread_added = sig("spread_in_psum"), sig("spread_added")
        out_ready, stored = sig("out_ready"), sig("stored")

        mix_use = {i: (i % MIX_SLOTS, i // MIX_SLOTS + 1) for i in range(N_MIX)}
        ffn_use = {i: (i % RING, i // RING + 1) for i in range(N_FFN)}
        per_slot_layer = [N_MIX // MIX_SLOTS * (s < MIX_SLOTS) + N_FFN // RING for s in range(RING)]
        before_moe = [per_slot_layer[s] + N_MIX // MIX_SLOTS * (s < MIX_SLOTS) for s in range(RING)]
        per_slot_pair = N_PAIR // RING

        def mix_landed(eng, l, i):
            s, k = mix_use[i]
            eng.wait_ge(slot_full[s].sem, l * (16 * per_slot_layer[s]) + 16 * k)

        def ffn_landed(eng, i):
            s, k = ffn_use[i]
            eng.wait_ge(slot_full[s].sem, 16 * (N_MIX // MIX_SLOTS * (s < MIX_SLOTS) + k))

        def moe_landed(eng, turn, i):
            s, k = i % RING, i // RING + 1
            eng.wait_ge(slot_full[s].sem, turn * (16 * per_slot_pair) + 16 * (before_moe[s] + k))

        assert (N_PAIR * UNITS) % UNIT_BUFS == 0

        def buf(n):
            return (N_FF_UNITS + n) % UNIT_BUFS

        def ff_unit(what, tile):
            c, f = tile // 4, tile % 4
            slot = slots[FFN_ITEMS.index((what, c)) % RING]
            width = min(4, FF_TILES - 4 * c) * P
            if what == "d":
                src = slot[:, f * D:(f + 1) * D]
            else:
                src = slot[:, 0:KD * width].rearrange("p (k n) -> p k n", k=KD)[:, :, f * P:(f + 1) * P]
            return FF_UNITS.index((what, tile)), src

        def unit(n):
            return ring[:, (n // UNITS % RING) * SLOT + n % UNITS * UNIT:][:, 0:UNIT]

        def item_unit(half, what, ch):
            return (half * N_EXP + MOE_ITEMS.index((what, ch))) * UNITS

        def per_pair(turn, n):
            return turn * (N_PAIR * UNITS) + (N_FF_UNITS + n)

        def ahead(eng, pair, turn, half, split):
            first = (half + 1) * N_EXP * UNITS
            if half == 0:
                for part in range(UNITS):
                    split(turn, first + part)
            else:
                with eng.If(pair < E // 2 - 1):
                    for part in range(UNITS):
                        split(turn, first + part)

        def slot_view(s, k, n):
            return slots[s][:, 0:k * n].rearrange("p (k n) -> p k n", k=k)

        def rows(w, k):
            return w.rearrange("(k p) n -> p k n", p=P)

        SPLIT_ITEMS = ["proj_a", "proj_s", "out0", "out1"]

        def mix_unit(what, part):
            i = SPLIT_ITEMS.index(what)
            at = slice(part * UNIT, (part + 1) * UNIT)
            slot = MIX_ITEMS.index(what) % MIX_SLOTS
            return i * UNITS + part, slots[slot][:, at], slot_lo[slot][:, at], mix_hi[:, i % 2, at]

        block = ctx.enter_context(nc.Block())

        @block.sync
        def _(sp):
            def layer_of(w, l):
                return w[bass.ds(l, 1)].rearrange("a r n -> (a r) n")

            def mixer_used(l, i):
                what = MIX_ITEMS[i]
                j = int(what[-1]) if what[-1].isdigit() else 0
                signal, n = {"lat": (lat_in_psum, TB), "u": (u_in_psum, S5M), "up": (qkv_in_psum, 8),
                             "gate": (gate_in_psum, 4 * j + 4), "glu": (glu_in_psum, S5M),
                             "proj_a": (attn_projected, 1), "proj_s": (proj_in_psum, KD),
                             "out": (mixed_in_psum, TB + j + 1)}[what.rstrip("0123456789")]
                sp.wait_ge(signal.sem, signal.at(l, n))

            def ffn_used(i):
                what, c = FFN_ITEMS[i]
                last = FF_UNITS.index((what, min(4 * c + 3, FF_TILES - 1)))
                sp.wait_ge(lo_ready.sem, last + 1)

            def expert_used(turn, i):
                sp.wait_ge(lo_ready.sem, per_pair(turn, UNITS * (i + 1)))

            def load_mixer(l, i):
                what, s = MIX_ITEMS[i], i % MIX_SLOTS
                if what in ("lat", "u") or what.startswith("gate"):
                    c0, n = {"lat": (0, LAT), "u": (LAT, S5W)}.get(what) or (LAT + S5W + 512 * int(what[-1]), 512)
                    dst, src = slot_view(s, KD, n), rows(layer_of(w_in, l)[:, c0:c0 + n], KD)
                elif what == "up":
                    sp.dma_start(slots[s][:, 0:2 * H * QK].rearrange("p (k n) -> p k n", k=2),
                                 rows(layer_of(w_uq, l), 2)).then_inc(uq_loaded.sem, 16)
                    dst, src = slots[s][:, 2048:2048 + 2 * 512], layer_of(w_ukv, l)
                elif what == "glu":
                    dst, src = slot_view(s, S5M, S5W), rows(layer_of(w_glu, l), S5M)
                elif what in ("proj_a", "proj_s"):
                    dst, src = slot_view(s, 4, D), rows(layer_of(w_pa if what == "proj_a" else w_ps, l), 4)
                else:
                    c0 = 512 * int(what[-1])
                    dst, src = slot_view(s, KD, 512), rows(layer_of(w_out, l)[:, c0:c0 + 512], KD)
                sp.dma_start(dst, src).then_inc(slot_full[s].sem, 16)

            def load_ffn(i):
                (what, c), s = FFN_ITEMS[i], i % RING
                n = min(512, FF - 512 * c)
                if what == "d":
                    dst, src = slot_view(s, n // P, D), rows(f_down[0, 512 * c:512 * c + n, :], n // P)
                else:
                    dst = slot_view(s, KD, n)
                    src = rows((f_gate if what == "g" else f_up)[0, :, 512 * c:512 * c + n], KD)
                sp.dma_start(dst, src).then_inc(slot_full[s].sem, 16)

            def load_expert(pair, i):
                half, (what, c), s = i // N_EXP, MOE_ITEMS[i % N_EXP], i % RING
                e = bass.ds(pair * 2 + half, 1)
                if what == "d":
                    dst, src = slot_view(s, 4, D), m_down[e, 512 * c:512 * c + 512, :]
                else:
                    dst, src = slot_view(s, KD, 512), (m_gate if what == "g" else m_up)[e, :, 512 * c:512 * c + 512]
                sp.dma_start(dst, src.rearrange("a (k p) n -> p (a k) n", p=P)).then_inc(slot_full[s].sem, 16)

            sp.dma_start(x, x_in.rearrange("(b p) d -> p b d", p=P)).then_inc(x_loaded.sem, 16)
            sp.dma_start(cst[:, :], consts).then_inc(consts_loaded.sem, 16)
            sp.dma_start(pl[:, :], params[0]).then_inc(params_loaded.sem, 16)
            for i in range(MIX_SLOTS):
                load_mixer(0, i)
            with sp.Fori(0, DEPTH) as l:
                for i in range(MIX_SLOTS, N_MIX):
                    mixer_used(l, i - MIX_SLOTS)
                    load_mixer(l, i)
                with sp.If(l < 1):
                    sp.wait_ge(attn_ready.sem, H // 2)
                    for i in range(N_FFN):
                        if i >= RING:
                            ffn_used(i - RING)
                        elif i < MIX_SLOTS:
                            mixer_used(0, N_MIX - MIX_SLOTS + i)
                        load_ffn(i)
                    for s in range(MIX_SLOTS):
                        ffn_used(N_FFN - RING + s)
                        load_mixer(1, s)
            sp.wait_ge(attn_ready.sem, DEPTH * (H // 2))
            for i in range(RING):
                if i < MIX_SLOTS:
                    mixer_used(1, N_MIX - MIX_SLOTS + i)
                load_expert(0, i)

            def experts(turn_0):
                def rest(pair):
                    for i in range(RING, N_PAIR):
                        expert_used(pair + turn_0, i - RING)
                        load_expert(pair, i)

                with sp.Fori(1, E // 2) as pair:
                    rest(pair - 1)
                    for i in range(RING):
                        expert_used(pair + (turn_0 - 1), N_PAIR - RING + i)
                        load_expert(pair, i)
                rest(E // 2 - 1)

            experts(0)
            sp.wait_ge(count_ready.sem, 1)
            most = sp.value_load(most_i[0:1, 0:1], min_val=0, max_val=SEQ)
            with sp.If(most > P):
                for i in range(RING):
                    expert_used(E // 2 - 1, N_PAIR - RING + i)
                    load_expert(0, i)
                experts(E // 2)
            sp.wait_ge(out_ready.sem, 1)
            sp.dma_start(out.rearrange("(b p) d -> p b d", p=P), x_out).then_inc(stored.sem, 16)
            sp.wait_ge(stored.sem, 16)

        @block.gpsimd
        def _(pool):
            g = nc.gpsimd
            c = Chain(pool, pool_chain.sem)
            low_c, low_s, high_c, high_s = (powers[:, i] for i in range(4))

            def over(v, n):
                return v.unsqueeze(2).broadcast_to([P, PAIRS, n])

            def doubled(tc, ts, n, wc, ws):
                t = pool_tmp.rearrange("p q (a b) -> p (q a) b", b=16)[:, 0:PAIRS, 0:n]
                new_c, new_s, old_c, old_s = tc[:, :, n:2 * n], ts[:, :, n:2 * n], tc[:, :, 0:n], ts[:, :, 0:n]
                c.add(g.tensor_tensor(new_c, old_c, over(wc, n), ALU.mult))
                c.link(g.tensor_tensor(t, old_s, over(ws, n), ALU.mult))
                c.add(g.tensor_tensor(new_c, new_c, t, ALU.subtract))
                c.link(g.tensor_tensor(new_s, old_s, over(wc, n), ALU.mult))
                c.link(g.tensor_tensor(t, old_c, over(ws, n), ALU.mult))
                c.link(g.tensor_tensor(new_s, new_s, t, ALU.add))

            def squared(wc, ws, out_c, out_s):
                c.add(g.tensor_tensor(out_c, wc, wc, ALU.mult))
                c.add(g.tensor_tensor(S["w_t"], ws, ws, ALU.mult))
                c.link(g.tensor_tensor(out_s, wc, ws, ALU.mult))
                c.add(g.tensor_tensor(out_c, out_c, S["w_t"], ALU.subtract))
                c.add(g.tensor_tensor(out_s, out_s, out_s, ALU.add))

            with pool.Fori(0, DEPTH) as l:
                c.start(l * POOL_MIX)
                pool.wait_ge(trig_ready.sem, trig_ready.at(l, 1))
                w = (S["cos"], S["sin"])
                spare = [(S["w_c"], S["w_s"]), (S["w_c2"], S["w_s2"])]
                squared(*w, *spare[0])
                for tc, ts in ((low_c, low_s), (high_c, high_s)):
                    c.add(g.memset(tc[:, :, 0:1], 1.0))
                    c.add(g.memset(ts[:, :, 0:1], 0.0))
                c.sync()
                for k in range(8):
                    tc, ts = (low_c, low_s) if k < 4 else (high_c, high_s)
                    doubled(tc, ts, 2 ** (k % 4), *w)
                    w = spare[k % 2]
                    if k < 6:
                        squared(*w, *spare[(k + 1) % 2])
                        c.sync()

                def table(m):
                    if m >= 2:
                        pool.wait_ge(states_ready.sem, states_ready.at(l, m - 1))
                    q = slice(PQ * m, PQ * m + PQ)
                    lo = [v[:, q].unsqueeze(2).broadcast_to([P, PQ, 16, 16]) for v in (low_c, low_s)]
                    hi = [v[:, q].unsqueeze(3).broadcast_to([P, PQ, 16, 16]) for v in (high_c, high_s)]
                    tc, ts, t = (v.rearrange("p q (a b) -> p q a b", b=16) for v in
                                 (tab_c[m % 2], tab_s[m % 2], pool_tmp))
                    c.add(g.tensor_tensor(tc, hi[0], lo[0], ALU.mult))
                    c.add(g.tensor_tensor(ts, hi[1], lo[0], ALU.mult))
                    c.link(g.tensor_tensor(t, hi[1], lo[1], ALU.mult))
                    c.link(g.tensor_tensor(tc, tc, t, ALU.subtract))
                    c.link(g.tensor_tensor(t, hi[0], lo[1], ALU.mult))
                    g.tensor_tensor(ts, ts, t, ALU.add).then_inc(table_ready.sem, 1)
                    pool.wait_ge(table_ready.sem, table_ready.at(l, m))

                pool.sem_inc(powers_ready.sem, 1)
                for m in range(1, S5M):
                    table(m)
                assert c.n == POOL_MIX, c.n
                for what in ("proj_a", "proj_s", "out0"):
                    for part in range(UNITS):
                        n, src, lo, hi = mix_unit(what, part)
                        pool.wait_ge(mix_w_hi.sem, mix_w_hi.at(l, n + 1))
                        g.tensor_tensor(lo, src, hi.bitcast(F32), ALU.subtract).then_inc(
                            (out0_w_lo if what == "out0" else proj_w_lo).sem, 1)

        @block.scalar
        def _(act):
            a = nc.scalar
            c = Chain(act, act_chain.sem)
            act.wait_ge(x_loaded.sem, 16)
            act.dma_start(router_sb, router[0].rearrange("(k p) e -> p k e", p=P)).then_inc(router_loaded.sem, 16)
            junk = [tail[:, D * i:D * (i + 1)] for i in range(4)]

            def norm(l, k):
                for b in range(TB):
                    act.wait_ge(x_ready.sem, x_ready.at(l, TB * k + b + 1))
                    c.link(a.activation((uT, attnT)[b].rearrange("p m t -> p (m t)"), x[:, b], ACT.Square,
                                        accum_out=ssq[:, b:b + 1]))
                    a.activation(std[:, b:b + 1], ssq[:, b:b + 1], ACT.Sqrt, scale=1.0 / D,
                                 bias=eps).then_inc(std_ready.sem, 1)

            def normed(l):
                for j in (0, 2):
                    act.wait_ge(hT_in_psum.sem, hT_in_psum.at(l, j + 1))
                    for i in range(2):
                        kt = 2 * j + i
                        a.activation(hT[:, kt], psum[:, 4 + j, i * SEQ:(i + 1) * SEQ], ACT.Copy,
                                     scale=field["g_mix"][:, kt:kt + 1]).then_inc(hT_act.sem, 1)

            def normed_split(l):
                for kt in range(KD):
                    j, i = kt // 2, kt % 2
                    act.wait_ge(hT_in_psum.sem, hT_in_psum.at(l, 4 + j + 1))
                    a.activation(hT_hi[:, kt], psum[:, 4 + j, i * SEQ:(i + 1) * SEQ], ACT.Copy,
                                 scale=field["g_ffn"][:, kt:kt + 1]).then_inc(hT_act.sem, 1)

            act.wait_ge(consts_set.sem, 3)
            with act.Fori(0, DEPTH) as l:
                c.start(l * ACT_MIX)
                norm(l, 0)
                act.wait_ge(params_loaded.sem, params_loaded.at(l, 16))
                a.activation(S["step"], field["log_step"], ACT.Exp).then_inc(step_exp.sem, 1)
                normed(l)
                act.wait_ge(theta_ready.sem, theta_ready.at(l, 1))
                a.activation(S["decay"], S["er"], ACT.Exp)
                a.activation(S["sin"], S["theta"], ACT.Sin, bias=zero)
                a.activation(S["cos"], S["absr"], ACT.Sin, scale=-1.0, bias=half_pi).then_inc(trig_ready.sem, 1)
                for m in range(S5M):
                    act.wait_ge(u_in_psum.sem, u_in_psum.at(l, m + 1))
                    a.activation(uT[:, m], psum[:, m, 0:SEQ], ACT.Identity,
                                 bias=field["b_u"][:, m:m + 1]).then_inc(u_ready.sem, 1)
                act.wait_ge(bbarT_in_psum.sem, bbarT_in_psum.at(l, 1))
                for j in range(2):
                    ins = a.activation(bT[:, 2 * j:2 * j + 2], psum[:, 6 + j].rearrange(
                        "p (m r s) -> p m r s", m=2, r=2), ACT.Copy)
                ins.then_inc(bbarT_ready.sem, 1)

                def gate(g):
                    act.wait_ge(gate_in_psum.sem, gate_in_psum.at(l, g + 1))
                    a.activation(gates[:, g], psum[:, 6 + g % 2, 0:SEQ], ACT.Sigmoid,
                                 bias=field["b_gate"][:, g:g + 1]).then_inc(gate_ready.sem, 1)

                def gelu(m):
                    act.wait_ge(y_ready.sem, y_ready.at(l, m + 1))
                    a.activation(uT[:, m], uT[:, m], ACT.Gelu_apprx_tanh).then_inc(gelu_ready.sem, 1)

                for g in range(2):
                    gate(g)
                act.wait_ge(lat_biased.sem, lat_biased.at(l, 1))
                for b in range(TB):
                    c.add(a.activation(junk[b][:, 0:QR], lat[:, b, 0:QR], ACT.Square, accum_out=lat_ssq[:, b:b + 1]))
                    c.add(a.activation(junk[2 + b][:, 0:KR], lat[:, b, QR:QR + KR], ACT.Square,
                                       accum_out=lat_ssq[:, 2 + b:3 + b]))
                c.sync()
                a.activation(lat_std_v[:, 0:2], lat_ssq[:, 0:2], ACT.Sqrt, scale=1.0 / QR, bias=eps)
                a.activation(lat_std_v[:, 2:4], lat_ssq[:, 2:4], ACT.Sqrt, scale=1.0 / KR,
                             bias=eps).then_inc(lat_std.sem, 1)
                for g in range(2, 4):
                    gate(g)
                act.wait_ge(latT_in_psum.sem, latT_in_psum.at(l, 1))
                for k in range(2):
                    a.activation(qlT[:, k], psum[:, 4, k * SEQ:(k + 1) * SEQ], ACT.Copy,
                                 scale=field["g_q"][:, k:k + 1]).then_inc(latT_ready.sem, 1)
                act.wait_ge(latT_in_psum.sem, latT_in_psum.at(l, 2))
                a.activation(kvT, psum[:, 5, 0:SEQ], ACT.Copy, scale=field["g_kv"][:, 0:1]).then_inc(latT_ready.sem, 1)

                gate(4)
                for n in range(8):
                    act.wait_ge(qkv_in_psum.sem, qkv_in_psum.at(l, n + 1))
                    b, half = n % 4 // 2, n % 2
                    heads = slice(4 * half, 4 * half + 4)
                    if n < 4:
                        ins = a.activation(q_tok[:, b, heads], psum[:, 4 + n % 2, 0:4 * QK].rearrange(
                            "p (h n) -> p h n", h=4), ACT.Copy)
                    else:
                        kv = psum[:, 4 + n % 2].rearrange("p (h n) -> p h n", h=4)
                        a.activation(k_tok[:, b, heads, 0:NOPE], kv[:, :, 0:NOPE], ACT.Copy)
                        ins = a.activation(v_tok[:, b, heads], kv[:, :, NOPE:], ACT.Copy)
                    ins.then_inc(qkv_copied.sem, 1)
                act.wait_ge(qkv_copied.sem, qkv_copied.at(l, 8))
                a.activation(squares, q_tok, ACT.Square).then_inc(head_sq.sem, 1)
                act.wait_ge(q_ssq.sem, q_ssq.at(l, 1))
                a.activation(squares[:, :, :, 0:NOPE], k_tok[:, :, :, 0:NOPE], ACT.Square).then_inc(head_sq.sem, 1)
                act.wait_ge(head_ssq.sem, head_ssq.at(l, 1))
                a.activation(hd_std, hd_ssq, ACT.Sqrt, scale=1.0 / QK, bias=eps).then_inc(head_std.sem, 1)
                for g in range(5, 16):
                    gate(g)
                gelu(0)
                gelu(1)
                for i, h in enumerate(HEADS):
                    act.wait_ge(qkT_in_psum.sem, qkT_in_psum.at(l, i + 1))
                    a.activation(qkT[0:QK, h], psum[0:QK, h].rearrange("p (w t) -> p w t", w=2),
                                 ACT.Copy).then_inc(qkT_copied.sem, 1)
                gelu(2)
                gelu(3)

                def split_mix(what, part):
                    n, src, _, hi = mix_unit(what, part)
                    if part == 0:
                        mix_landed(act, l, MIX_ITEMS.index(what))
                        signal, k = {"proj_a": (states_ready, S5M), "proj_s": (y_in_psum, S5M),
                                     "out0": (attn_projected, 1), "out1": (proj_in_psum, KD)}[what]
                        act.wait_ge(signal.sem, signal.at(l, k))
                    a.activation(hi, src, ACT.Copy).then_inc(mix_w_hi.sem, 1)

                for i in range(H + 3):
                    if i < H:
                        h = HEADS[i]
                        act.wait_ge(max_ready.sem, max_ready.at(l, i + 1))
                        a.activation(probs[:, h, 0:P], psum[:, h, 0:P], ACT.Exp, scale=SCALE,
                                     bias=neg_max[:, 2 * h:2 * h + 1], accum_out=row_sum[:, 2 * h:2 * h + 1])
                        a.activation(probs[:, h, P:3 * P], psum[:, h, P:3 * P], ACT.Exp, scale=SCALE,
                                     bias=neg_max[:, 2 * h + 1:2 * h + 2],
                                     accum_out=row_sum[:, 2 * h + 1:2 * h + 2]).then_inc(exp_ready.sem, 1)
                    if i >= 3:
                        h = HEADS[i - 3]
                        act.wait_ge(probsT_in_psum.sem, probsT_in_psum.at(l, i - 2))
                        a.activation(probsT[:, h], psum[:, h, 0:3 * P], ACT.Copy).then_inc(probsT_copied.sem, 1)
                    if 4 <= i:
                        split_mix("proj_a" if i < 8 else "proj_s", i % 4)
                split_mix("proj_s", 3)
                for i in range(H // 2):
                    j = HEADS[2 * i] // 2
                    act.wait_ge(attn_ready.sem, attn_ready.at(l, i + 1))
                    a.activation(attn_hi[:, j], attnT[:, j], ACT.Copy).then_inc(attn_hi_ready.sem, 1)
                for m in range(S5M):
                    act.wait_ge(glu_in_psum.sem, glu_in_psum.at(l, m + 1))
                    a.activation(glu_sigma[:, m], psum[:, 2 * m + 1, 0:SEQ], ACT.Sigmoid,
                                 bias=field["b_glu"][:, m:m + 1]).then_inc(glu_sig.sem, 1)
                for m in range(S5M):
                    act.wait_ge(ssm_ready.sem, ssm_ready.at(l, m + 1))
                    a.activation(ssm_hi[:, m], ssmT[:, m], ACT.Copy).then_inc(ssm_hi_ready.sem, 1)
                for part in range(UNITS):
                    split_mix("out0", part)
                for m in range(KD):
                    act.wait_ge(mixed.sem, mixed.at(l, m + 1))
                    a.activation(mixed_hi[:, m], gates[:, m], ACT.Copy).then_inc(mixed_hi_ready.sem, 1)
                for part in range(UNITS):
                    split_mix("out1", part)
                norm(l, 1)
                normed_split(l)
                assert c.n == ACT_MIX, c.n
                with act.If(l < 1):
                    act.wait_ge(hT_dve.sem, 12)
                    act.wait_ge(hT_act.sem, 12)
                    act.dma_start(pl[:, :], params[1]).then_inc(params_loaded.sem, 16)

                    def split(what, tile):
                        n, src = ff_unit(what, tile)
                        if tile % 4 == 0:
                            ffn_landed(act, FFN_ITEMS.index((what, tile // 4)))
                        act.wait_ge(unit_used.sem, n + 1)
                        dst = w_hi[:, n % UNIT_BUFS]
                        if what != "d":
                            dst = dst.rearrange("p (k n) -> p k n", k=KD)
                        a.activation(dst, src, ACT.Copy).then_inc(hi_ready.sem, 1)

                    for n in range(FF_TILES + 2):
                        if n < FF_TILES:
                            split("g", n)
                        if 1 <= n <= FF_TILES:
                            act.wait_ge(unit_used.sem, FF_UNITS.index(("g", n - 1)) + 1 + UNIT_BUFS)
                            if n >= 3:
                                act.wait_ge(ff_act.sem, n - 2)
                            a.activation(ff_sigma[:, (n - 1) % 2], psum[:, 4 + (n - 1) % 2, 0:SEQ],
                                         ACT.Sigmoid).then_inc(ff_sig.sem, 1)
                        if n < FF_TILES:
                            split("u", n)
                        if 1 <= n <= FF_TILES:
                            act.wait_ge(ff_act.sem, n)
                            a.activation(ff_hi[:, (n - 1) % 4], ff_a[:, (n - 1) % 2],
                                         ACT.Copy).then_inc(ff_hi_ready.sem, 1)
                        if n >= 2:
                            split("d", n - 2)

            def rows_split(n):
                act.wait_ge(rows_f_ready.sem, n)
                a.activation(rows_hi, rows_f, ACT.Copy).then_inc(rows_hi_ready.sem, 1)

            def split(turn, n):
                i, m = n // UNITS % N_PAIR, n % (N_PAIR * UNITS)
                if n % UNITS == 0:
                    moe_landed(act, turn + n // (N_PAIR * UNITS), i)
                act.wait_ge(unit_used.sem, per_pair(turn, n + 1))
                a.activation(w_hi[:, buf(m)], unit(m), ACT.Copy).then_inc(hi_ready.sem, 1)

            def experts(pair, turn):
                for half in range(2):
                    def at(per, n):
                        return turn * (2 * per) + (half * per + n)

                    def sigma(ch):
                        act.wait_ge(unit_used.sem, per_pair(turn, item_unit(half, "g", ch) + UNITS + UNIT_BUFS))
                        if ch >= 1 or half == 1:
                            act.wait_ge(ex_act.sem, at(FEC, ch))
                        a.activation(ex_sigma, psum[:, ch % 2], ACT.Sigmoid).then_inc(ex_sig.sem, 1)

                    def turned(ch):
                        act.wait_ge(actT_in_psum.sem, at(FEC, ch + 1))
                        a.activation(aT_hi[:, ch % 2], psum[:, 6], ACT.Copy).then_inc(aT_hi_ready.sem, 1)

                    for ch in range(FEC):
                        for part in range(UNITS):
                            if ch:
                                split(turn, item_unit(half, "g", ch) + part)
                            if ch == 1 and part == 1:
                                sigma(0)
                        for part in range(UNITS):
                            split(turn, item_unit(half, "u", ch) + part)
                            if ch and part == 2:
                                turned(ch - 1)
                        for part in range(UNITS if ch else 0):
                            split(turn, item_unit(half, "d", ch - 1) + part)
                            if part == 2:
                                sigma(ch)
                    for part in range(UNITS):
                        split(turn, item_unit(half, "d", FEC - 1) + part)
                        if part == 1:
                            turned(FEC - 1)
                            rows_split(at(1, 2))
                    ahead(act, pair, turn, half, split)
                    act.wait_ge(unit_used.sem, per_pair(turn, (half + 1) * N_EXP * UNITS + UNIT_BUFS))
                    a.activation(y_rows[:, 0:512], psum[:, 4], ACT.Copy).then_inc(y_rows_ready.sem, 1)

            for part in range(UNITS):
                split(0, part)
            act.wait_ge(top_ready.sem, 1)
            a.activation(ediff[:, :, 0:1], diff[:, :, 0:1], ACT.Exp).then_inc(top_exp.sem, 1)
            rows_split(1)
            with act.Fori(0, E // 2) as pair:
                experts(pair, pair)
            act.wait_ge(count_ready.sem, 1)
            most = act.value_load(most_i[0:1, 0:1], min_val=0, max_val=SEQ)
            with act.If(most > P):
                for part in range(UNITS):
                    split(E // 2, part)
                with act.Fori(0, E // 2) as pair:
                    experts(pair, pair + E // 2)

        @block.tensor
        def _(pe):
            t = nc.tensor

            pe.sem_inc(unit_used.sem, UNIT_BUFS)
            pe.wait_ge(consts_loaded.sem, 16)

            def norm_transposes(l, k):
                for b in range(TB):
                    pe.wait_ge(diag_ready.sem, diag_ready.at(l, TB * k + b + 1))
                    for kt in range(KD):
                        at = (kt % 2) * SEQ + b * P
                        ins = t.matmul(psum[:, 4 + kt // 2, at:at + P], x[:, b, kt * P:(kt + 1) * P], diag[:, b],
                                       start=True, stop=True)
                        if b == TB - 1 and kt % 2:
                            ins.then_inc(hT_in_psum.sem, 1)

            with pe.Fori(0, DEPTH) as l:
                norm_transposes(l, 0)
                mix_landed(pe, l, MIX_ITEMS.index("u"))
                w = slot_view(MIX_ITEMS.index("u"), KD, S5W)
                for m in range(S5M):
                    for kt in range(KD):
                        if m == 0:
                            signal = (hT_act, hT_dve)[kt // 2 % 2]
                            pe.wait_ge(signal.sem, signal.at(l, kt // 4 * 2 + kt % 2 + 1))
                        ins = t.matmul(psum[:, m, 0:SEQ], w[:, kt, m * P:(m + 1) * P], hT[:, kt],
                                       start=kt == 0, stop=kt == KD - 1)
                    ins.then_inc(u_in_psum.sem, 1)
                pe.wait_ge(bbar_ready.sem, bbar_ready.at(l, 1))
                for m in range(S5M):
                    for r, f in enumerate(("b_re", "b_im")):
                        at = (m % 2) * 2 * P + r * P
                        ins = t.transpose(psum[:, 6 + m // 2, at:at + P], field[f][:, m * P:(m + 1) * P], ident)
                ins.then_inc(bbarT_in_psum.sem, 1)

                def latents(b):
                    item = MIX_ITEMS.index("lat")
                    mix_landed(pe, l, item)
                    w = slot_view(item, KD, LAT)
                    for kt in range(KD):
                        ins = t.matmul(psum[:, 4 + b, 0:LAT], hT[:, kt, b * P:(b + 1) * P], w[:, kt],
                                       start=kt == 0, stop=kt == KD - 1)
                    ins.then_inc(lat_in_psum.sem, 1)

                def turn_latents():
                    pe.wait_ge(lat_ready.sem, lat_ready.at(l, 1))
                    for k in range(2):
                        for b in range(TB):
                            ins = t.transpose(psum[:, 4, k * SEQ + b * P:k * SEQ + (b + 1) * P],
                                              lat[:, b, k * P:(k + 1) * P], ident)
                    ins.then_inc(latT_in_psum.sem, 1)
                    for b in range(TB):
                        ins = t.transpose(psum[:, 5, b * P:(b + 1) * P], lat[:, b, QR:QR + KR], ident)
                    ins.then_inc(latT_in_psum.sem, 1)

                def input_states(m):
                    if m == 0:
                        pe.wait_ge(u_ready.sem, u_ready.at(l, S5M))
                        pe.wait_ge(bbarT_ready.sem, bbarT_ready.at(l, 1))
                    else:
                        pe.wait_ge(bu_read.sem, bu_read.at(l, m))
                    for r in range(2):
                        for q in range(PQ):
                            rows_q = slice(32 * q, 32 * q + 32)
                            ins = t.matmul(psum[:, q, r * SEQ:(r + 1) * SEQ], bT[rows_q, m, r],
                                           uT[rows_q, m], start=True, stop=True)
                    ins.then_inc(bu_in_psum.sem, 1)

                def read_out(m):
                    pe.wait_ge(states_ready.sem, states_ready.at(l, m + 1))
                    if m >= 2:
                        pe.wait_ge(y_ready.sem, y_ready.at(l, m - 1))
                    re, im = quads(st_re[m % 2]), quads(st_im[m % 2])
                    for q in range(PQ):
                        col = (PQ * m + q) * 32
                        o = psum[32 * q:32 * q + 32, 4 + m % 2, 0:SEQ]
                        t.matmul(o, field["c_re"][:, col:col + 32], re[:, q], start=True, stop=False)
                        ins = t.matmul(o, field["c_im"][:, col:col + 32], im[:, q], start=False, stop=True)
                    ins.then_inc(y_in_psum.sem, 1)

                def gate_products(j, which=range(4)):
                    item = MIX_ITEMS.index(f"gate{j}")
                    mix_landed(pe, l, item)
                    w = slot_view(item % MIX_SLOTS, KD, 512)
                    for i in which:
                        g = 4 * j + i
                        if g >= 2:
                            pe.wait_ge(gate_ready.sem, gate_ready.at(l, g - 1))
                        for kt in range(KD):
                            ins = t.matmul(psum[:, 6 + g % 2, 0:SEQ], w[:, kt, i * P:(i + 1) * P], hT[:, kt],
                                           start=kt == 0, stop=kt == KD - 1)
                        ins.then_inc(gate_in_psum.sem, 1)

                latents(0)
                input_states(0)
                latents(1)
                gate_products(0, range(0, 2))
                input_states(1)
                gate_products(0, range(2, 4))
                turn_latents()
                gate_products(1, range(0, 1))
                pe.wait_ge(latT_ready.sem, latT_ready.at(l, 3))
                item = MIX_ITEMS.index("up")
                mix_landed(pe, l, item)
                pe.wait_ge(uq_loaded.sem, uq_loaded.at(l, 16))
                s = item % MIX_SLOTS
                wq = slots[s][:, 0:2 * H * QK].rearrange("p (k n) -> p k n", k=2)
                for n in range(8):
                    b, half = n % 4 // 2, n % 2
                    if n >= 2:
                        pe.wait_ge(qkv_copied.sem, qkv_copied.at(l, n - 1))
                    if n < 4:
                        for k in range(2):
                            ins = t.matmul(psum[:, 4 + n % 2, 0:4 * QK], qlT[:, k, b * P:(b + 1) * P],
                                           wq[:, k, half * 4 * QK:(half + 1) * 4 * QK], start=k == 0, stop=k == 1)
                    else:
                        ins = t.matmul(psum[:, 4 + n % 2], kvT[:, b * P:(b + 1) * P],
                                       slots[s][:, 2048 + half * 512:2048 + half * 512 + 512], start=True, stop=True)
                    ins.then_inc(qkv_in_psum.sem, 1)
                gate_products(1, range(1, 2))
                pe.wait_ge(qkv_copied.sem, qkv_copied.at(l, 8))
                read_out(0)
                input_states(2)
                gate_products(1, range(2, 4))
                read_out(1)
                gate_products(2)
                input_states(3)
                gate_products(3)
                read_out(2)

                def turn_head(h):
                    for i, tok in enumerate((q_tok, k_tok)):
                        for b in range(TB):
                            ins = t.transpose(psum[0:QK, h, i * SEQ + b * P:i * SEQ + (b + 1) * P], tok[:, b, h],
                                              ident)
                    ins.then_inc(qkT_in_psum.sem, 1)

                pe.wait_ge(qk_ready.sem, qk_ready.at(l, 1))
                pe.wait_ge(bu_read.sem, bu_read.at(l, S5M))
                pe.wait_ge(gate_ready.sem, gate_ready.at(l, 2 * KD))
                for h in HEADS[:6]:
                    turn_head(h)
                read_out(3)
                pe.wait_ge(y_ready.sem, y_ready.at(l, S5M))
                for h in HEADS[6:]:
                    turn_head(h)
                for i, h in enumerate(HEADS):
                    pe.wait_ge(qkT_copied.sem, qkT_copied.at(l, i + 1))
                    o = psum[:, h]
                    t.matmul(o[:, 0:P], qkT[0:QK, h, 0, 0:P], qkT[0:QK, h, 1, 0:P], start=True, stop=False)
                    t.matmul(o[:, 0:P], ident, mask, start=False, stop=True)
                    t.matmul(o[:, P:3 * P], qkT[0:QK, h, 0, P:2 * P], qkT[0:QK, h, 1], start=True, stop=False)
                    t.matmul(o[:, 2 * P:3 * P], ident, mask, start=False, stop=True).then_inc(scores_in_psum.sem, 1)

                def values_of(i):
                    j = HEADS[2 * i] // 2
                    pe.wait_ge(probsT_copied.sem, probsT_copied.at(l, 2 * i + 2))
                    for k in range(2):
                        h = 2 * j + k
                        o = psum[VD * k:VD * k + VD, 2 * j]
                        t.matmul(o[:, 0:P], v_tok[:, 0, h], probsT[:, h, 0:P], start=True, stop=True)
                        t.matmul(o[:, P:2 * P], v_tok[:, 0, h], probsT[:, h, P:2 * P], start=True, stop=False)
                        ins = t.matmul(o[:, P:2 * P], v_tok[:, 1, h], probsT[:, h, 2 * P:3 * P],
                                       start=False, stop=True)
                    ins.then_inc(av_in_psum.sem, 1)

                for i, h in enumerate(HEADS):
                    pe.wait_ge(probs_ready.sem, probs_ready.at(l, i + 1))
                    for k in range(3):
                        ins = t.transpose(psum[:, h, k * P:(k + 1) * P], probs[:, h, k * P:(k + 1) * P], ident)
                    ins.then_inc(probsT_in_psum.sem, 1)
                    if i >= 3 and i % 2:
                        values_of(i // 2 - 1)
                values_of(H // 2 - 1)
                item = MIX_ITEMS.index("glu")
                mix_landed(pe, l, item)
                pe.wait_ge(gelu_ready.sem, gelu_ready.at(l, S5M))
                w = slot_view(item % MIX_SLOTS, S5M, S5W)
                for m in range(S5M):
                    for kt in range(S5M):
                        ins = t.matmul(psum[:, 2 * m + 1, 0:SEQ], w[:, kt, m * P:(m + 1) * P], uT[:, kt],
                                       start=kt == 0, stop=kt == S5M - 1)
                    ins.then_inc(glu_in_psum.sem, 1)
                pe.wait_ge(glu_sig.sem, glu_sig.at(l, S5M))
                for i, (what, hi, lo, signal) in enumerate((("proj_a", attn_hi, attn_lo, attn_lo_ready),
                                                            ("proj_s", ssm_hi, ssm_lo, ssm_lo_ready))):
                    pe.wait_ge(signal.sem, signal.at(l, 4))
                    for m in range(KD):
                        o = psum[:, m, i * SEQ:(i + 1) * SEQ]
                        for kt in range(4):
                            if m == 0:
                                pe.wait_ge(proj_w_lo.sem, proj_w_lo.at(l, i * UNITS + kt + 1))
                            _, _, wl, wh = mix_unit(what, kt)
                            at_w = slice(m * P, (m + 1) * P)
                            t.matmul(o, wh[:, at_w], hi[:, kt], start=kt == 0, stop=False)
                            t.matmul(o, wh[:, at_w], lo[:, kt], start=False, stop=False)
                            ins = t.matmul(o, wl[:, at_w], hi[:, kt], start=False, stop=kt == 3)
                        if i:
                            ins.then_inc(proj_in_psum.sem, 1)
                    if i == 0:
                        ins.then_inc(attn_projected.sem, 1)
                for b in range(TB):
                    for c in range(2):
                        signal = (out0_w_lo, out1_w_lo)[c]
                        for kt in range(KD):
                            if b == 0:
                                pe.wait_ge(signal.sem, signal.at(l, kt // 2 + 1))
                                if c == 0:
                                    pe.wait_ge(mix_ready.sem, mix_ready.at(l, kt + 1))
                            _, _, wl, wh = mix_unit(f"out{c}", kt // 2)
                            at_w = slice(kt % 2 * 512, kt % 2 * 512 + 512)
                            hi, lo = (v[:, kt, b * P:(b + 1) * P] for v in (mixed_hi, mixed_lo))
                            o = psum[:, 2 * b + c]
                            t.matmul(o, hi, wh[:, at_w], start=kt == 0, stop=False)
                            t.matmul(o, hi, wl[:, at_w], start=False, stop=False)
                            ins = t.matmul(o, lo, wh[:, at_w], start=False, stop=kt == KD - 1)
                        ins.then_inc(mixed_in_psum.sem, 1)
                norm_transposes(l, 1)
                with pe.If(l < 1):
                    def pair_of(what, tile):
                        n, _ = ff_unit(what, tile)
                        pe.wait_ge(lo_ready.sem, n + 1)
                        return w_hi[:, n % UNIT_BUFS], w_lo[:, n % UNIT_BUFS]

                    for n in range(FF_TILES + 2):
                        if n < FF_TILES:
                            if n >= 2:
                                pe.wait_ge(ff_act.sem, n - 1)
                            for i, what in enumerate("gu"):
                                wh, wl = pair_of(what, n)
                                o = psum[:, 4 + 2 * i + n % 2, 0:SEQ]
                                for kt in range(KD):
                                    if n == 0 and what == "g":
                                        pe.wait_ge(hT_dve.sem, 4 + kt // 2 * 2 + 2)
                                    at_w = slice(kt * P, (kt + 1) * P)
                                    t.matmul(o, wh[:, at_w], hT_hi[:, kt], start=kt == 0, stop=False)
                                    t.matmul(o, wh[:, at_w], hT_lo[:, kt], start=False, stop=False)
                                    ins = t.matmul(o, wl[:, at_w], hT_hi[:, kt], start=False, stop=kt == KD - 1)
                                ins.then_inc(unit_used.sem, 1)
                        if n >= 2:
                            m = n - 2
                            wh, wl = pair_of("d", m)
                            pe.wait_ge(ff_lo_ready.sem, m + 1)
                            for b in range(TB):
                                ah, al = (a[:, m % 4, b * P:(b + 1) * P] for a in (ff_hi, ff_lo))
                                for a, w in ((ah, wh), (ah, wl), (al, wh)):
                                    for j in range(2):
                                        ins = t.matmul(psum[:, 2 * b + j], a, w[:, 512 * j:512 * j + 512],
                                                       start=m == 0 and a is ah and w is wh,
                                                       stop=m == FF_TILES - 1 and a is al)
                            ins.then_inc(unit_used.sem, 1)

            pe.wait_ge(router_loaded.sem, 16)
            pe.wait_ge(hT_dve.sem, hT_dve.at(1, 12))
            for b in range(TB):
                for i, part in enumerate((hT_hi, hT_lo)):
                    for kt in range(KD):
                        ins = t.matmul(psum[:, 4, b * E:(b + 1) * E], part[:, kt, b * P:(b + 1) * P].bitcast(F32),
                                       router_sb[:, kt], start=i + kt == 0, stop=i == 1 and kt == KD - 1)
            ins.then_inc(logits_in_psum.sem, 1)
            pe.wait_ge(chosen.sem, 1)
            before, ones = const["before"], const["ones"]
            t.matmul(psum[:, 5, 0:E], before, sel[:, 0], start=True, stop=True)
            t.matmul(psum[:, 5, E:2 * E], before, sel[:, 1], start=True, stop=False)
            t.matmul(psum[:, 5, E:2 * E], ones, sel[:, 0], start=False, stop=True)
            t.matmul(psum[:, 5, 2 * E:3 * E], ones, sel[:, 0], start=True, stop=False)
            t.matmul(psum[:, 5, 2 * E:3 * E], ones, sel[:, 1], start=False, stop=True).then_inc(places_in_psum.sem, 1)

            def gather(n):
                pe.wait_ge(pick_ready.sem, n)
                for kt in range(KD):
                    for b in range(TB):
                        ins = t.matmul(psum[:, 1 + 2 * (kt // 4), (kt % 4) * P:(kt % 4 + 1) * P],
                                       x[:, b, kt * P:(kt + 1) * P], pick[:, b], start=b == 0, stop=b == TB - 1)
                    if kt % 4 == 3:
                        ins.then_inc(rows_in_psum.sem, 1)

            gather(1)

            def experts(turn):
                for half in range(2):
                    def at(per, n):
                        return turn * (2 * per) + (half * per + n)

                    def units(what, ch, steps, products):
                        first = item_unit(half, what, ch)
                        for part in range(UNITS):
                            n = first + part
                            pe.wait_ge(lo_ready.sem, per_pair(turn, n + 1))
                            wh, wl = w_hi[:, buf(n)], w_lo[:, buf(n)]
                            for k in range(part * steps, (part + 1) * steps):
                                ins = products(k, k - part * steps, wh, wl)
                            ins.then_inc(unit_used.sem, 1)

                    def product(what, ch):
                        bank = ch % 2 + (2 if what == "u" else 0)
                        o = psum[:, bank]

                        def step(k, i, wh, wl):
                            at_w = slice(512 * i, 512 * i + 512)
                            t.matmul(o, rows_hi[:, k], wh[:, at_w], start=k == 0, stop=False)
                            t.matmul(o, rows_hi[:, k], wl[:, at_w], start=False, stop=False)
                            return t.matmul(o, rows_lo[:, k], wh[:, at_w], start=False, stop=k == KD - 1)

                        units(what, ch, KD // UNITS, step)

                    def turn_act(ch):
                        pe.wait_ge(ex_act.sem, at(FEC, ch + 1))
                        for k in range(4):
                            ins = t.transpose(psum[:, 6, k * P:(k + 1) * P], ex_a[:, ch % 2, k * P:(k + 1) * P],
                                              ident)
                        ins.then_inc(actT_in_psum.sem, 1)

                    def down(ch):
                        pe.wait_ge(aT_lo_ready.sem, at(FEC, ch + 1))

                        def step(k, i, wh, wl):
                            ah, al = (a[:, ch % 2, k * P:(k + 1) * P] for a in (aT_hi, aT_lo))
                            first, last = ch == 0 and k == 0, ch == FEC - 1 and k == 3
                            for j in range(2):
                                at_w = slice(D * i + 512 * j, D * i + 512 * j + 512)
                                t.matmul(psum[:, 4 + j], ah, wh[:, at_w], start=first, stop=False)
                                t.matmul(psum[:, 4 + j], ah, wl[:, at_w], start=False, stop=False)
                            for j in range(2):
                                at_w = slice(D * i + 512 * j, D * i + 512 * j + 512)
                                ins = t.matmul(psum[:, 4 + j], al, wh[:, at_w], start=False, stop=last)
                            return ins

                        units("d", ch, 4 // UNITS, step)

                    pe.wait_ge(rows_lo_ready.sem, at(1, 1))
                    for ch in range(FEC):
                        product("g", ch)
                        if ch:
                            turn_act(ch - 1)
                        product("u", ch)
                        if ch == 1:
                            for b in range(TB):
                                ins = t.transpose(psum[:, 7, b * P:(b + 1) * P], spread_tok[:, b], ident)
                            ins.then_inc(spreadT_in_psum.sem, 1)
                        if ch:
                            down(ch - 1)
                    turn_act(FEC - 1)
                    gather(at(1, 2))
                    down(FEC - 1)
                    pe.wait_ge(spread_ready.sem, at(1, 1))
                    pe.wait_ge(y_rows_ready.sem, at(1, 1))
                    for n in range(4):
                        if n == 1:
                            pe.wait_ge(y_rows_ready_dve.sem, at(1, 1))
                        if n >= 2:
                            pe.wait_ge(spread_added.sem, at(4, n - 1))
                        b, j = n // 2, n % 2
                        t.matmul(psum[:, 7 - n % 2], spread[:, b], y_rows[:, 512 * j:512 * j + 512],
                                 start=True, stop=True).then_inc(spread_in_psum.sem, 1)

            with pe.Fori(0, E // 2) as pair:
                experts(pair)
            pe.wait_ge(count_ready.sem, 1)
            most = pe.value_load(most_i[0:1, 0:1], min_val=0, max_val=SEQ)
            with pe.If(most > P):
                with pe.Fori(0, E // 2) as pair:
                    experts(pair + E // 2)

        @block.vector
        def _(dve):
            v = nc.vector
            c = Chain(dve, dve_chain.sem)

            def tt(o, a, b, op):
                return v.tensor_tensor(o, a, b, op)

            def row(f, n, shape):
                return field[f][:, 0:n].unsqueeze(1).broadcast_to(shape)

            def norm(l, k):
                for b in range(TB):
                    dve.wait_ge(std_ready.sem, std_ready.at(l, TB * k + b + 1))
                    c.link(v.reciprocal(rstd[:, b:b + 1], std[:, b:b + 1]))
                    v.tensor_scalar(diag[:, b], ident, rstd[:, b:b + 1], None, ALU.mult).then_inc(diag_ready.sem, 1)

            def normed(l):
                for j in (1, 3):
                    dve.wait_ge(hT_in_psum.sem, hT_in_psum.at(l, j + 1))
                    for i in range(2):
                        kt = 2 * j + i
                        v.tensor_scalar(hT[:, kt], psum[:, 4 + j, i * SEQ:(i + 1) * SEQ], field["g_mix"][:, kt:kt + 1],
                                        None, ALU.mult).then_inc(hT_dve.sem, 1)

            def normed_split(l):
                for j in range(4):
                    dve.wait_ge(hT_act.sem, hT_act.at(l, 4 + 2 * j + 2))
                    for i in range(2):
                        kt = 2 * j + i
                        v.scalar_tensor_tensor(hT_lo[:, kt], psum[:, 4 + j, i * SEQ:(i + 1) * SEQ],
                                               field["g_ffn"][:, kt:kt + 1], hT_hi[:, kt].bitcast(F32),
                                               ALU.mult, ALU.subtract).then_inc(hT_dve.sem, 1)

            v.memset(eps, EPS).then_inc(consts_set.sem, 1)
            v.memset(half_pi, float(np.pi / 2)).then_inc(consts_set.sem, 1)
            v.memset(zero, 0.0).then_inc(consts_set.sem, 1)
            dve.wait_ge(x_loaded.sem, 16)
            dve.sem_inc(x_ready.sem, TB)
            dve.wait_ge(consts_loaded.sem, 16)
            with dve.Fori(0, DEPTH) as l:
                c.start(l * (DVE_MIX + DVE_FFN))
                norm(l, 0)
                dve.wait_ge(step_exp.sem, step_exp.at(l, 1))
                c.add(tt(S["er"], field["lam_re"], S["step"], ALU.mult))
                c.link(tt(S["theta"], field["lam_im"], S["step"], ALU.mult))
                c.link(v.tensor_scalar(S["turns"], S["theta"], float(1 / (2 * np.pi)), MAGIC, ALU.mult, ALU.add))
                c.link(v.tensor_scalar(S["turns"], S["turns"], MAGIC, None, ALU.subtract))
                for part in (PI2_A, PI2_B, PI2_C):
                    c.link(v.scalar_tensor_tensor(S["theta"], S["turns"], -part, S["theta"], ALU.mult, ALU.add))
                c.link(v.tensor_scalar(S["theta"], S["theta"], float(np.float32(3.1415925)), -float(np.float32(3.1415925)),
                                       ALU.min, ALU.max))
                c.link(v.tensor_scalar(S["t1"], S["theta"], -1.0, None, ALU.mult))
                tt(S["absr"], S["theta"], S["t1"], ALU.max).then_inc(theta_ready.sem, 1)
                normed(l)
                dve.wait_ge(trig_ready.sem, trig_ready.at(l, 1))
                c.add(tt(S["n_re"], S["decay"], S["cos"], ALU.mult))
                c.add(tt(S["n_im"], S["decay"], S["sin"], ALU.mult))
                c.add(tt(S["den"], field["lam_re"], field["lam_re"], ALU.mult))
                c.link(tt(S["t1"], field["lam_im"], field["lam_im"], ALU.mult))
                c.add(v.tensor_scalar(S["n_re"], S["n_re"], 1.0, None, ALU.subtract))
                c.link(tt(S["den"], S["den"], S["t1"], ALU.add))
                c.add(v.reciprocal(S["den"], S["den"]))
                c.add(tt(S["f_re"], S["n_re"], field["lam_re"], ALU.mult))
                c.add(tt(S["t1"], S["n_im"], field["lam_im"], ALU.mult))
                c.add(tt(S["f_im"], S["n_im"], field["lam_re"], ALU.mult))
                c.link(tt(S["t2"], S["n_re"], field["lam_im"], ALU.mult))
                c.add(tt(S["f_re"], S["f_re"], S["t1"], ALU.add))
                c.link(tt(S["f_im"], S["f_im"], S["t2"], ALU.subtract))
                c.add(tt(S["f_re"], S["f_re"], S["den"], ALU.mult))
                c.link(tt(S["f_im"], S["f_im"], S["den"], ALU.mult))
                b_re, b_im = (field[f].rearrange("p (q n) -> p q n", q=PAIRS) for f in ("b_re", "b_im"))
                f_re, f_im = (S[f].unsqueeze(2).broadcast_to([P, PAIRS, 32]) for f in ("f_re", "f_im"))
                tmp = [dve_tmp[:, 512 * i:512 * i + 512].rearrange("p (q n) -> p q n", q=PAIRS) for i in range(2)]
                c.add(tt(tmp[0], b_im, f_im, ALU.mult))
                c.link(tt(tmp[1], b_re, f_im, ALU.mult))
                c.add(tt(b_re, b_re, f_re, ALU.mult))
                c.link(tt(b_im, b_im, f_re, ALU.mult))
                c.add(tt(b_re, b_re, tmp[0], ALU.subtract))
                tt(b_im, b_im, tmp[1], ALU.add).then_inc(bbar_ready.sem, 1)
                c.add(v.tensor_scalar(field["c_im"], field["c_im"], -1.0, None, ALU.mult))
                dve.wait_ge(bbar_ready.sem, bbar_ready.at(l, 1))
                c.sync()
                dve.wait_ge(powers_ready.sem, powers_ready.at(l, 1))
                lo = [powers[:, i, 0:PQ].unsqueeze(2).broadcast_to([P, PQ, 16, 16]) for i in (0, 1)]
                hi = [powers[:, i, 0:PQ].unsqueeze(3).broadcast_to([P, PQ, 16, 16]) for i in (2, 3)]
                tc, ts, tmp = (w.rearrange("p q (a b) -> p q a b", b=16) for w in (tab_c[0], tab_s[0], quads(dve_tmp)))
                c.add(tt(tc, hi[0], lo[0], ALU.mult))
                c.add(tt(ts, hi[1], lo[0], ALU.mult))
                c.link(tt(tmp, hi[1], lo[1], ALU.mult))
                c.link(tt(tc, tc, tmp, ALU.subtract))
                c.link(tt(tmp, hi[0], lo[1], ALU.mult))
                c.link(tt(ts, ts, tmp, ALU.add))

                def states(m):
                    i = m % 2
                    dve.wait_ge(bu_in_psum.sem, bu_in_psum.at(l, m + 1))
                    if m:
                        dve.wait_ge(table_ready.sem, table_ready.at(l, m))
                    if m >= 2:
                        dve.wait_ge(y_in_psum.sem, y_in_psum.at(l, m - 1))
                    bu_re, bu_im = psum[:, 0:PQ, 0:SEQ], psum[:, 0:PQ, SEQ:2 * SEQ]
                    re, im, tmp = quads(st_re[i]), quads(st_im[i]), quads(dve_tmp)
                    if m:
                        dve.wait_ge(states_ready.sem, states_ready.at(l, m))
                    c.add(tt(re, bu_re, tab_c[i], ALU.mult))
                    c.add(tt(im, bu_im, tab_c[i], ALU.mult))
                    c.link(tt(tmp, bu_im, tab_s[i], ALU.mult))
                    c.link(tt(re, re, tmp, ALU.add))
                    tt(tmp, bu_re, tab_s[i], ALU.mult).then_inc(bu_read.sem, 1)
                    dve.wait_ge(bu_read.sem, bu_read.at(l, m + 1))
                    c.link(tt(im, im, tmp, ALU.subtract))
                    for s in (re, im):
                        for q in range(PQ):
                            decay = S["decay"][:, PQ * m + q:PQ * m + q + 1].broadcast_to([P, SEQ])
                            ins = v.tensor_tensor_scan(s[:, q], decay, s[:, q], 0.0, ALU.mult, ALU.add)
                            c.add(ins)
                    c.sync()
                    t_re, t_im = turn_tmp
                    c.add(tt(t_re, im, tab_s[i], ALU.mult))
                    c.link(tt(t_im, re, tab_s[i], ALU.mult))
                    c.add(tt(re, re, tab_c[i], ALU.mult))
                    c.link(tt(im, im, tab_c[i], ALU.mult))
                    tt(re, re, t_re, ALU.subtract)
                    tt(im, im, t_im, ALU.add).then_inc(states_ready.sem, 1)

                def skip(m):
                    dve.wait_ge(y_in_psum.sem, y_in_psum.at(l, m + 1))
                    v.scalar_tensor_tensor(uT[:, m], uT[:, m], field["s5_d"][:, m:m + 1], psum[:, 4 + m % 2, 0:SEQ],
                                           ALU.mult, ALU.add).then_inc(y_ready.sem, 1)

                states(0)
                for b in range(TB):
                    dve.wait_ge(lat_in_psum.sem, lat_in_psum.at(l, b + 1))
                    ins = tt(lat[:, b], psum[:, 4 + b, 0:LAT], field["b_lat"], ALU.add)
                    if b == 0:
                        c.add(ins)
                ins.then_inc(lat_biased.sem, 1)
                dve.wait_ge(lat_std.sem, lat_std.at(l, 1))
                dve.wait_ge(lat_biased.sem, lat_biased.at(l, 1))
                c.link(v.reciprocal(lat_rstd, lat_std_v))
                for b in range(TB):
                    c.add(v.tensor_scalar(lat[:, b, 0:QR], lat[:, b, 0:QR], lat_rstd[:, b:b + 1], None, ALU.mult))
                    ins = v.tensor_scalar(lat[:, b, QR:QR + KR], lat[:, b, QR:QR + KR], lat_rstd[:, 2 + b:3 + b],
                                          None, ALU.mult)
                    if b == 0:
                        c.add(ins)
                ins.then_inc(lat_ready.sem, 1)
                states(1)
                cos, sin = (const[f].rearrange("p (b n) -> p b n", b=TB) for f in ("cos", "sin"))
                kr = lat[:, :, QR + KR:LAT]
                flat = qkT_flat[:, 2048:2048 + 16 * 32]
                kg = flat[:, 0:TB * ROPE].rearrange("p (b n) -> p b n", b=TB)
                kt = flat[:, 64:64 + TB * ROPE].rearrange("p (b n) -> p b n", b=TB)
                krt = flat[:, 128:128 + TB * ROPE].rearrange("p (b n) -> p b n", b=TB)
                c.add(tt(kg, kr, row("g_kh", QK, [P, TB, QK])[:, :, NOPE:], ALU.mult))
                c.link(tt(kt, kr, kr, ALU.mult))
                c.link(v.tensor_reduce(kr_ssq, kt, AX_X, ALU.add))

                def rope(o, a, cos, sin, tmp):
                    a1, a2 = a[..., 0:HALF], a[..., HALF:]
                    c.add(tt(tmp[0], a1, cos, ALU.mult))
                    c.add(tt(tmp[1], a2, sin, ALU.mult))
                    c.add(tt(tmp[2], a2, cos, ALU.mult))
                    c.link(tt(tmp[3], a1, sin, ALU.mult))
                    c.add(tt(o[..., 0:HALF], tmp[0], tmp[1], ALU.subtract))
                    return tt(o[..., HALF:], tmp[2], tmp[3], ALU.add)

                t4 = [flat[:, 192 + 32 * i:224 + 32 * i].rearrange("p (b n) -> p b n", b=TB) for i in range(4)]
                c.link(rope(krt, kg, cos, sin, t4))
                dve.wait_ge(qkv_copied.sem, qkv_copied.at(l, 8))
                flat_h = squares.rearrange("p b h n -> p (b h) n")
                qf, kf = (w.rearrange("p b h n -> p (b h) n") for w in (q_tok, k_tok))
                dve.wait_ge(head_sq.sem, head_sq.at(l, 1))
                v.tensor_reduce(hd_ssq[:, 0:16], flat_h, AX_X, ALU.add).then_inc(q_ssq.sem, 1)
                dve.wait_ge(head_sq.sem, head_sq.at(l, 2))
                c.link(v.tensor_reduce(hd_ssq[:, 16:32], flat_h[:, :, 0:NOPE], AX_X, ALU.add))
                k_ssq = hd_ssq[:, 16:32].rearrange("p (b h) -> p b h", b=TB)
                tt(k_ssq, k_ssq, kr_ssq.unsqueeze(2).broadcast_to([P, TB, H]), ALU.add).then_inc(head_ssq.sem, 1)
                dve.wait_ge(head_std.sem, head_std.at(l, 1))
                c.link(v.reciprocal(hd_rstd, hd_std))
                rq = hd_rstd[:, 0:16].unsqueeze(2)
                rk = hd_rstd[:, 16:32].unsqueeze(2)
                c.add(tt(qf, qf, rq.broadcast_to([P, TB * H, QK]), ALU.mult))
                c.add(tt(kf[:, :, 0:NOPE], kf[:, :, 0:NOPE], rk.broadcast_to([P, TB * H, NOPE]), ALU.mult))
                rkb = hd_rstd[:, 16:32].rearrange("p (b h) -> p b h", b=TB).unsqueeze(3)
                c.link(tt(k_tok[:, :, :, NOPE:], krt.unsqueeze(2).broadcast_to([P, TB, H, ROPE]),
                          rkb.broadcast_to([P, TB, H, ROPE]), ALU.mult))
                c.add(tt(kf[:, :, 0:NOPE], kf[:, :, 0:NOPE], row("g_kh", NOPE, [P, TB * H, NOPE]), ALU.mult))
                c.link(tt(qf, qf, row("g_qh", QK, [P, TB * H, QK]), ALU.mult))
                cos_h, sin_h = (w.unsqueeze(2).broadcast_to([P, TB, H, HALF]) for w in (cos, sin))
                t4 = [qkT_flat[:, 256 * i:256 * i + 256].rearrange("p (b h n) -> p b h n", b=TB, h=H)
                      for i in range(4)]
                rope(q_tok[:, :, :, NOPE:], q_tok[:, :, :, NOPE:], cos_h, sin_h, t4).then_inc(qk_ready.sem, 1)
                for m in range(2, S5M):
                    states(m)
                    skip(m - 2)
                skip(2)
                skip(3)
                for i in range(H + 2):
                    if i < H:
                        h = HEADS[i]
                        dve.wait_ge(scores_in_psum.sem, scores_in_psum.at(l, i + 1))
                        c.add(v.tensor_reduce(row_max[:, 2 * h:2 * h + 1], psum[:, h, 0:P], AX_X, ALU.max))
                        c.link(v.tensor_reduce(row_max[:, 2 * h + 1:2 * h + 2], psum[:, h, P:3 * P], AX_X, ALU.max))
                        v.tensor_scalar(neg_max[:, 2 * h:2 * h + 2], row_max[:, 2 * h:2 * h + 2], -SCALE, None,
                                        ALU.mult).then_inc(max_ready.sem, 1)
                    if i >= 2:
                        h = HEADS[i - 2]
                        dve.wait_ge(exp_ready.sem, exp_ready.at(l, i - 1))
                        c.link(v.reciprocal(row_inv[:, 2 * h:2 * h + 2], row_sum[:, 2 * h:2 * h + 2]))
                        c.add(v.tensor_scalar(probs[:, h, 0:P], probs[:, h, 0:P], row_inv[:, 2 * h:2 * h + 1], None,
                                              ALU.mult))
                        v.tensor_scalar(probs[:, h, P:3 * P], probs[:, h, P:3 * P], row_inv[:, 2 * h + 1:2 * h + 2],
                                        None, ALU.mult).then_inc(probs_ready.sem, 1)
                for i in range(H // 2):
                    j = HEADS[2 * i] // 2
                    dve.wait_ge(av_in_psum.sem, av_in_psum.at(l, i + 1))
                    v.tensor_copy(attnT[:, j], psum[:, 2 * j, 0:SEQ]).then_inc(attn_ready.sem, 1)
                for i in range(H // 2):
                    j = HEADS[2 * i] // 2
                    dve.wait_ge(attn_hi_ready.sem, attn_hi_ready.at(l, i + 1))
                    tt(attn_lo[:, j], attnT[:, j], attn_hi[:, j].bitcast(F32), ALU.subtract).then_inc(
                        attn_lo_ready.sem, 1)
                for m in range(S5M):
                    dve.wait_ge(glu_sig.sem, glu_sig.at(l, m + 1))
                    tt(ssmT[:, m], uT[:, m], glu_sigma[:, m], ALU.mult).then_inc(ssm_ready.sem, 1)
                for m in range(S5M):
                    dve.wait_ge(ssm_hi_ready.sem, ssm_hi_ready.at(l, m + 1))
                    tt(ssm_lo[:, m], ssmT[:, m], ssm_hi[:, m].bitcast(F32), ALU.subtract).then_inc(
                        ssm_lo_ready.sem, 1)
                for m in range(KD + 1):
                    if m < KD:
                        dve.wait_ge(proj_in_psum.sem, proj_in_psum.at(l, m + 1))
                        both = gates_w[:, :, m]
                        c.link(tt(both, both, psum[:, m].rearrange("p (w t) -> p w t", w=2), ALU.mult))
                        tt(gates[:, m], gates[:, m], gates[:, KD + m], ALU.add).then_inc(mixed.sem, 1)
                    if m >= 1:
                        dve.wait_ge(mixed_hi_ready.sem, mixed_hi_ready.at(l, m))
                        tt(mixed_lo[:, m - 1], gates[:, m - 1], mixed_hi[:, m - 1].bitcast(F32),
                           ALU.subtract).then_inc(mix_ready.sem, 1)
                for part in range(UNITS):
                    n, src, lo, hi = mix_unit("out1", part)
                    dve.wait_ge(mix_w_hi.sem, mix_w_hi.at(l, n + 1))
                    tt(lo, src, hi.bitcast(F32), ALU.subtract).then_inc(out1_w_lo.sem, 1)
                for n in range(4):
                    dve.wait_ge(mixed_in_psum.sem, mixed_in_psum.at(l, n + 1))
                    xs = x[:, n // 2, 512 * (n % 2):512 * (n % 2) + 512]
                    ins = tt(xs, xs, psum[:, n], ALU.add)
                    if n % 2:
                        ins.then_inc(x_ready.sem, 1)
                norm(l, 1)
                normed_split(l)
                assert c.n == DVE_MIX, c.n
                with dve.If(l < 1):
                    c.start(DVE_MIX)

                    def split(what, tile):
                        n, src = ff_unit(what, tile)
                        hi, lo = w_hi[:, n % UNIT_BUFS].bitcast(F32), w_lo[:, n % UNIT_BUFS]
                        if what != "d":
                            hi, lo = (w.rearrange("p (k n) -> p k n", k=KD) for w in (hi, lo))
                        dve.wait_ge(hi_ready.sem, n + 1)
                        tt(lo, src, hi, ALU.subtract).then_inc(lo_ready.sem, 1)

                    for n in range(FF_TILES + 2):
                        m = n - 1
                        if n < FF_TILES:
                            split("g", n)
                        if 0 <= m < FF_TILES:
                            gate_ps, up_ps = (psum[:, i + m % 2, 0:SEQ] for i in (4, 6))
                            dve.wait_ge(ff_sig.sem, m + 1)
                            if m >= 2:
                                dve.wait_ge(ff_hi_ready.sem, m - 1)
                            c.link(tt(ff_a[:, m % 2], ff_sigma[:, m % 2], gate_ps, ALU.mult))
                            dve.wait_ge(unit_used.sem, FF_UNITS.index(("u", m)) + 1 + UNIT_BUFS)
                            tt(ff_a[:, m % 2], ff_a[:, m % 2], up_ps, ALU.mult).then_inc(ff_act.sem, 1)
                        if n < FF_TILES:
                            split("u", n)
                        if n >= 2:
                            split("d", n - 2)
                        if 0 <= m < FF_TILES:
                            dve.wait_ge(ff_hi_ready.sem, m + 1)
                            tt(ff_lo[:, m % 4], ff_a[:, m % 2], ff_hi[:, m % 4].bitcast(F32),
                               ALU.subtract).then_inc(ff_lo_ready.sem, 1)
                    dve.wait_ge(unit_used.sem, N_FF_UNITS + UNIT_BUFS)
                    for n in range(4):
                        xs = x[:, n // 2, 512 * (n % 2):512 * (n % 2) + 512]
                        ins = tt(xs, xs, psum[:, n], ALU.add)
                        if n % 2:
                            ins.then_inc(x_ready.sem, 1)
                    assert c.n == DVE_FFN, c.n

            def split(turn, n):
                m = n % (N_PAIR * UNITS)
                dve.wait_ge(hi_ready.sem, per_pair(turn, n + 1))
                tt(w_lo[:, buf(m)], unit(m), w_hi[:, buf(m)].bitcast(F32),
                   ALU.subtract).then_inc(lo_ready.sem, 1)

            for part in range(UNITS):
                split(0, part)
            c.start(DEPTH * DVE_MIX + DVE_FFN)
            dve.wait_ge(logits_in_psum.sem, 1)
            c.link(tt(logits, psum[:, 4, 0:TB * E].rearrange("p (b e) -> p b e", b=TB),
                      const["r_b"].unsqueeze(1).broadcast_to([P, TB, E]), ALU.add))
            for b in range(TB):
                c.add(v.max(top[:, b], logits[:, b]))
            c.sync()
            for b in range(TB):
                c.add(v.max_index(top_i[:, b], top[:, b], logits[:, b]))
            tt(diff[:, :, 0:1], top[:, :, 1:2], top[:, :, 0:1], ALU.subtract).then_inc(top_ready.sem, 1)
            c.sync()
            c.link(v.tensor_copy(top_f, top_i))
            dve.wait_ge(top_exp.sem, 1)
            c.link(v.tensor_scalar(den2[:, :, 0:1], ediff[:, :, 0:1], 1.0, None, ALU.add))
            c.link(v.reciprocal(w_first[:, :, 0:1], den2[:, :, 0:1]))
            c.link(tt(w_second[:, :, 0:1], ediff[:, :, 0:1], w_first[:, :, 0:1], ALU.mult))
            iota = const["iota"]
            for b in range(TB):
                i0, i1 = top_f[:, b, 0:1], top_f[:, b, 1:2]
                c.add(v.tensor_scalar(hot0[:, b], iota[:, 0:E], i0, None, ALU.is_equal))
                c.link(v.tensor_scalar(hot1[:, b], iota[:, 0:E], i1, None, ALU.is_equal))
                c.link(tt(sel[:, b], hot0[:, b], hot1[:, b], ALU.add))
                c.add(v.tensor_scalar(hot0[:, b], hot0[:, b], w_first[:, b, 0:1], None, ALU.mult))
                c.link(v.tensor_scalar(hot1[:, b], hot1[:, b], w_second[:, b, 0:1], None, ALU.mult))
                ins = tt(comb[:, b], hot0[:, b], hot1[:, b], ALU.add)
                if b == 0:
                    c.add(ins)
            ins.then_inc(chosen.sem, 1)
            c.link(v.tensor_copy(g_rows, field["g_ffn"]))
            c.add(v.tensor_copy(x_out, x))
            dve.wait_ge(places_in_psum.sem, 1)
            dve.wait_ge(chosen.sem, 1)
            c.add(v.tensor_reduce(diff[:, 0, 1:2], psum[:, 5, 2 * E:3 * E], AX_X, ALU.max))
            c.link(v.scalar_tensor_tensor(place[:, :, 0:E], psum[:, 5, 0:2 * E].rearrange("p (b e) -> p b e", b=TB), 1.0,
                                          sel, ALU.add, ALU.mult))
            v.tensor_copy(most_i[:, 0:1], diff[:, 0, 1:2]).then_inc(count_ready.sem, 1)
            c.add(v.tensor_scalar(place[:, :, E:2 * E], place[:, :, 0:E], 1.0 + P, None, ALU.subtract))
            c.sync()
            c.add(v.tensor_scalar(place[:, :, 0:E], place[:, :, 0:E], 1.0, None, ALU.subtract))
            c.add(v.memset(place[:, :, 2 * E:], -1.0))
            c.add(v.memset(weight[:, :, 2 * E:], 0.0))
            c.add(v.tensor_copy(weight[:, :, 0:E], comb))
            c.link(v.tensor_copy(weight[:, :, E:2 * E], comb))
            assert c.n == DVE_ROUTE, c.n

            def choose(g, n):
                if isinstance(n, int):
                    assert n == 1
                else:
                    dve.wait_ge(spreadT_in_psum.sem, n - 1)
                    dve.wait_ge(rows_in_psum.sem, (n - 1) * 2)
                for b in range(TB):
                    v.tensor_scalar(pick[:, b], iota, place[:, b, g], rstd[:, b:b + 1], ALU.is_equal, ALU.mult)
                    ins = v.tensor_scalar(spread_tok[:, b], iota, place[:, b, g], weight[:, b, g],
                                          ALU.is_equal, ALU.mult)
                ins.then_inc(pick_ready.sem, 1)

            def take_rows(n):
                for j in range(2):
                    dve.wait_ge(rows_in_psum.sem, n * 2 - 1 + j)
                    gain = g_rows[:, 4 * j:4 * j + 4].unsqueeze(2).broadcast_to([P, 4, P])
                    ins = tt(rows_f[:, 4 * j:4 * j + 4], psum[:, 1 + 2 * j].rearrange("p (k j) -> p k j", k=4), gain,
                             ALU.mult)
                ins.then_inc(rows_f_ready.sem, 1)
                dve.wait_ge(rows_hi_ready.sem, n)
                tt(rows_lo, rows_f, rows_hi.bitcast(F32), ALU.subtract).then_inc(rows_lo_ready.sem, 1)

            choose(slice(0, 1), 1)
            take_rows(1)

            def experts(pair, turn):
                c.start(turn * DVE_PAIR + (DEPTH * DVE_MIX + DVE_FFN + DVE_ROUTE))
                for half in range(2):
                    def at(per, n):
                        return turn * (2 * per) + (half * per + n)

                    def act_of(ch):
                        dve.wait_ge(ex_sig.sem, at(FEC, ch + 1))
                        if ch >= 2:
                            dve.wait_ge(actT_in_psum.sem, at(FEC, ch - 1))
                        c.link(tt(ex_a[:, ch % 2], ex_sigma, psum[:, ch % 2], ALU.mult))
                        dve.wait_ge(unit_used.sem, per_pair(turn, item_unit(half, "u", ch) + UNITS + UNIT_BUFS))
                        tt(ex_a[:, ch % 2], ex_a[:, ch % 2], psum[:, 2 + ch % 2], ALU.mult).then_inc(ex_act.sem, 1)

                    def rest_of_act(ch):
                        dve.wait_ge(aT_hi_ready.sem, at(FEC, ch + 1))
                        tt(aT_lo[:, ch % 2], psum[:, 6], aT_hi[:, ch % 2].bitcast(F32), ALU.subtract).then_inc(
                            aT_lo_ready.sem, 1)

                    for ch in range(FEC):
                        for part in range(UNITS):
                            if ch:
                                split(turn, item_unit(half, "g", ch) + part)
                            if ch and part == 1:
                                act_of(ch - 1)
                        for part in range(UNITS):
                            split(turn, item_unit(half, "u", ch) + part)
                            if ch and part == 2:
                                rest_of_act(ch - 1)
                        if ch == 2:
                            dve.wait_ge(spreadT_in_psum.sem, at(1, 1))
                            v.tensor_copy(spread.rearrange("p b t -> p (b t)"), psum[:, 7, 0:TB * P]).then_inc(
                                spread_ready.sem, 1)
                        if ch == 3:
                            choose(bass.ds(turn * 2 + (half + 1), 1), at(1, 2))
                        for part in range(UNITS if ch else 0):
                            split(turn, item_unit(half, "d", ch - 1) + part)
                    for part in range(UNITS):
                        split(turn, item_unit(half, "d", FEC - 1) + part)
                        if part == 0:
                            act_of(FEC - 1)
                        if part == 1:
                            rest_of_act(FEC - 1)
                            take_rows(at(1, 2))
                    ahead(dve, pair, turn, half, split)
                    dve.wait_ge(unit_used.sem, per_pair(turn, (half + 1) * N_EXP * UNITS + UNIT_BUFS))
                    v.tensor_copy(y_rows[:, 512:], psum[:, 5]).then_inc(y_rows_ready_dve.sem, 1)
                    for n in range(4):
                        b, j = n // 2, n % 2
                        dve.wait_ge(spread_in_psum.sem, at(4, n + 1))
                        xs = x_out[:, b, 512 * j:512 * j + 512]
                        tt(xs, xs, psum[:, 7 - n % 2], ALU.add).then_inc(spread_added.sem, 1)
                assert c.n == DVE_PAIR, c.n

            with dve.Fori(0, E // 2) as pair:
                experts(pair, pair)
            dve.wait_ge(count_ready.sem, 1)
            most = dve.value_load(most_i[0:1, 0:1], min_val=0, max_val=SEQ)
            with dve.If(most > P):
                for part in range(UNITS):
                    split(E // 2, part)
                with dve.Fori(0, E // 2) as pair:
                    experts(pair, pair + E // 2)
            dve.drain().then_inc(out_ready.sem, 1)


def _packed(i):
    def channels(a):
        return a.reshape(DEPTH, -1, P).transpose(0, 2, 1)

    def pairs(a):
        return a.reshape(DEPTH, PAIRS, 2 * STATES).transpose(0, 2, 1)

    def two_groups(a):
        a = a.reshape(DEPTH, PAIRS, 2, STATES, CH)
        wide = np.zeros((DEPTH, PAIRS, 2, STATES, 2, CH), a.dtype)
        for g in range(2):
            wide[:, :, g, :, g] = a[:, :, g]
        return wide.reshape(DEPTH, PAIRS, P, 32).transpose(0, 2, 1, 3).reshape(DEPTH, P, PAIRS * 32)

    def spread(a):
        return np.broadcast_to(a[:, None, :], (DEPTH, P, a.shape[1]))

    b_in = i["b_in"]
    step = np.broadcast_to(i["s5_log_step"][:, :, None], (DEPTH, GROUPS, STATES))
    values = {
        "g_mix": channels(i["ln_mix_g"]), "g_ffn": channels(i["ln_ffn_g"]), "b_u": channels(b_in[:, LAT:LAT + S5W]),
        "b_gate": channels(b_in[:, LAT + S5W:]), "s5_d": channels(i["s5_d"]), "b_glu": channels(i["b_glu"]),
        "g_q": channels(i["q_norm_g"]), "g_kv": channels(i["kv_norm_g"]), "lam_re": pairs(i["s5_lam_re"]),
        "lam_im": pairs(i["s5_lam_im"]), "log_step": pairs(step), "b_re": two_groups(i["s5_b_re"]),
        "b_im": two_groups(i["s5_b_im"]), "c_re": two_groups(i["s5_c_re"].transpose(0, 1, 3, 2)),
        "c_im": two_groups(i["s5_c_im"].transpose(0, 1, 3, 2)), "b_lat": spread(b_in[:, :LAT]),
        "g_qh": spread(i["q_head_g"]), "g_kh": spread(i["k_head_g"]),
    }
    return np.ascontiguousarray(np.concatenate([values[n] for n, _ in FIELDS], 2))


def _constants(router_b):
    rows = np.arange(P)
    causal = np.where(rows[None, :] <= rows[:, None], 0.0, NEG)
    inv = np.power(np.float32(10000.0), -np.arange(0, ROPE, 2, dtype=np.float32) / np.float32(ROPE))
    angle = (np.arange(SEQ, dtype=np.float32)[:, None] * inv[None, :]).reshape(TB, P, HALF).transpose(1, 0, 2)
    values = {"ident": np.eye(P), "mask": causal,
              "cos": np.cos(angle).reshape(P, -1), "sin": np.sin(angle).reshape(P, -1),
              "before": rows[:, None] < rows[None, :], "ones": np.ones((P, P)),
              "iota": np.broadcast_to(rows[None, :], (P, P)), "r_b": np.broadcast_to(router_b, (P, E))}
    return np.concatenate([values[n].astype(np.float32) for n, _ in CONSTS], 1)


def kernel(**inputs):
    import concourse.bacc as bacc
    from concourse.bass_utils import run_bass_kernel_spmd

    nc = bacc.Bacc("TRN2", target_bir_lowering=False, num_devices=1)
    i = {n: np.asarray(a) for n, a in inputs.items()}
    given = {"x": i["x"].reshape(SEQ, D), "params": _packed(i), "consts": _constants(i["router_b"])}
    for n in ("w_in", "w_uq", "w_ukv", "w_glu", "w_proj_attn", "w_proj_ssm", "w_out", "ffn_w_gate", "ffn_w_up",
              "ffn_w_down", "router_w"):
        given[n] = i[n]
    for n in ("moe_w_gate", "moe_w_up", "moe_w_down"):
        given[n] = i[n][0]
    arrays = {f"{n}_dram": np.ascontiguousarray(a) for n, a in given.items()}
    args = [nc.dram_tensor(n, a.shape, mybir.dt.from_np(a.dtype), kind="ExternalInput").ap()
            for n, a in arrays.items()]
    out = nc.dram_tensor("out_dram", (SEQ, D), F32, kind="ExternalOutput").ap()
    hybrid_trunk(nc, *args, out)
    r = run_bass_kernel_spmd(nc, [arrays], core_ids=[0])
    return r.results[0]["out_dram"].reshape(1, SEQ, D)
```
